# Optimizing a Trainium2 kernel written in Bass

```python
import jax, jax.numpy as jnp
from jax import lax
import numpy as np

D_MODEL = 1024
BATCH = 1
SEQ = 256
DEPTH = 2

N_HEADS = 8
HEAD_DIM = 64
ATTN_WIDTH = 512
ROPE_DIM = 16
ROPE_THETA = 500000.0
IDX_HEADS = 8
IDX_DIM = 32
IDX_ROPE_DIM = 8
TOPK_MAX = 256
Q_BLOCK = 128
POOL_GROUPS = 4
POOL_GROUP_DIM = 128
POOL_WIDTH = 512
POOL_WINDOWS = (2, 4, 8, 16)
D_FF = 2816
N_EXPERTS = 8
TOP_K_EXPERTS = 2
D_FF_EXPERT = 3584
N_DENSE = (DEPTH + 1) // 2
N_MOE = DEPTH // 2
EPS = 1e-6
IN_SPLIT_SIZES = (ATTN_WIDTH, ATTN_WIDTH, ATTN_WIDTH, IDX_HEADS * IDX_DIM, IDX_DIM, IDX_HEADS, POOL_WIDTH, D_MODEL, D_MODEL)
IN_WIDTH = 4392

kernel_name = 'hybrid_dsa_pool_moe_block'

def rmsnorm(x, g):
    xf = x.astype(jnp.float32)
    y = xf * lax.rsqrt(jnp.mean(xf * xf, axis=-1, keepdims=True) + EPS)
    return (y * g.astype(jnp.float32)).astype(x.dtype)

def rope_partial(x, pos, rot_dim):
    inv = jnp.power(ROPE_THETA, -jnp.arange(0, rot_dim, 2, dtype=jnp.float32) / rot_dim)
    ang = pos[:, None] * inv[None, :]
    cos = jnp.cos(ang)[None, :, None, :]
    sin = jnp.sin(ang)[None, :, None, :]
    xr = x[..., :rot_dim].astype(jnp.float32)
    x1, x2 = xr[..., : rot_dim // 2], xr[..., rot_dim // 2:]
    rot = jnp.concatenate([x1 * cos - x2 * sin, x2 * cos + x1 * sin], axis=-1)
    return jnp.concatenate([rot.astype(x.dtype), x[..., rot_dim:]], axis=-1)

def dsa_attention(q, k, v, qi, ki, wi):
    B, S, H, hd = q.shape
    topk = min(TOPK_MAX, S // 4)
    nb = S // Q_BLOCK
    kpos = jnp.arange(S, dtype=jnp.int32)
    ki32 = ki.astype(jnp.float32)

    def to_blocks(a):
        return a.reshape((B, nb, Q_BLOCK) + a.shape[2:]).swapaxes(0, 1)

    def block(args):
        qb, qib, wib, qpos = args
        dots = jnp.einsum('bqhd,bsd->bqhs', qib.astype(jnp.float32), ki32) * (IDX_DIM ** -0.5)
        score = jnp.einsum('bqh,bqhs->bqs', wib.astype(jnp.float32) * (IDX_HEADS ** -0.5), jax.nn.relu(dots))
        causal = kpos[None, :] <= qpos[:, None]
        score = jnp.where(causal[None], score, -jnp.inf)
        _, sel = lax.top_k(score, topk)
        valid = sel <= qpos[None, :, None]
        k_sel = jax.vmap(lambda kk, ii: kk[ii])(k, sel)
        v_sel = jax.vmap(lambda vv, ii: vv[ii])(v, sel)
        logits = jnp.einsum('bqhd,bqkhd->bqhk', qb.astype(jnp.float32), k_sel.astype(jnp.float32)) * (HEAD_DIM ** -0.5)
        logits = jnp.where(valid[:, :, None, :], logits, -jnp.inf)
        p = jax.nn.softmax(logits, axis=-1)
        return jnp.einsum('bqhk,bqkhd->bqhd', p.astype(v.dtype), v_sel)

    pos_b = kpos.reshape(nb, Q_BLOCK)
    out = lax.map(block, (to_blocks(q), to_blocks(qi), to_blocks(wi), pos_b))
    return out.swapaxes(0, 1).reshape(B, S, H * hd)

def pool_mixer(u, w_pool, pool_scale):
    B, S, C = u.shape
    cs = jnp.pad(jnp.cumsum(u.astype(jnp.float32), axis=1), ((0, 0), (1, 0), (0, 0)))
    t1 = jnp.arange(1, S + 1, dtype=jnp.float32)
    means = []
    for g, w in enumerate(POOL_WINDOWS):
        c = cs[:, :, g * POOL_GROUP_DIM:(g + 1) * POOL_GROUP_DIM]
        lagged = jnp.pad(c[:, :S + 1 - w], ((0, 0), (w - 1, 0), (0, 0)))
        means.append((c[:, 1:] - lagged) / jnp.minimum(t1, w)[None, :, None])
    pooled = jnp.stack(means, axis=2)
    diff = pooled - u.reshape(B, S, POOL_GROUPS, POOL_GROUP_DIM).astype(jnp.float32)
    mixed = jnp.einsum('bsgc,gcd->bsgd', diff.astype(u.dtype), w_pool)
    return mixed.reshape(B, S, C) * pool_scale

def swiglu(h, w1, w3, w2):
    return (jax.nn.silu(h @ w1) * (h @ w3)) @ w2

def moe_swiglu(h, w_router, w1, w3, w2):
    logits = jnp.einsum('bsd,de->bse', h.astype(jnp.float32), w_router.astype(jnp.float32))
    top_v, top_i = lax.top_k(logits, TOP_K_EXPERTS)
    top_w = jax.nn.softmax(top_v, axis=-1)
    gate = jnp.sum(jax.nn.one_hot(top_i, N_EXPERTS, dtype=jnp.float32) * top_w[..., None], axis=-2)
    gate = gate.astype(h.dtype)
    y = jnp.zeros_like(h)
    for e in range(N_EXPERTS):
        y = y + gate[..., e:e + 1] * swiglu(h, w1[e], w3[e], w2[e])
    return y

def setup_inputs(seed: int = 0) -> dict:
    key = jax.random.key(seed)
    ks = jax.random.split(key, 20)

    def nrm(k, shape, scale):
        return jax.random.normal(k, shape, jnp.float32) * scale

    return {
        'x': nrm(ks[0], (BATCH, SEQ, D_MODEL), 1.0),
        'mix_norm': 1.0 + nrm(ks[1], (DEPTH, D_MODEL), 0.02),
        'w_in': nrm(ks[2], (DEPTH, D_MODEL, IN_WIDTH), D_MODEL ** -0.5),
        'q_norm': 1.0 + nrm(ks[3], (DEPTH, HEAD_DIM), 0.02),
        'k_norm': 1.0 + nrm(ks[4], (DEPTH, HEAD_DIM), 0.02),
        'w_pool': nrm(ks[5], (DEPTH, POOL_GROUPS, POOL_GROUP_DIM, POOL_GROUP_DIM), POOL_GROUP_DIM ** -0.5),
        'pool_scale': 1.0 + nrm(ks[6], (DEPTH, POOL_WIDTH), 0.1),
        'w_attn_proj': nrm(ks[7], (DEPTH, ATTN_WIDTH, D_MODEL), ATTN_WIDTH ** -0.5),
        'w_pool_proj': nrm(ks[8], (DEPTH, POOL_WIDTH, D_MODEL), POOL_WIDTH ** -0.5),
        'w_out': nrm(ks[9], (DEPTH, D_MODEL, D_MODEL), D_MODEL ** -0.5),
        'ffn_norm': 1.0 + nrm(ks[10], (DEPTH, D_MODEL), 0.02),
        'dense_w1': nrm(ks[11], (N_DENSE, D_MODEL, D_FF), D_MODEL ** -0.5),
        'dense_w3': nrm(ks[12], (N_DENSE, D_MODEL, D_FF), D_MODEL ** -0.5),
        'dense_w2': nrm(ks[13], (N_DENSE, D_FF, D_MODEL), D_FF ** -0.5),
        'moe_router': nrm(ks[14], (N_MOE, D_MODEL, N_EXPERTS), D_MODEL ** -0.5),
        'moe_w1': nrm(ks[15], (N_MOE, N_EXPERTS, D_MODEL, D_FF_EXPERT), D_MODEL ** -0.5),
        'moe_w3': nrm(ks[16], (N_MOE, N_EXPERTS, D_MODEL, D_FF_EXPERT), D_MODEL ** -0.5),
        'moe_w2': nrm(ks[17], (N_MOE, N_EXPERTS, D_FF_EXPERT, D_MODEL), D_FF_EXPERT ** -0.5),
    }

def reference(x, mix_norm, w_in, q_norm, k_norm, w_pool, pool_scale, w_attn_proj, w_pool_proj, w_out, ffn_norm, dense_w1, dense_w3, dense_w2, moe_router, moe_w1, moe_w3, moe_w2):
    B, S, _ = x.shape
    pos = jnp.arange(S, dtype=jnp.float32)
    offsets = [int(o) for o in np.cumsum(IN_SPLIT_SIZES)[:-1]]
    for layer in range(DEPTH):
        h = rmsnorm(x, mix_norm[layer])
        z = h @ w_in[layer]
        q, k, v, qi, ki, wi, u, ga, gp = jnp.split(z, offsets, axis=-1)
        q = rope_partial(rmsnorm(q.reshape(B, S, N_HEADS, HEAD_DIM), q_norm[layer]), pos, ROPE_DIM)
        k = rope_partial(rmsnorm(k.reshape(B, S, N_HEADS, HEAD_DIM), k_norm[layer]), pos, ROPE_DIM)
        v = v.reshape(B, S, N_HEADS, HEAD_DIM)
        qi = rope_partial(qi.reshape(B, S, IDX_HEADS, IDX_DIM), pos, IDX_ROPE_DIM)
        ki = rope_partial(ki[:, :, None, :], pos, IDX_ROPE_DIM)[:, :, 0, :]
        a = dsa_attention(q, k, v, qi, ki, wi)
        p = pool_mixer(u, w_pool[layer], pool_scale[layer])
        merged = jax.nn.sigmoid(ga) * (a @ w_attn_proj[layer]) + jax.nn.sigmoid(gp) * (p @ w_pool_proj[layer])
        x = x + merged @ w_out[layer]
        h2 = rmsnorm(x, ffn_norm[layer])
        if layer % 2 == 0:
            i = layer // 2
            x = x + swiglu(h2, dense_w1[i], dense_w3[i], dense_w2[i])
        else:
            i = layer // 2
            x = x + moe_swiglu(h2, moe_router[i], moe_w1[i], moe_w3[i], moe_w2[i])
    return x


_drawn_inputs = setup_inputs


def setup_inputs(seed=0):
    import zlib

    import numpy as np

    out = dict(_drawn_inputs(seed))
    spreads = {}
    factors = {'q_norm': 4.132, 'k_norm': 2.883}
    for name, (base, spread) in spreads.items():
        noise = np.random.default_rng([zlib.crc32(name.encode()), seed]).standard_normal(out[name].shape)
        drawn = base * np.exp(spread * noise) if base else spread * noise
        out[name] = __import__('jax').numpy.asarray(drawn.astype(out[name].dtype))
    for name, factor in factors.items():
        out[name] = (out[name] * factor).astype(out[name].dtype)
    return out
```

```python
from contextlib import ExitStack

import numpy as np

import concourse.bass as bass
from concourse import mybir

F32 = mybir.dt.float32
FR = mybir.dt.float32r
I32 = mybir.dt.int32
U32 = mybir.dt.uint32
ALU = mybir.AluOpType
ACT = mybir.ActivationFunctionType
AX = mybir.AxisListType

P = 128
D = 1024
S = 256
TT = S // P
KC = D // P
HEADS, HD, ROT = 8, 64, 16
AW = HEADS * HD
IH, IDIM, IROT = 8, 32, 8
IDXW = IH * IDIM + IDIM + IH
TOPK = 64
GROUPS = 4
WINDOWS = (2, 4, 8, 16)
FF = 2816
E = 8
FFE = 3584
EPS = 1e-6
NEG = -1e38
MARK = -3e38
MASKED = -1e30
THETA = 500000.0

SLOTS = 4
LOOK = SLOTS
LEAD = 2
FULL = 2048
HALF = 1024
NB_D = FF // 256
NB_E = FFE // 256
KC_D = FF // P
KC_E = FFE // P
ZCOL = [0, 512, 1024, 1832, 2344, 2856, 3368, 3880]
ZQ, ZK, ZV, ZU, ZGA, ZGP = 0, 1, 2, 3, 4, 6
MIX_CHUNKS = 2 + 2 * len(ZCOL) + 4 + 4
DENSE0 = MIX_CHUNKS
LAYER1 = DENSE0 + 2 * NB_D + KC_D
MOE0 = LAYER1 + MIX_CHUNKS
JOB_CHUNKS = 2 * NB_E + KC_E
NJ = 12

C_ID, C_TRI, C_NEG, C_IOTA, C_ONE = 0, 128, 256, 384, 512
C_COS, C_SIN, C_COSI, C_SINI = 640, 656, 672, 680
C_END = 688


def chunk_words(c):
    m = c - (LAYER1 if c >= LAYER1 else 0)
    if m < 2:
        return (KC // 2) * IDXW
    if DENSE0 + 2 * NB_D <= c < LAYER1:
        return HALF
    return FULL


def build(nc, A, out):
    with ExitStack() as ctx:
        def sb(name, shape, dt=F32, where=ctx):
            return where.enter_context(nc.sbuf_tensor(name, shape, dt))

        def sem(name):
            return ctx.enter_context(nc.semaphore(name))

        raw = sb("w_raw", [P, SLOTS, FULL])
        whi = sb("w_hi", [P, SLOTS, FULL], FR)
        wlo = sb("w_lo", [P, SLOTS, FULL], FR)
        X = sb("x_residual", [P, TT, D])
        hThi = sb("hT_hi", [P, KC, S], FR)
        hTlo = sb("hT_lo", [P, KC, S], FR)
        cst = sb("shape_constants", [P, C_END])
        pcol = sb("param_columns", [P, 40])
        gain = sb("qk_gain", [P, 2, 2, HD])
        st = sb("norm_stats", [P, 4, TT])
        ident = cst[:, C_ID:C_ID + P]
        mixer = ExitStack()
        zb = sb("z_blocks", [P, 8, TT, 512], F32, mixer)
        zi = sb("z_index", [P, TT, IDXW], F32, mixer)
        wis = sb("w_index", [P, TT, IH], F32, mixer)
        wpool = sb("w_pool", [P, GROUPS, P], F32, mixer)
        band = sb("pool_band", [P, GROUPS, 3 * P], F32, mixer)
        diffT = sb("pool_diffT", [P, GROUPS, S], F32, mixer)
        work = sb("topk_work", [P, P + S], F32, mixer)
        madd = sb("mask_add", [P, P + S], F32, mixer)
        m8 = sb("max8", [P, TT, 8], F32, mixer)
        ao = sb("attn_out", [P, TT, AW], F32, mixer)
        ki4 = ao[:, :, 0:4 * IDIM].rearrange("p t (a d) -> p t a d", d=IDIM)
        hs32 = sb("head_stats", [P, 3, 32], F32, mixer)
        sx = sb("softmax_stats", [P, TT, 4, HEADS], F32, mixer)
        PT = sb("probsT", [P, 2, HEADS, P], F32, mixer)
        att = ExitStack()
        qT = sb("qT", [P, 4, S], F32, att)
        kT = sb("kT", [P, 4, S], F32, att)
        L = sb("logits", [P, HEADS, S], F32, att)
        qiT = sb("qiT", [P, 2, S], F32, att)
        kiT = sb("kiT", [P, S], F32, att)
        att.close()
        proj = ExitStack()
        aThi = sb("aT_hi", [P, 4, S], FR, proj)
        aTlo = sb("aT_lo", [P, 4, S], FR, proj)
        pThi = sb("pT_hi", [P, 4, S], FR, proj)
        pTlo = sb("pT_lo", [P, 4, S], FR, proj)
        proj.close()
        mixer.close()
        setup = ExitStack()
        xs = sb("x_normed", [P, TT, D], F32, setup)
        prow = sb("param_rows", [40, P], F32, setup)
        nrow = sb("gain_row", [1, 4 * HD], F32, setup)
        dense = ExitStack()
        hidDhi = sb("hidden_hi", [P, KC_D, S], FR, dense)
        hidDlo = sb("hidden_lo", [P, KC_D, S], FR, dense)
        sgD = sb("silu_out", [P, 2, TT, 256], F32, dense)
        hsD = sb("hidden", [P, 2, TT, 256], F32, dense)
        dense.close()
        moe = ExitStack()
        xrhi = sb("x_rows_hi", [P, TT, D], FR, moe)
        xrlo = sb("x_rows_lo", [P, TT, D], FR, moe)
        hehi = sb("gathered_hi", [P, KC, P], FR, moe)
        helo = sb("gathered_lo", [P, KC, P], FR, moe)
        hidMhi = sb("hiddenM_hi", [P, KC_E, P], FR, moe)
        hidMlo = sb("hiddenM_lo", [P, KC_E, P], FR, moe)
        yhi = sb("expert_out_hi", [P, D], FR, moe)
        ylo = sb("expert_out_lo", [P, D], FR, moe)
        sgM = sb("siluM_out", [P, 2, 256], F32, moe)
        hsM = sb("hiddenM", [P, 2, 256], F32, moe)
        selR = sb("select", [P, TT, P], FR, moe)
        selT = sb("selectT", [P, S], FR, moe)
        identR = sb("identity_r", [P, P], FR, moe)
        wr = sb("w_router", [P, KC, E], F32, moe)
        wrhi = sb("w_router_hi", [P, KC, E], FR, moe)
        wrlo = sb("w_router_lo", [P, KC, E], FR, moe)
        lg = sb("router_logits", [P, TT, E], F32, moe)
        v8 = sb("router_top", [P, TT, 8], F32, moe)
        ix8 = sb("router_index", [P, TT, 8], U32, moe)
        ixf = sb("router_index_f", [P, TT, 8], F32, moe)
        m0 = sb("mask_first", [P, TT, E], F32, moe)
        m1 = sb("mask_second", [P, TT, E], F32, moe)
        pr = sb("gate_probs", [P, 4, TT], F32, moe)
        gate = sb("gate", [P, TT, E], F32, moe)
        pm = sb("slot_of_token", [P, TT, E], F32, moe)
        ov = sb("overflow", [P, 4, E], F32, moe)
        tmp8 = sb("routing_tmp", [P, TT, E], F32, moe)
        posj = sb("slot_by_job", [P, TT, NJ], F32, moe)
        gatej = sb("gate_by_job", [P, TT, NJ], F32, moe)
        tabf = sb("job_table_f", [P, 16], F32, moe)
        tabi = sb("job_table", [P, 16], I32, moe)
        moe.close()
        setup.close()

        bank = [ctx.enter_context(nc.psum_tensor(f"bank{i}", [P, 512], F32)) for i in range(8)]

        s_x = sem("x_loaded")
        s_cst = sem("constants_loaded")
        s_par = sem("params_loaded")
        s_wrl = sem("router_loaded")
        s_pool = [sem(f"pool_weights_loaded{i}") for i in range(2)]
        s_ld = [sem(f"chunk_loaded{i}") for i in range(SLOTS)]
        s_hi = sem("chunk_hi")
        s_lo = sem("chunk_lo")
        s_use = sem("chunk_used")
        s_prt = sem("paramsT_done")
        s_pcol = sem("param_columns_ready")
        s_sq = sem("sumsq_done")
        s_ms = sem("meansq_done")
        s_rms = sem("rms_done")
        s_xs = sem("xs_done")
        s_tr = sem("transposed")
        s_thi = sem("hT_hi_done")
        s_tlo = sem("hT_lo_done")
        s_z = sem("z_block_done")
        s_za = sem("z_evac_act")
        s_zd = sem("z_evac_dve")
        s_idx = sem("index_ready")
        s_idxT = sem("indexT_done")
        s_idxs = sem("indexT_in_sbuf")
        s_dot = sem("index_dots_done")
        s_rel = sem("relu_done")
        s_sc = sem("scores_done")
        s_qms = sem("qk_meansq")
        s_qrm = sem("qk_rms")
        s_qk = sem("qk_roped")
        s_qkT = sem("qkT_done")
        s_qks = sem("qkT_in_sbuf")
        s_lg = sem("qk_products")
        s_mx = sem("row_max_ready")
        s_ex = sem("exp_done")
        s_pt = sem("probsT_done")
        s_pta = sem("probsT_evac_act")
        s_ptd = sem("probsT_evac_dve")
        s_pv = sem("pv_done")
        s_ao = sem("attn_out_ready")
        s_aT = sem("aT_done")
        s_ahi = sem("aT_hi_done")
        s_alo = sem("aT_lo_done")
        s_df = sem("pool_diff_done")
        s_dfs = sem("pool_diff_in_sbuf")
        s_pp = sem("pool_mixed_done")
        s_phi = sem("pT_hi_done")
        s_plo = sem("pT_lo_done")
        s_sg = sem("gates_ready")
        s_pj = sem("projection_done")
        s_m = sem("merged_ready")
        s_wo = sem("w_out_done")
        s_xd = sem("x_updated")
        s_fb = sem("ffn_block_done")
        s_si = sem("ffn_silu_done")
        s_hm = sem("ffn_hidden_done")
        s_ft = sem("ffn_hiddenT_done")
        s_fhi = sem("ffn_hiddenT_hi")
        s_flo = sem("ffn_hiddenT_lo")
        s_w2 = sem("ffn_down_done")
        s_xr = sem("x_rows_hi_done")
        s_xrl = sem("x_rows_lo_done")
        s_wrh = sem("router_hi_done")
        s_rt = sem("router_done")
        s_gd = sem("gate_diff")
        s_ge = sem("gate_exp")
        s_mk = sem("expert_mask_ready")
        s_pos = sem("positions_done")
        s_tab = sem("job_table_ready")
        s_sel = sem("select_ready")
        s_g = sem("gather_done")
        s_ghi = sem("gather_hi")
        s_glo = sem("gather_lo")
        s_st = sem("selectT_done")
        s_sts = sem("selectT_in_sbuf")
        m_fb = sem("moe_block_done")
        m_si = sem("moe_silu_done")
        m_hm = sem("moe_hidden_done")
        m_ft = sem("moe_hiddenT_done")
        m_fhi = sem("moe_hiddenT_hi")
        m_flo = sem("moe_hiddenT_lo")
        m_w2 = sem("moe_down_done")
        m_yhi = sem("moe_y_hi")
        m_ylo = sem("moe_y_lo")
        m_sc = sem("moe_scatter_done")
        m_xa = sem("moe_x_added")
        s_dve = sem("dve_step")
        s_act = sem("act_step")
        s_out = sem("out_stored")

        block = ctx.enter_context(nc.Block())

        @block.sync
        def _(sp):
            def load(c, parts, dyn=0):
                if not (isinstance(dyn, int) and c < SLOTS):
                    sp.wait_ge(s_lo, dyn * SLOTS + (c - SLOTS + 1))
                for dst, src in parts:
                    sp.dma_start(dst, src).then_inc(s_ld[c % SLOTS], 16)

            def k_halves(c, w, rows, col, width):
                t = raw[:, c % SLOTS, 0:4 * width].rearrange("p (k n) -> p k n", n=width)
                v = w[rows:rows + 512, col:col + width].rearrange("(k p) n -> p k n", p=P)
                return [(t[:, 0:2], v[:, 0:2]), (t[:, 2:4], v[:, 2:4])]

            def up_pair(c, w1, w3, half, col):
                t = raw[:, c % SLOTS, :].rearrange("p (k n) -> p k n", n=512)
                rows = slice(half * 512, half * 512 + 512)
                return [(t[:, :, 256 * j:256 * j + 256],
                         w[rows, col].rearrange("(k p) n -> p k n", p=P)) for j, w in enumerate((w1, w3))]

            def down_row(c, w2, row):
                t = raw[:, c % SLOTS, 0:HALF]
                return [(t[:, 512 * j:512 * j + 512], w2[row, 512 * j:512 * j + 512]) for j in range(2)]

            def mixer_loads(l, c):
                w = A["w_in"][l]
                for h in range(2):
                    load(c, k_halves(c, w, 512 * h, 1536, IDXW))
                    c += 1
                for col in ZCOL:
                    for h in range(2):
                        load(c, k_halves(c, w, 512 * h, col, 512))
                        c += 1
                for nh in range(2):
                    for name in ("w_attn_proj", "w_pool_proj"):
                        load(c, k_halves(c, A[name][l], 0, 512 * nh, 512))
                        c += 1
                for nh in range(2):
                    for h in range(2):
                        load(c, k_halves(c, A["w_out"][l], 512 * h, 512 * nh, 512))
                        c += 1

            sp.dma_start(X[:], A["x"][0].rearrange("(t p) d -> p t d", p=P)).then_inc(s_x, 16)
            sp.dma_start(cst[:], A["consts"]).then_inc(s_cst, 16)
            for name, r, n in (("mix_norm", 0, 16), ("ffn_norm", 16, 16), ("pool_scale", 32, 8)):
                sp.dma_start(prow[r:r + n, :], A[name].rearrange("l (k p) -> (l k) p", p=P)).then_inc(s_par, 16)
            for j, name in enumerate(("q_norm", "k_norm")):
                v = nrow[:].rearrange("o (l j d) -> o l j d", l=2, j=2)
                for l in range(2):
                    sp.dma_start(v[:, l, j], A[name][l:l + 1, :]).then_inc(s_par, 16)
            for l in range(2):
                base = l * LAYER1
                mixer_loads(l, base)
                if l == 0:
                    for b in range(NB_D):
                        for h in range(2):
                            c = DENSE0 + 2 * b + h
                            load(c, up_pair(c, A["dense_w1"][0], A["dense_w3"][0], h, slice(256 * b, 256 * b + 256)))
                    for k in range(KC_D):
                        c = DENSE0 + 2 * NB_D + k
                        load(c, down_row(c, A["dense_w2"][0], slice(P * k, P * k + P)))

            def job_loads(i, e):
                w1, w3, w2 = (A[n][0].rearrange("e k n -> (e k) n") for n in ("moe_w1", "moe_w3", "moe_w2"))
                per = JOB_CHUNKS // SLOTS
                with sp.Fori(0, NB_E // 2) as it:
                    for k in range(SLOTS):
                        t = raw[:, k, :].rearrange("p (k n) -> p k n", n=512)
                        sp.wait_ge(s_lo, i * JOB_CHUNKS + it * SLOTS + (MOE0 + k - SLOTS + 1))
                        for j, w in enumerate((w1, w3)):
                            src = w[bass.ds(e * D + (k % 2) * 512, 512), bass.ds(it * 512 + (k // 2) * 256, 256)]
                            sp.dma_start(t[:, :, 256 * j:256 * j + 256],
                                         src.rearrange("(k p) n -> p k n", p=P)).then_inc(s_ld[k], 16)
                with sp.Fori(0, KC_E // SLOTS) as it:
                    for k in range(SLOTS):
                        sp.wait_ge(s_lo, i * JOB_CHUNKS + it * SLOTS + (MOE0 + 2 * NB_E + k - SLOTS + 1))
                        for j in range(2):
                            sp.dma_start(raw[:, k, 512 * j:512 * j + 512],
                                         w2[bass.ds(e * FFE + it * 512 + k * P, P), 512 * j:512 * j + 512]
                                         ).then_inc(s_ld[k], 16)

            with sp.Fori(0, E - 1) as i:
                job_loads(i, i)
            sp.wait_ge(s_tab, 1)
            njobs = sp.value_load(tabi[0:1, 15:16], min_val=E, max_val=NJ - 1)
            with sp.Fori(E - 1, njobs) as i:
                e = sp.value_load(tabi[0:1, bass.ds(i, 1)], min_val=0, max_val=E - 1)
                job_loads(i, e)
            for k in range(SLOTS):
                sp.wait_ge(s_lo, njobs * JOB_CHUNKS + (MOE0 + k - SLOTS + 1))
                for j in range(2):
                    sp.dma_start(raw[:, k, 1024 * j:1024 * j + 1024],
                                 A["moe_w2"][0, 0, 0:P, :]).then_inc(s_ld[k], 16)
            sp.wait_ge(m_xa, njobs * 4 + LEAD)
            sp.dma_start(out[0].rearrange("(t p) d -> p t d", p=P), X[:]).then_inc(s_out, 16)
            sp.wait_ge(s_out, 16)

        @block.gpsimd
        def _(pool):
            for l in range(2):
                if l:
                    pool.wait_ge(s_xd, 2)
                pool.dma_start(band[:], A["pool_band"]).then_inc(s_pool[0], 16)
                pool.dma_start(wpool[:], A["w_pool"][l].rearrange("g c d -> c g d")).then_inc(s_pool[1], 16)
            pool.wait_ge(s_xd, 3)
            pool.dma_start(wr[:], A["moe_router"][0].rearrange("(k p) e -> p k e", p=P)).then_inc(s_wrl, 16)

        @block.scalar
        def _(act):
            steps = [0]

            def chain(ins):
                steps[0] += 1
                ins.then_inc(s_act, 1)
                act.wait_ge(s_act, steps[0])

            def split(c, n, dyn=0):
                act.wait_ge(s_ld[c % SLOTS], dyn * 32 + 32 * (c // SLOTS + 1))
                if not (isinstance(dyn, int) and c < SLOTS):
                    act.wait_ge(s_use, dyn * SLOTS + (c - SLOTS + 1))
                act.activation(whi[:, c % SLOTS, 0:n], raw[:, c % SLOTS, 0:n], ACT.Copy).then_inc(s_hi, 1)

            def ahead(c):
                split(c + LOOK, chunk_words(c + LOOK) if c + LOOK < MOE0 else FULL)

            def hT_hi(te, scale0):
                for j in range(4):
                    act.wait_ge(s_tr, 4 * te + j + 1)
                    if scale0 is None:
                        act.activation(hThi[:, 2 * j:2 * j + 2, :], bank[j][:].rearrange("p (k t) -> p k t", t=S),
                                       ACT.Copy).then_inc(s_thi, 1)
                        continue
                    for q in range(2):
                        k = 2 * j + q
                        ins = act.activation(hThi[:, k, :], bank[j][:, q * S:q * S + S], ACT.Copy,
                                             scale=pcol[:, scale0 + k:scale0 + k + 1])
                    ins.then_inc(s_thi, 1)

            def norm(k):
                if k:
                    act.wait_ge(s_xd, k)
                else:
                    act.wait_ge(s_x, 16)
                for t in range(TT):
                    act.activation(xs[:, t, :], X[:, t, :], ACT.Square, accum_out=st[:, 0, t:t + 1]).then_inc(s_sq, 1)
                act.wait_ge(s_ms, k + 1)
                act.activation(st[:, 2, :], st[:, 1, :], ACT.Sqrt).then_inc(s_rms, 1)

            def layer(l, c0):
                norm(2 * l)
                if l == 0:
                    act.wait_ge(s_pcol, 1)
                hT_hi(3 * l, 8 * l)
                c = c0
                for n in range(9):
                    ahead(c)
                    ahead(c + 1)
                    c += 2
                    act.wait_ge(s_z, 9 * l + n + 1)
                    if n == 0:
                        act.activation(zi[:, 0, :], bank[4][:, 0:IDXW], ACT.Copy).then_inc(s_za, 1)
                    else:
                        act.activation(zb[:, n - 1, 0, :], bank[4 + 2 * (n % 2)][:], ACT.Copy).then_inc(s_za, 1)
                act.wait_ge(s_zd, 9 * (l + 1))
                chainless = act.wait_ge(s_za, 9 * (l + 1))
                act.activation(zb[:, ZGA:ZGA + 4].rearrange("p b t n -> p (b t n)"),
                               zb[:, ZGA:ZGA + 4].rearrange("p b t n -> p (b t n)"), ACT.Sigmoid).then_inc(s_sg, 1)
                act.wait_ge(s_idxT, l + 1)
                act.activation(qiT[:].rearrange("p c t -> p (c t)"), bank[0][:], ACT.Copy).then_inc(s_idxs, 1)
                act.activation(kiT[:], bank[1][:, 0:S], ACT.Copy).then_inc(s_idxs, 1)
                for t in range(TT):
                    nk = P * (t + 1)
                    act.wait_ge(s_dot, 2 * l + t + 1)
                    if t:
                        act.wait_ge(s_sc, 2 * l + t)
                    for j in range(4):
                        ins = act.activation(L[:, 2 * j:2 * j + 2, 0:nk],
                                             bank[4 * t + j][:].rearrange("p (c s) -> p c s", s=S)[:, :, 0:nk],
                                             ACT.Relu, scale=IDIM ** -0.5)
                    ins.then_inc(s_rel, 1)
                    if t == 0:
                        act.wait_ge(s_qms, l + 1)
                        act.activation(hs32[:, 1, :], hs32[:, 0, :], ACT.Sqrt).then_inc(s_qrm, 1)
                for j in range(4):
                    act.wait_ge(s_qkT, 4 * l + j + 1)
                    dst = (qT if j < 2 else kT)[:, 2 * (j % 2):2 * (j % 2) + 2, :]
                    act.activation(dst, bank[j][:].rearrange("p (k t) -> p k t", t=S), ACT.Copy).then_inc(s_qks, 1)
                Pr = zb[:, 0:2].rearrange("p b t (h s) -> p (b t h) s", s=S)
                for t in range(TT):
                    nk = P * (t + 1)
                    act.wait_ge(s_mx, 2 * l + t + 1)
                    if t:
                        act.wait_ge(s_pt, 6 * l + 2)
                    for h in range(HEADS):
                        ins = act.activation(Pr[:, h, 0:nk], L[:, h, 0:nk], ACT.Exp, bias=sx[:, t, 1, h:h + 1],
                                             accum_out=sx[:, t, 2, h:h + 1])
                    ins.then_inc(s_ex, 1)
                    for j in range(t + 1):
                        act.wait_ge(s_pt, 6 * l + 2 * t + 2 * j + 1)
                        act.activation(PT[:, j, 0:4, :], bank[4 * t + 2 * j][:].rearrange("p (h s) -> p h s", s=P),
                                       ACT.Copy).then_inc(s_pta, 1)
                for j in range(2):
                    act.wait_ge(s_df, 2 * l + j + 1)
                    act.activation(diffT[:, 2 * j:2 * j + 2, :], bank[4 + j][:].rearrange("p (k t) -> p k t", t=S),
                                   ACT.Copy).then_inc(s_dfs, 1)
                for j in range(2):
                    act.wait_ge(s_pp, 2 * l + j + 1)
                    for q in range(2):
                        g = 2 * j + q
                        ins = act.activation(pThi[:, g, :], bank[6 + j][:, q * S:q * S + S], ACT.Copy,
                                             scale=pcol[:, 32 + 4 * l + g:33 + 4 * l + g])
                    ins.then_inc(s_phi, 1)
                for j in range(2):
                    act.wait_ge(s_aT, 2 * l + j + 1)
                    act.activation(aThi[:, 2 * j:2 * j + 2, :], bank[j][:].rearrange("p (k t) -> p k t", t=S),
                                   ACT.Copy).then_inc(s_ahi, 1)
                for _ in range(4):
                    ahead(c)
                    c += 1
                hT_hi(3 * l + 1, None)
                for _ in range(4):
                    ahead(c)
                    c += 1
                norm(2 * l + 1)
                hT_hi(3 * l + 2, 16 + 8 * l)

            for c in range(LOOK):
                split(c, chunk_words(c))
            layer(0, 0)

            def silu_d(b, q):
                act.wait_ge(s_fb, b + 1)
                for t in range(TT):
                    ins = act.activation(sgD[:, q, t, :], bank[4 + 2 * q + t][:, 0:256], ACT.Silu)
                ins.then_inc(s_si, 1)

            def hid_hi_d(b, q):
                act.wait_ge(s_ft, b + 1)
                act.activation(hidDhi[:, bass.ds(b * 2, 2), :] if not isinstance(b, int) else hidDhi[:, 2 * b:2 * b + 2, :],
                               bank[q][:].rearrange("p (k t) -> p k t", t=S), ACT.Copy).then_inc(s_fhi, 1)

            for b in (0,):
                ahead(DENSE0)
                ahead(DENSE0 + 1)
                silu_d(0, 0)
            with act.Fori(0, 4) as it:
                for u in range(2):
                    c = DENSE0 + 2 + 2 * u
                    split(c + LOOK, FULL, it)
                    hid_hi_d(it * 2 + u, u)
                    split(c + 1 + LOOK, FULL, it)
                    silu_d(it * 2 + (1 + u), 1 - u)
            for b in range(9, NB_D):
                ahead(DENSE0 + 2 * b)
                hid_hi_d(b - 1, (b - 1) % 2)
                ahead(DENSE0 + 2 * b + 1)
                silu_d(b, b % 2)
            hid_hi_d(NB_D - 1, (NB_D - 1) % 2)
            c = DENSE0 + 2 * NB_D
            with act.Fori(0, 4) as it:
                for k in range(SLOTS):
                    split(c + k + LOOK, HALF, it)
            for k in range(16, KC_D):
                ahead(c + k)

            layer(1, LAYER1)

            act.wait_ge(s_xs, 2 * 4)
            for t in range(TT):
                act.activation(xrhi[:, t, :], xs[:, t, :], ACT.Copy).then_inc(s_xr, 1)
            act.activation(identR[:], ident, ACT.Copy)
            act.wait_ge(s_wrl, 16)
            act.activation(wrhi[:], wr[:], ACT.Copy).then_inc(s_wrh, 1)
            act.wait_ge(s_gd, 1)
            act.activation(pr[:, 1, :], pr[:, 0, :], ACT.Exp).then_inc(s_ge, 1)

            def gathered_hi(i):
                for j in range(2):
                    act.wait_ge(s_g, i * 2 + (j + 1))
                    for q in range(4):
                        k = 4 * j + q
                        ins = act.activation(hehi[:, k, :], bank[2 + j][:, q * P:q * P + P], ACT.Copy,
                                             scale=pcol[:, 24 + k:25 + k])
                    ins.then_inc(s_ghi, 1)

            gathered_hi(0)
            act.wait_ge(s_tab, 1)
            njobs = act.value_load(tabi[0:1, 15:16], min_val=E, max_val=NJ - 1)
            with act.Fori(0, njobs) as i:
                jd = JOB_CHUNKS // SLOTS

                def silu_m(b, q):
                    act.wait_ge(m_fb, i * NB_E + b + 1)
                    act.activation(sgM[:, q, :], bank[4 + q][:, 0:256], ACT.Silu).then_inc(m_si, 1)

                def hid_hi_m(b, q):
                    act.wait_ge(m_ft, i * NB_E + b + 1)
                    dst = hidMhi[:, 2 * b:2 * b + 2, :] if isinstance(b, int) else hidMhi[:, bass.ds(b * 2, 2), :]
                    act.activation(dst, bank[q][:, 0:256].rearrange("p (k t) -> p k t", t=P),
                                   ACT.Copy).then_inc(m_fhi, 1)

                def pair(it, n, first=False):
                    for u in range(2):
                        c = MOE0 + 2 * u
                        split(c + LOOK, n, i * jd + it)
                        if first and u == 0:
                            act.wait_ge(s_st, i + 1)
                            act.activation(selT[:], bank[1][:, 0:S], ACT.Copy).then_inc(s_sts, 1)
                        else:
                            hid_hi_m(it * 2 + (u - 1), 1 - u)
                        split(c + 1 + LOOK, n, i * jd + it)
                        silu_m(it * 2 + u, u)

                pair(0, FULL, first=True)
                with act.Fori(1, 6) as it:
                    pair(it, FULL)
                pair(6, HALF)
                d0 = MOE0 + 2 * NB_E
                for k in range(SLOTS):
                    split(d0 + k + LOOK, HALF, i * jd)
                gathered_hi(i + 1)
                hid_hi_m(NB_E - 1, (NB_E - 1) % 2)
                with act.Fori(1, 6) as it:
                    for k in range(SLOTS):
                        split(d0 + k + LOOK, HALF, i * jd + it)
                for k in range(SLOTS):
                    split(d0 + k + LOOK, FULL, i * jd + 6)
                act.wait_ge(m_w2, i + 1)
                for j in range(2):
                    act.activation(yhi[:, 512 * j:512 * j + 512], bank[6 + j][:], ACT.Copy).then_inc(m_yhi, 1)

        @block.tensor
        def _(pe):
            def three(dst, ahi, alo, bhi, blo, start, stop):
                pe.matmul(dst, ahi, bhi, start=start, stop=False)
                pe.matmul(dst, ahi, blo, start=False, stop=False)
                return pe.matmul(dst, alo, bhi, start=False, stop=stop)

            def weights(c, n, width):
                s = c % SLOTS
                return [t[:, s, 0:n * width].rearrange("p (k n) -> p k n", n=width) for t in (whi, wlo)]

            def chunk(c, dst, ahi, alo, k0, width, start, stop, dyn=0, tiles=TT, n=4):
                pe.wait_ge(s_lo, dyn * SLOTS + c + 1)
                bhi, blo = weights(c, n, width)
                for t in range(tiles):
                    for k in range(n):
                        a = [x[:, k0 + k, t * P:(t + 1) * P] for x in (ahi, alo)]
                        ins = three(dst[t], *a, bhi[:, k, :], blo[:, k, :], start and k == 0, stop and k == n - 1)
                ins.then_inc(s_use, 1)
                return ins

            def transposes_hT(te, src):
                for j in range(4):
                    for q in range(2):
                        for t in range(TT):
                            ins = pe.transpose(bank[j][:, q * S + t * P:q * S + t * P + P], src(2 * j + q, t), ident)
                    ins.then_inc(s_tr, 1)

            def norm_T(k, te):
                pe.wait_ge(s_xs, TT * (k + 1))
                transposes_hT(te, lambda kc, t: xs[:, t, kc * P:kc * P + P])

            def layer(l, c0):
                norm_T(2 * l, 3 * l)
                pe.wait_ge(s_tlo, 4 * (3 * l + 1))
                c = c0
                for n in range(9):
                    if n >= 2:
                        pe.wait_ge(s_za, 9 * l + n - 1)
                        pe.wait_ge(s_zd, 9 * l + n - 1)
                    w = IDXW if n == 0 else 512
                    b = [bank[4 + 2 * (n % 2) + t][:, 0:w] for t in range(TT)]
                    chunk(c, b, hThi, hTlo, 0, w, True, False)
                    last = chunk(c + 1, b, hThi, hTlo, 4, w, False, True)
                    pe.nop().then_inc(s_z, 1)
                    c += 2
                pe.wait_ge(s_idx, l + 1)
                for hc in range(2):
                    for t in range(TT):
                        pe.transpose(bank[0][:, hc * S + t * P:hc * S + t * P + P], zi[:, t, hc * P:hc * P + P], ident)
                for t in range(TT):
                    ins = pe.transpose(bank[1][:, t * P:t * P + P], ao[:, t, 0:4 * IDIM], ident)
                ins.then_inc(s_idxT, 1)
                pe.wait_ge(s_idxs, 2 * (l + 1))
                for t in range(TT):
                    nk = P * (t + 1)
                    if t:
                        pe.wait_ge(s_za, 9 * (l + 1))
                        pe.wait_ge(s_zd, 9 * (l + 1))
                    for hc in range(2):
                        for r in range(4):
                            rows = slice(32 * r, 32 * r + 32)
                            ins = pe.matmul(bank[4 * t + r][:, hc * S:hc * S + nk], qiT[rows, hc, t * P:t * P + P],
                                            kiT[rows, 0:nk], start=True, stop=True)
                    ins.then_inc(s_dot, 1)
                pe.wait_ge(s_qk, l + 1)
                pe.wait_ge(s_rel, 2 * l + 1)
                for j in range(4):
                    z = zb[:, ZQ if j < 2 else ZK]
                    for q in range(2):
                        hp = 2 * (j % 2) + q
                        for t in range(TT):
                            ins = pe.transpose(bank[j][:, q * S + t * P:q * S + t * P + P],
                                               z[:, t, hp * P:hp * P + P], ident)
                    ins.then_inc(s_qkT, 1)
                pe.wait_ge(s_qks, 4 * (l + 1))
                for t in range(TT):
                    nk = P * (t + 1)
                    if t:
                        pe.wait_ge(s_rel, 2 * l + 2)
                    for hp in range(4):
                        for p in range(2):
                            rows = slice(64 * p, 64 * p + 64)
                            ins = pe.matmul(bank[4 * t + 2 * p + hp // 2][:, (hp % 2) * S:(hp % 2) * S + nk],
                                            qT[rows, hp, t * P:t * P + P], kT[rows, hp, 0:nk], start=True, stop=True)
                    ins.then_inc(s_lg, 1)
                Pr = zb[:, 0:2].rearrange("p b t (h s) -> p (b t h) s", s=S)
                for t in range(TT):
                    pe.wait_ge(s_ex, 2 * l + t + 1)
                    for j in range(t + 1):
                        for q in range(2):
                            for h in range(4):
                                ins = pe.transpose(bank[4 * t + 2 * j + q][:, h * P:h * P + P],
                                                   Pr[:, 4 * q + h, j * P:j * P + P], ident)
                            ins.then_inc(s_pt, 1)
                    pe.wait_ge(s_pta, 3 * l + 2 * t + 1)
                    pe.wait_ge(s_ptd, 3 * l + 2 * t + 1)
                    for h in range(HEADS):
                        i = (h % 2) * 4 + h // 2
                        for j in range(t + 1):
                            ins = pe.matmul(bank[2 + t][:, h * HD:h * HD + HD], PT[:, j, i, :],
                                            zb[:, ZV, j, h * HD:h * HD + HD], start=(j == 0), stop=(j == t))
                    ins.then_inc(s_pv, 1)
                for s in s_pool:
                    pe.wait_ge(s, 16 * (l + 1))
                for j in range(2):
                    for q in range(2):
                        g = 2 * j + q
                        for t in range(TT):
                            rhs = band[:, g, 0:S] if t == 0 else band[:, g, S:S + P]
                            ins = pe.matmul(bank[4 + j][:, q * S + t * P:q * S + S], zb[:, ZU, t, g * P:g * P + P], rhs,
                                            start=(t == 0), stop=(t == 1), skip_group_check=True)
                    ins.then_inc(s_df, 1)
                for j in range(2):
                    pe.wait_ge(s_dfs, 2 * l + j + 1)
                    for q in range(2):
                        g = 2 * j + q
                        ins = pe.matmul(bank[6 + j][:, q * S:q * S + S], wpool[:, g, :], diffT[:, g, :],
                                        start=True, stop=True)
                    ins.then_inc(s_pp, 1)
                pe.wait_ge(s_ao, 2 * (l + 1))
                for j in range(2):
                    for q in range(2):
                        for t in range(TT):
                            k = 2 * j + q
                            ins = pe.transpose(bank[j][:, q * S + t * P:q * S + t * P + P], ao[:, t, k * P:k * P + P],
                                               ident)
                    ins.then_inc(s_aT, 1)
                pe.wait_ge(s_alo, 2 * (l + 1))
                pe.wait_ge(s_plo, 2 * (l + 1))
                for nh in range(2):
                    for j, (hi, lo) in enumerate(((aThi, aTlo), (pThi, pTlo))):
                        chunk(c, [bank[4 * nh + 2 * j + t][:] for t in range(TT)], hi, lo, 0, 512, True, True)
                        pe.nop().then_inc(s_pj, 1)
                        c += 1
                pe.wait_ge(s_m, 2 * (l + 1))
                transposes_hT(3 * l + 1, lambda kc, t: zb[:, ZGA + kc // 4, t, (kc % 4) * P:(kc % 4) * P + P])
                pe.wait_ge(s_tlo, 4 * (3 * l + 2))
                for nh in range(2):
                    b = [bank[4 + 2 * nh + t][:] for t in range(TT)]
                    chunk(c, b, hThi, hTlo, 0, 512, True, False)
                    chunk(c + 1, b, hThi, hTlo, 4, 512, False, True)
                    pe.nop().then_inc(s_wo, 1)
                    c += 2
                norm_T(2 * l + 1, 3 * l + 2)
                pe.wait_ge(s_tlo, 4 * (3 * l + 3))

            pe.wait_ge(s_cst, 16)
            pe.wait_ge(s_par, 7 * 16)
            pe.transpose(bank[6][:, 0:40], prow[:], cst[0:40, C_ID:C_ID + 40])
            pe.matmul(bank[7][:, 0:4 * HD], cst[0:1, C_ONE:C_ONE + P], nrow[:], start=True, stop=True).then_inc(s_prt, 1)
            layer(0, 0)

            def hiddenT_d(b, q):
                pe.wait_ge(s_hm, b + 1)
                for f in range(2):
                    for t in range(TT):
                        ins = pe.transpose(bank[q][:, f * S + t * P:f * S + t * P + P],
                                           hsD[:, q, t, f * P:f * P + P], ident)
                ins.then_inc(s_ft, 1)

            def block_d(b, q, c, dyn, prev=True, prev2=True):
                dst = [bank[4 + 2 * q + t][:] for t in range(TT)]
                chunk(c, dst, hThi, hTlo, 0, 512, True, False, dyn)
                if prev:
                    if prev2:
                        pe.wait_ge(s_flo, b - 2 + LEAD)
                    hiddenT_d(b - 1, 1 - q)
                chunk(c + 1, dst, hThi, hTlo, 4, 512, False, True, dyn)
                pe.nop().then_inc(s_fb, 1)

            block_d(0, 0, DENSE0, 0, prev=False)
            with pe.Fori(0, 5) as it:
                for u in range(2):
                    block_d(it * 2 + (1 + u), 1 - u, DENSE0 + 2 + 2 * u, it)
            hiddenT_d(NB_D - 1, (NB_D - 1) % 2)
            for k in range(KC_D):
                c = DENSE0 + 2 * NB_D + k
                pe.wait_ge(s_flo, k // 2 + 1 + LEAD)
                pe.wait_ge(s_lo, c + 1)
                if k == 0:
                    pe.wait_ge(s_hm, NB_D)
                for t in range(TT):
                    a = [x[:, k, t * P:t * P + P] for x in (hidDhi, hidDlo)]
                    for nh in range(2):
                        w = [x[:, c % SLOTS, 512 * nh:512 * nh + 512] for x in (whi, wlo)]
                        ins = three(bank[4 + 2 * t + nh][:], *a, *w, k == 0, k == KC_D - 1)
                ins.then_inc(s_use, 1)
            pe.nop().then_inc(s_w2, 1)

            layer(1, LAYER1)

            pe.wait_ge(s_wrh, 2)
            for t in range(TT):
                for k in range(KC):
                    ins = three(bank[4][:, t * E:t * E + E], hThi[:, k, t * P:t * P + P], hTlo[:, k, t * P:t * P + P],
                                wrhi[:, k, :], wrlo[:, k, :], k == 0, k == KC - 1)
            ins.then_inc(s_rt, 1)
            pe.wait_ge(s_mk, 1)
            tri, ones = cst[:, C_TRI:C_TRI + P], cst[:, C_ONE:C_ONE + P]
            pe.matmul(bank[5][:, 0:E], tri, tmp8[:, 0, :], start=True, stop=True)
            pe.matmul(bank[5][:, E:2 * E], tri, tmp8[:, 1, :], start=True, stop=False)
            pe.matmul(bank[5][:, E:2 * E], ones, tmp8[:, 0, :], start=False, stop=True)
            pe.matmul(bank[5][:, 2 * E:3 * E], ones, tmp8[:, 0, :], start=True, stop=False)
            pe.matmul(bank[5][:, 2 * E:3 * E], ones, tmp8[:, 1, :], start=False, stop=True).then_inc(s_pos, 1)

            def gather(i):
                pe.wait_ge(s_sel, i + 1)
                for j in range(2):
                    for q in range(4):
                        k = 4 * j + q
                        for t in range(TT):
                            for x in (xrhi, xrlo):
                                ins = pe.matmul(bank[2 + j][:, q * P:q * P + P], x[:, t, k * P:k * P + P],
                                                selR[:, t, :], start=(t == 0 and x is xrhi),
                                                stop=(t == TT - 1 and x is xrlo))
                    ins.then_inc(s_g, 1)

            pe.wait_ge(s_xrl, 2)
            gather(0)
            pe.wait_ge(s_tab, 1)
            njobs = pe.value_load(tabi[0:1, 15:16], min_val=E, max_val=NJ - 1)
            with pe.Fori(0, njobs) as i:
                jd = JOB_CHUNKS // SLOTS

                def hiddenT_m(b, q):
                    pe.wait_ge(m_hm, i * NB_E + b + 1)
                    for f in range(2):
                        ins = pe.transpose(bank[q][:, f * P:f * P + P], hsM[:, q, f * P:f * P + P], ident)
                    ins.then_inc(m_ft, 1)

                def pair(it, first=False):
                    for u in range(2):
                        c = MOE0 + 2 * u
                        b = it * 2 + u
                        if not first:
                            pe.wait_ge(m_hm, i * NB_E + b - 1)
                        chunk(c, [bank[4 + u][:]], hehi, helo, 0, 512, True, False, i * jd + it, tiles=1)
                        if first and u == 0:
                            pe.wait_ge(m_xa, i * 4 + LEAD)
                            for t in range(TT):
                                ins = pe.matmul(bank[1][:, t * P:t * P + P], selR[:, t, :], identR[:],
                                                start=True, stop=True)
                            ins.then_inc(s_st, 1)
                        else:
                            if not first:
                                pe.wait_ge(m_flo, i * NB_E + b - 2 + LEAD)
                            hiddenT_m(b - 1, 1 - u)
                        chunk(c + 1, [bank[4 + u][:]], hehi, helo, 4, 512, False, True, i * jd + it, tiles=1)
                        pe.nop().then_inc(m_fb, 1)

                pe.wait_ge(s_glo, i * 2 + 2)
                pair(0, first=True)
                with pe.Fori(1, NB_E // 2) as it:
                    pair(it)
                pe.wait_ge(s_sel, i + 2)
                gather(i + 1)
                for k in range(KC_E):
                    c = MOE0 + 2 * NB_E + k
                    if k == 4:
                        hiddenT_m(NB_E - 1, (NB_E - 1) % 2)
                    if k == 0:
                        pe.wait_ge(m_flo, i * NB_E + NB_E - 1 + LEAD)
                    if k == KC_E - 2:
                        pe.wait_ge(m_flo, i * NB_E + NB_E + LEAD)
                    pe.wait_ge(s_lo, i * JOB_CHUNKS + c + 1)
                    for nh in range(2):
                        w = [x[:, c % SLOTS, 512 * nh:512 * nh + 512] for x in (whi, wlo)]
                        ins = three(bank[6 + nh][:], hidMhi[:, k, :], hidMlo[:, k, :], *w, k == 0, k == KC_E - 1)
                    ins.then_inc(s_use, 1)
                pe.nop().then_inc(m_w2, 1)
                pe.wait_ge(m_ylo, i * 2 + 2)
                pe.wait_ge(s_sts, i + 1)
                pe.wait_ge(s_glo, i * 2 + 4)
                for t in range(TT):
                    for nh in range(2):
                        for y in (yhi, ylo):
                            ins = pe.matmul(bank[2 * t + nh][:], selT[:, t * P:t * P + P],
                                            y[:, 512 * nh:512 * nh + 512], start=(y is yhi), stop=(y is ylo))
                        ins.then_inc(m_sc, 1)

        @block.vector
        def _(dve):
            steps = [0]

            def chain(ins):
                steps[0] += 1
                ins.then_inc(s_dve, 1)
                dve.wait_ge(s_dve, steps[0])

            def split(c, n, dyn=0):
                dve.wait_ge(s_hi, dyn * SLOTS + c + 1)
                s = c % SLOTS
                dve.tensor_tensor(wlo[:, s, 0:n], raw[:, s, 0:n], whi[:, s, 0:n], ALU.subtract).then_inc(s_lo, 1)

            def ahead(c):
                split(c + LOOK, chunk_words(c + LOOK) if c + LOOK < MOE0 else FULL)

            def hT_lo(te, scale0):
                for j in range(4):
                    dve.wait_ge(s_thi, 4 * te + j + 1)
                    if scale0 is None:
                        dve.tensor_tensor(hTlo[:, 2 * j:2 * j + 2, :], bank[j][:].rearrange("p (k t) -> p k t", t=S),
                                          hThi[:, 2 * j:2 * j + 2, :], ALU.subtract).then_inc(s_tlo, 1)
                        continue
                    for q in range(2):
                        k = 2 * j + q
                        ins = dve.scalar_tensor_tensor(hTlo[:, k, :], bank[j][:, q * S:q * S + S],
                                                       pcol[:, scale0 + k:scale0 + k + 1], hThi[:, k, :],
                                                       ALU.mult, ALU.subtract)
                    ins.then_inc(s_tlo, 1)

            def rsqrt(r, rms, ms, t):
                chain(dve.reciprocal(r, rms))
                chain(dve.tensor_tensor(t, r, r, ALU.mult))
                chain(dve.tensor_tensor(t, t, ms, ALU.mult))
                chain(dve.tensor_scalar(t, t, -0.5, 1.5, ALU.mult, ALU.add))
                chain(dve.tensor_tensor(r, r, t, ALU.mult))

            def norm(k):
                dve.wait_ge(s_sq, TT * (k + 1))
                dve.tensor_scalar(st[:, 1, :], st[:, 0, :], 1.0 / D, EPS, ALU.mult, ALU.add).then_inc(s_ms, 1)
                dve.wait_ge(s_rms, k + 1)
                dve.wait_ge(s_ms, k + 1)
                rsqrt(st[:, 3, :], st[:, 2, :], st[:, 1, :], st[:, 0, :])
                for t in range(TT):
                    dve.tensor_scalar(xs[:, t, :], X[:, t, :], st[:, 3, t:t + 1], None, ALU.mult).then_inc(s_xs, 1)

            def rope(v, half, cos, sin, tmp):
                x1, x2 = v[:, :, :, 0:half], v[:, :, :, half:2 * half]
                dve.tensor_tensor(tmp[0], x1, cos, ALU.mult)
                dve.tensor_tensor(tmp[1], x2, sin, ALU.mult)
                dve.tensor_tensor(tmp[2], x2, cos, ALU.mult)
                chain(dve.tensor_tensor(tmp[3], x1, sin, ALU.mult))
                dve.tensor_tensor(x1, tmp[0], tmp[1], ALU.subtract)
                return dve.tensor_tensor(x2, tmp[2], tmp[3], ALU.add)

            def table(off, half, heads):
                v = cst[:, off:off + TT * half].rearrange("p (t o d) -> p t o d", t=TT, o=1)
                return v.broadcast_to([P, TT, heads, half])

            def layer(l, c0):
                norm(2 * l)
                if l == 0:
                    dve.wait_ge(s_pcol, 2)
                hT_lo(3 * l, 8 * l)
                c = c0
                for n in range(9):
                    ahead(c)
                    ahead(c + 1)
                    c += 2
                    dve.wait_ge(s_z, 9 * l + n + 1)
                    if n == 0:
                        dve.tensor_copy(zi[:, 1, :], bank[5][:, 0:IDXW]).then_inc(s_zd, 1)
                    else:
                        dve.tensor_copy(zb[:, n - 1, 1, :], bank[5 + 2 * (n % 2)][:]).then_inc(s_zd, 1)
                dve.wait_ge(s_za, 9 * (l + 1))
                dve.wait_ge(s_zd, 9 * (l + 1))
                flat = PT[:].rearrange("p a h s -> p (a h s)")

                def tmps(heads, half):
                    n = TT * heads * half
                    return [flat[:, i * n:i * n + n].rearrange("p (t h d) -> p t h d", t=TT, h=heads) for i in range(4)]

                zh = zi[:, :, 0:9 * IDIM].rearrange("p t (h d) -> p t h d", d=IDIM)
                chain(rope(zh, IROT // 2, table(C_COSI, IROT // 2, 9), table(C_SINI, IROT // 2, 9), tmps(9, IROT // 2)))
                dve.tensor_copy(ki4, zh[:, :, 8:9, :].broadcast_to([P, TT, 4, IDIM]))
                dve.tensor_scalar(wis[:], zi[:, :, 9 * IDIM:IDXW], IH ** -0.5, None, ALU.mult).then_inc(s_idx, 1)
                zq = zb[:, 0:2].rearrange("p b t n -> p (b t n)")
                zqh = zb[:, 0:2].rearrange("p b t (h d) -> p (b t h) d", d=HD)
                chain(dve.tensor_tensor(flat, zq, zq, ALU.mult))
                chain(dve.tensor_reduce(hs32[:, 2, :], flat.rearrange("p (g d) -> p g d", d=HD), AX.X, ALU.add))
                chain(dve.tensor_scalar(hs32[:, 0, :], hs32[:, 2, :], 1.0 / HD, EPS, ALU.mult, ALU.add))
                dve.nop().then_inc(s_qms, 1)

                def scores(t):
                    nk = P * (t + 1)
                    w = work[:, t * P:t * P + nk]
                    dve.wait_ge(s_rel, 2 * l + t + 1)
                    for i in range(HEADS):
                        h = (i % 2) * 4 + i // 2
                        if i == 0:
                            chain(dve.tensor_scalar(w, L[:, i, 0:nk], wis[:, t, h:h + 1], None, ALU.mult))
                        else:
                            chain(dve.scalar_tensor_tensor(w, L[:, i, 0:nk], wis[:, t, h:h + 1], w, ALU.mult, ALU.add))
                    d = work[:, 2 * t * P:2 * t * P + P]
                    chain(dve.tensor_tensor(d, d, cst[:, C_NEG:C_NEG + P], ALU.add))
                    dve.nop().then_inc(s_sc, 1)

                scores(0)
                dve.wait_ge(s_qrm, l + 1)
                rsqrt(hs32[:, 2, :], hs32[:, 1, :], hs32[:, 0, :], flat[:, 0:32])
                chain(dve.tensor_tensor(zqh, zqh, hs32[:, 2, :].rearrange("p (g o) -> p g o", o=1).broadcast_to([P, 32, HD]),
                                        ALU.mult))
                for b in range(2):
                    g = gain[:, l, b:b + 1, :].broadcast_to([P, TT * HEADS, HD])
                    v = zb[:, b].rearrange("p t (h d) -> p (t h) d", d=HD)
                    chain(dve.tensor_tensor(v, v, g, ALU.mult))
                for b in range(2):
                    v = zb[:, b].rearrange("p t (h d) -> p t h d", d=HD)
                    ins = rope(v, ROT // 2, table(C_COS, ROT // 2, HEADS), table(C_SIN, ROT // 2, HEADS),
                               tmps(HEADS, ROT // 2))
                    if b == 0:
                        chain(ins)
                ins.then_inc(s_qk, 1)
                scores(1)
                w = [work[:, 0:P], work[:, P:P + S]]
                for r in range(TOPK // 8):
                    for t in range(TT):
                        chain(dve.max(m8[:, t, :], w[t]))
                    for t in range(TT):
                        chain(dve.match_replace(w[t], m8[:, t, :], w[t], MARK))
                chain(dve.tensor_scalar(madd[:], work[:], MARK, MASKED, ALU.not_equal, ALU.mult))
                for t in range(TT):
                    d = madd[:, 2 * t * P:2 * t * P + P]
                    chain(dve.tensor_tensor(d, d, cst[:, C_NEG:C_NEG + P], ALU.add))
                for t in range(TT):
                    nk = P * (t + 1)
                    dve.wait_ge(s_lg, 2 * l + t + 1)
                    if t:
                        dve.wait_ge(s_ex, 2 * l + t)
                    ma = madd[:, t * P:t * P + nk].rearrange("p (o s) -> p o s", o=1).broadcast_to([P, 2, nk])
                    for j in range(4):
                        ins = dve.scalar_tensor_tensor(L[:, 2 * j:2 * j + 2, 0:nk],
                                                       bank[4 * t + j][:].rearrange("p (c s) -> p c s", s=S)[:, :, 0:nk],
                                                       HD ** -0.5, ma, ALU.mult, ALU.add)
                    chain(ins)
                    chain(dve.tensor_reduce(sx[:, t, 0, :], L[:, :, 0:nk], AX.X, ALU.max))
                    dve.tensor_scalar(sx[:, t, 1, :], sx[:, t, 0, :], -1.0, None, ALU.mult).then_inc(s_mx, 1)
                    for j in range(t + 1):
                        dve.wait_ge(s_pt, 6 * l + 2 * t + 2 * j + 2)
                        if t and j == 0:
                            dve.wait_ge(s_pv, 2 * l + 1)
                        dve.tensor_copy(PT[:, j, 4:8, :], bank[4 * t + 2 * j + 1][:].rearrange("p (h s) -> p h s", s=P)
                                        ).then_inc(s_ptd, 1)
                    dve.wait_ge(s_ex, 2 * l + t + 1)
                    chain(dve.reciprocal(sx[:, t, 3, :], sx[:, t, 2, :]))
                    dve.wait_ge(s_pv, 2 * l + t + 1)
                    dve.tensor_tensor(ao[:, t, :].rearrange("p (a q d) -> p a q d", a=4, q=2),
                                      bank[2 + t][:].rearrange("p (a q d) -> p a q d", a=4, q=2),
                                      sx[:, t, 3, :].rearrange("p (q a o) -> p a q o", q=2, o=1).broadcast_to([P, 4, 2, HD]),
                                      ALU.mult).then_inc(s_ao, 1)
                for j in range(2):
                    dve.wait_ge(s_phi, 2 * l + j + 1)
                    for q in range(2):
                        g = 2 * j + q
                        ins = dve.scalar_tensor_tensor(pTlo[:, g, :], bank[6 + j][:, q * S:q * S + S],
                                                       pcol[:, 32 + 4 * l + g:33 + 4 * l + g], pThi[:, g, :],
                                                       ALU.mult, ALU.subtract)
                    ins.then_inc(s_plo, 1)
                for j in range(2):
                    dve.wait_ge(s_ahi, 2 * l + j + 1)
                    dve.tensor_tensor(aTlo[:, 2 * j:2 * j + 2, :], bank[j][:].rearrange("p (k t) -> p k t", t=S),
                                      aThi[:, 2 * j:2 * j + 2, :], ALU.subtract).then_inc(s_alo, 1)
                dve.wait_ge(s_sg, l + 1)
                for nh in range(2):
                    for _ in range(2):
                        ahead(c)
                        c += 1
                    dve.wait_ge(s_pj, 4 * l + 2 * nh + 2)
                    ga, gp = zb[:, ZGA + nh], zb[:, ZGP + nh]
                    for t in range(TT):
                        dve.tensor_tensor(ga[:, t], ga[:, t], bank[4 * nh + t][:], ALU.mult)
                        ins = dve.tensor_tensor(gp[:, t], gp[:, t], bank[4 * nh + 2 + t][:], ALU.mult)
                    chain(ins)
                    dve.tensor_tensor(ga, ga, gp, ALU.add).then_inc(s_m, 1)
                hT_lo(3 * l + 1, None)
                for nh in range(2):
                    for _ in range(2):
                        ahead(c)
                        c += 1
                    dve.wait_ge(s_wo, 2 * l + nh + 1)
                    for t in range(TT):
                        v = X[:, t, 512 * nh:512 * nh + 512]
                        ins = dve.tensor_tensor(v, v, bank[4 + 2 * nh + t][:], ALU.add)
                ins.then_inc(s_xd, 1)
                norm(2 * l + 1)
                hT_lo(3 * l + 2, 16 + 8 * l)

            for s in (s_flo, m_flo, m_xa):
                dve.nop().then_inc(s, LEAD)
            dve.wait_ge(s_prt, 1)
            dve.tensor_copy(pcol[:], bank[6][:, 0:40]).then_inc(s_pcol, 1)
            dve.tensor_copy(gain[:].rearrange("p l j d -> p (l j d)"), bank[7][:, 0:4 * HD]).then_inc(s_pcol, 1)
            for c in range(LOOK):
                split(c, chunk_words(c))
            layer(0, 0)

            def mul_d(b, q):
                dve.wait_ge(s_si, b + 1)
                for t in range(TT):
                    ins = dve.tensor_tensor(hsD[:, q, t, :], sgD[:, q, t, :], bank[4 + 2 * q + t][:, 256:512], ALU.mult)
                ins.then_inc(s_hm, 1)

            def hid_lo_d(b, q):
                dve.wait_ge(s_fhi, b + 1)
                hi, lo = (x[:, 2 * b:2 * b + 2, :] if isinstance(b, int) else x[:, bass.ds(b * 2, 2), :]
                          for x in (hidDhi, hidDlo))
                dve.tensor_tensor(lo, bank[q][:].rearrange("p (k t) -> p k t", t=S), hi, ALU.subtract).then_inc(s_flo, 1)

            ahead(DENSE0)
            ahead(DENSE0 + 1)
            mul_d(0, 0)
            with dve.Fori(0, 4) as it:
                for u in range(2):
                    c = DENSE0 + 2 + 2 * u
                    split(c + LOOK, FULL, it)
                    hid_lo_d(it * 2 + u, u)
                    split(c + 1 + LOOK, FULL, it)
                    mul_d(it * 2 + (1 + u), 1 - u)
            for b in range(9, NB_D):
                ahead(DENSE0 + 2 * b)
                hid_lo_d(b - 1, (b - 1) % 2)
                ahead(DENSE0 + 2 * b + 1)
                mul_d(b, b % 2)
            hid_lo_d(NB_D - 1, (NB_D - 1) % 2)
            c = DENSE0 + 2 * NB_D
            with dve.Fori(0, 4) as it:
                for k in range(SLOTS):
                    split(c + k + LOOK, HALF, it)
            for k in range(16, KC_D):
                ahead(c + k)
            dve.wait_ge(s_w2, 1)
            for t in range(TT):
                for nh in range(2):
                    v = X[:, t, 512 * nh:512 * nh + 512]
                    ins = dve.tensor_tensor(v, v, bank[4 + 2 * t + nh][:], ALU.add)
            ins.then_inc(s_xd, 1)

            layer(1, LAYER1)

            for t in range(TT):
                dve.wait_ge(s_xr, t + 1)
                dve.tensor_tensor(xrlo[:, t, :], xs[:, t, :], xrhi[:, t, :], ALU.subtract).then_inc(s_xrl, 1)
            dve.wait_ge(s_wrh, 1)
            dve.tensor_tensor(wrlo[:], wr[:], wrhi[:], ALU.subtract).then_inc(s_wrh, 1)
            dve.wait_ge(s_rt, 1)
            chain(dve.tensor_copy(lg[:].rearrange("p t e -> p (t e)"), bank[4][:, 0:TT * E]))
            for t in range(TT):
                chain(dve.max(v8[:, t, :], lg[:, t, :]))
            for t in range(TT):
                chain(dve.max_index(ix8[:, t, :], v8[:, t, :], lg[:, t, :]))
            dve.tensor_tensor(pr[:, 0, :], v8[:, :, 1], v8[:, :, 0], ALU.subtract).then_inc(s_gd, 1)
            chain(dve.tensor_copy(ixf[:], ix8[:]))
            iota8 = cst[:, C_IOTA:C_IOTA + E]
            for t in range(TT):
                dve.tensor_scalar(m0[:, t, :], iota8, ixf[:, t, 0:1], None, ALU.is_equal)
                chain(dve.tensor_scalar(m1[:, t, :], iota8, ixf[:, t, 1:2], None, ALU.is_equal))
            chain(dve.tensor_tensor(tmp8[:], m0[:], m1[:], ALU.add))
            dve.nop().then_inc(s_mk, 1)
            dve.wait_ge(s_ge, 1)
            chain(dve.tensor_scalar(pr[:, 2, :], pr[:, 1, :], 1.0, None, ALU.add))
            chain(dve.reciprocal(pr[:, 2, :], pr[:, 2, :]))
            chain(dve.tensor_tensor(pr[:, 3, :], pr[:, 1, :], pr[:, 2, :], ALU.mult))
            for t in range(TT):
                chain(dve.tensor_scalar(gate[:, t, :], m0[:, t, :], pr[:, 2, t:t + 1], None, ALU.mult))
                chain(dve.scalar_tensor_tensor(gate[:, t, :], m1[:, t, :], pr[:, 3, t:t + 1], gate[:, t, :],
                                               ALU.mult, ALU.add))
            dve.wait_ge(s_pos, 1)
            pos = bank[5][:, 0:2 * E].rearrange("p (t e) -> p t e", t=TT)
            chain(dve.scalar_tensor_tensor(pm[:], pos, 1.0, tmp8[:], ALU.add, ALU.mult))
            chain(dve.tensor_scalar(pm[:], pm[:], -1.0, None, ALU.add))
            dve.tensor_copy(posj[:, :, 0:E], pm[:])
            chain(dve.tensor_copy(gatej[:, :, 0:E], gate[:]))

            def select(i):
                for t in range(TT):
                    col = posj[:, t, i:i + 1] if isinstance(i, int) else posj[:, t, bass.ds(i, 1)]
                    ins = dve.tensor_scalar(selR[:, t, :], cst[:, C_IOTA:C_IOTA + P], col, None, ALU.is_equal)
                ins.then_inc(s_sel, 1)

            select(0)
            over, cum, rank, one8 = (ov[:, i, :] for i in range(4))
            dve.tensor_scalar(over, bank[5][:, 2 * E:3 * E], float(P), None, ALU.is_gt)
            chain(dve.memset(one8, 1.0))
            chain(dve.tensor_tensor_scan(cum, one8, over, 0.0, ALU.mult, ALU.add))
            chain(dve.tensor_tensor(rank, cum, over, ALU.mult))
            dve.tensor_copy(tabf[:, 0:E], iota8)
            dve.memset(tabf[:, NJ:15], 0.0)
            chain(dve.tensor_scalar(tabf[:, 15:16], cum[:, E - 1:E], float(E), None, ALU.add))
            for q in range(NJ - E):
                chain(dve.tensor_scalar(one8, rank, float(q + 1), None, ALU.is_equal))
                pick = ov[:, 3:4, :].broadcast_to([P, TT, E])
                chain(dve.tensor_tensor(tmp8[:], pm[:], pick, ALU.mult))
                chain(dve.tensor_reduce(pr[:, 0, :], tmp8[:], AX.X, ALU.add))
                dve.tensor_scalar(posj[:, :, E + q], pr[:, 0, :], -float(P), None, ALU.add)
                chain(dve.tensor_tensor(tmp8[:], gate[:], pick, ALU.mult))
                chain(dve.tensor_reduce(gatej[:, :, E + q], tmp8[:], AX.X, ALU.add))
                chain(dve.tensor_tensor(tmp8[:, 0, :], iota8, one8, ALU.mult))
                chain(dve.tensor_reduce(tabf[:, E + q:E + q + 1], tmp8[:, 0, :], AX.X, ALU.add))
            dve.tensor_copy(tabi[:], tabf[:]).then_inc(s_tab, 1)

            def gathered_lo(i):
                for j in range(2):
                    dve.wait_ge(s_ghi, i * 2 + (j + 1))
                    for q in range(4):
                        k = 4 * j + q
                        ins = dve.scalar_tensor_tensor(helo[:, k, :], bank[2 + j][:, q * P:q * P + P],
                                                       pcol[:, 24 + k:25 + k], hehi[:, k, :], ALU.mult, ALU.subtract)
                    ins.then_inc(s_glo, 1)

            gathered_lo(0)
            dve.wait_ge(s_tab, 1)
            njobs = dve.value_load(tabi[0:1, 15:16], min_val=E, max_val=NJ - 1)
            with dve.Fori(0, njobs) as i:
                jd = JOB_CHUNKS // SLOTS

                def mul_m(b, q):
                    dve.wait_ge(m_si, i * NB_E + b + 1)
                    dve.tensor_tensor(hsM[:, q, :], sgM[:, q, :], bank[4 + q][:, 256:512], ALU.mult).then_inc(m_hm, 1)

                def hid_lo_m(b, q):
                    dve.wait_ge(m_fhi, i * NB_E + b + 1)
                    hi, lo = (x[:, 2 * b:2 * b + 2, :] if isinstance(b, int) else x[:, bass.ds(b * 2, 2), :]
                              for x in (hidMhi, hidMlo))
                    dve.tensor_tensor(lo, bank[q][:, 0:256].rearrange("p (k t) -> p k t", t=P), hi,
                                      ALU.subtract).then_inc(m_flo, 1)

                def pair(it, n, first=False):
                    for u in range(2):
                        c = MOE0 + 2 * u
                        split(c + LOOK, n, i * jd + it)
                        if first and u == 0:
                            dve.wait_ge(s_st, i + 1)
                            select(i + 1)
                        else:
                            hid_lo_m(it * 2 + (u - 1), 1 - u)
                        split(c + 1 + LOOK, n, i * jd + it)
                        mul_m(it * 2 + u, u)

                pair(0, FULL, first=True)
                with dve.Fori(1, 6) as it:
                    pair(it, FULL)
                pair(6, HALF)
                d0 = MOE0 + 2 * NB_E
                for k in range(SLOTS):
                    split(d0 + k + LOOK, HALF, i * jd)
                gathered_lo(i + 1)
                hid_lo_m(NB_E - 1, (NB_E - 1) % 2)
                with dve.Fori(1, 6) as it:
                    for k in range(SLOTS):
                        split(d0 + k + LOOK, HALF, i * jd + it)
                for k in range(SLOTS):
                    split(d0 + k + LOOK, FULL, i * jd + 6)
                for j in range(2):
                    dve.wait_ge(m_yhi, i * 2 + j + 1)
                    dve.tensor_tensor(ylo[:, 512 * j:512 * j + 512], bank[6 + j][:], yhi[:, 512 * j:512 * j + 512],
                                      ALU.subtract).then_inc(m_ylo, 1)
                for t in range(TT):
                    for nh in range(2):
                        dve.wait_ge(m_sc, i * 4 + 2 * t + nh + 1)
                        v = X[:, t, 512 * nh:512 * nh + 512]
                        dve.scalar_tensor_tensor(v, bank[2 * t + nh][:], gatej[:, t, bass.ds(i, 1)], v,
                                                 ALU.mult, ALU.add).then_inc(m_xa, 1)


def shape_constants():
    c = np.zeros((P, C_END), np.float32)
    i = np.arange(P)
    c[:, C_ID:C_ID + P] = np.eye(P)
    c[:, C_TRI:C_TRI + P] = i[:, None] < i[None, :]
    c[:, C_NEG:C_NEG + P] = np.where(i[None, :] <= i[:, None], 0.0, NEG)
    c[:, C_IOTA:C_IOTA + P] = i[None, :]
    c[:, C_ONE:C_ONE + P] = 1.0
    pos = np.arange(S, dtype=np.float32)
    for rot, co, so in ((ROT, C_COS, C_SIN), (IROT, C_COSI, C_SINI)):
        inv = np.power(np.float32(THETA), -np.arange(0, rot, 2, dtype=np.float32) / np.float32(rot))
        ang = (pos[:, None] * inv[None, :]).astype(np.float32)
        for f, o in ((np.cos, co), (np.sin, so)):
            t = f(ang.astype(np.float64)).astype(np.float32).reshape(TT, P, rot // 2)
            c[:, o:o + TT * rot // 2] = t.transpose(1, 0, 2).reshape(P, -1)
    band = np.zeros((GROUPS, S, S))
    for g, w in enumerate(WINDOWS):
        for t in range(S):
            band[g, max(0, t - w + 1):t + 1, t] = 1.0 / min(t + 1, w)
            band[g, t, t] -= 1.0
    b = np.concatenate([band[:, 0:P, :], band[:, P:, P:]], axis=2).transpose(1, 0, 2)
    return c, np.ascontiguousarray(b.astype(np.float32))


_INS = ["x", "mix_norm", "w_in", "q_norm", "k_norm", "w_pool", "pool_scale", "w_attn_proj", "w_pool_proj", "w_out",
        "ffn_norm", "dense_w1", "dense_w3", "dense_w2", "moe_router", "moe_w1", "moe_w3", "moe_w2"]


def kernel(**inputs):
    import concourse.bacc as _bacc
    from concourse.bass_utils import run_bass_kernel_spmd as _run

    nc = _bacc.Bacc("TRN2", target_bir_lowering=False, num_devices=1)
    arrays = {f"in_{n}": np.ascontiguousarray(inputs[n]) for n in _INS}
    arrays["in_consts"], arrays["in_pool_band"] = shape_constants()
    A = {n[3:]: nc.dram_tensor(n, a.shape, mybir.dt.from_np(a.dtype), kind="ExternalInput").ap()
         for n, a in arrays.items()}
    o = nc.dram_tensor("out_0", (1, S, D), F32, kind="ExternalOutput").ap()
    build(nc, A, o)
    r = _run(nc, [arrays], core_ids=[0])
    return r.results[0]["out_0"]
```

```python
from contextlib import ExitStack

import numpy as np

import concourse.bass as bass
from concourse import mybir

F32 = mybir.dt.float32
FR = mybir.dt.float32r
I32 = mybir.dt.int32
U32 = mybir.dt.uint32
ALU = mybir.AluOpType
ACT = mybir.ActivationFunctionType
AX = mybir.AxisListType

P = 128
D = 1024
S = 256
TT = S // P
KC = D // P
HEADS, HD, ROT = 8, 64, 16
AW = HEADS * HD
IH, IDIM, IROT = 8, 32, 8
IDXW = IH * IDIM + IDIM + IH
TOPK = 64
GROUPS = 4
WINDOWS = (2, 4, 8, 16)
FF = 2816
E = 8
FFE = 3584
EPS = 1e-6
NEG = -1e38
MARK = -3e38
MASKED = -1e30
THETA = 500000.0

SLOTS = 4
LOOK = SLOTS
LEAD = 2
FULL = 2048
HALF = 1024
NB_D = FF // 256
NB_E = FFE // 256
KC_D = FF // P
KC_E = FFE // P
ZCOL = [0, 512, 1024, 1832, 2344, 2856, 3368, 3880]
ZQ, ZK, ZV, ZU, ZGA, ZGP = 0, 1, 2, 3, 4, 6
MIX_CHUNKS = 2 + 2 * len(ZCOL) + 4 + 4
DENSE0 = MIX_CHUNKS
LAYER1 = DENSE0 + 2 * NB_D + KC_D
MOE0 = LAYER1 + MIX_CHUNKS
JOB_CHUNKS = 2 * NB_E + KC_E
NJ = 12

C_ID, C_TRI, C_NEG, C_IOTA, C_ONE = 0, 128, 256, 384, 512
C_COS, C_SIN, C_COSI, C_SINI = 640, 656, 672, 680
C_END = 688


def chunk_words(c):
    m = c - (LAYER1 if c >= LAYER1 else 0)
    if m < 2:
        return (KC // 2) * IDXW
    if DENSE0 + 2 * NB_D <= c < LAYER1:
        return HALF
    return FULL


def build(nc, A, out):
    with ExitStack() as ctx:
        def sb(name, shape, dt=F32, where=ctx):
            return where.enter_context(nc.sbuf_tensor(name, shape, dt))

        def sem(name):
            return ctx.enter_context(nc.semaphore(name))

        raw = sb("w_raw", [P, SLOTS, FULL])
        whi = sb("w_hi", [P, SLOTS, FULL], FR)
        wlo = sb("w_lo", [P, SLOTS, FULL], FR)
        X = sb("x_residual", [P, TT, D])
        hThi = sb("hT_hi", [P, KC, S], FR)
        hTlo = sb("hT_lo", [P, KC, S], FR)
        cst = sb("shape_constants", [P, C_END])
        pcol = sb("param_columns", [P, 40])
        gain = sb("qk_gain", [P, 2, 2, HD])
        st = sb("norm_stats", [P, 4, TT])
        ident = cst[:, C_ID:C_ID + P]
        mixer = ExitStack()
        zb = sb("z_blocks", [P, 8, TT, 512], F32, mixer)
        zi = sb("z_index", [P, TT, IDXW], F32, mixer)
        wis = sb("w_index", [P, TT, IH], F32, mixer)
        wpool = sb("w_pool", [P, GROUPS, P], F32, mixer)
        band = sb("pool_band", [P, GROUPS, 3 * P], F32, mixer)
        diffT = sb("pool_diffT", [P, GROUPS, S], F32, mixer)
        work = sb("topk_work", [P, P + S], F32, mixer)
        madd = sb("mask_add", [P, P + S], F32, mixer)
        m8 = sb("max8", [P, TT, 8], F32, mixer)
        ao = sb("attn_out", [P, TT, AW], F32, mixer)
        ki4 = ao[:, :, 0:4 * IDIM].rearrange("p t (a d) -> p t a d", d=IDIM)
        hs32 = sb("head_stats", [P, 3, 32], F32, mixer)
        sx = sb("softmax_stats", [P, TT, 4, HEADS], F32, mixer)
        PT = sb("probsT", [P, 2, HEADS, P], F32, mixer)
        att = ExitStack()
        qT = sb("qT", [P, 4, S], F32, att)
        kT = sb("kT", [P, 4, S], F32, att)
        L = sb("logits", [P, HEADS, S], F32, att)
        qiT = sb("qiT", [P, 2, S], F32, att)
        kiT = sb("kiT", [P, S], F32, att)
        att.close()
        proj = ExitStack()
        aThi = sb("aT_hi", [P, 4, S], FR, proj)
        aTlo = sb("aT_lo", [P, 4, S], FR, proj)
        pThi = sb("pT_hi", [P, 4, S], FR, proj)
        pTlo = sb("pT_lo", [P, 4, S], FR, proj)
        proj.close()
        mixer.close()
        setup = ExitStack()
        xs = sb("x_normed", [P, TT, D], F32, setup)
        prow = sb("param_rows", [40, P], F32, setup)
        nrow = sb("gain_row", [1, 4 * HD], F32, setup)
        dense = ExitStack()
        hidDhi = sb("hidden_hi", [P, KC_D, S], FR, dense)
        hidDlo = sb("hidden_lo", [P, KC_D, S], FR, dense)
        hsD = sb("hidden", [P, 2, TT, 256], F32, dense)
        dense.close()
        setup.close()
        moe = ExitStack()
        raw7 = sb("w_raw_7", [P, FULL], F32, moe)
        raw456 = sb("w_raw_456", [P, 3, FULL], F32, moe)
        raw8 = [raw[:, k] for k in range(4)] + [raw456[:, k] for k in range(3)] + [raw7[:]]
        xrhi = sb("x_rows_hi", [P, TT, D], FR, moe)
        xrlo = sb("x_rows_lo", [P, TT, D], FR, moe)
        hehi, helo = hThi[:, :, 0:P], hTlo[:, :, 0:P]
        yhi, ylo = hThi[:, :, P:S], hTlo[:, :, P:S]
        hidMhi = sb("hiddenM_hi", [P, KC_E, P], FR, moe)
        hidMlo = sb("hiddenM_lo", [P, KC_E, P], FR, moe)
        hsM = sb("hiddenM", [P, 2, 256], F32, moe)
        selR = sb("select", [P, TT, P], FR, moe)
        selT = sb("selectT", [P, S], FR, moe)
        identR = sb("identity_r", [P, P], FR, moe)
        wr = sb("w_router", [P, KC, E], F32, moe)
        wrhi = sb("w_router_hi", [P, KC, E], FR, moe)
        wrlo = sb("w_router_lo", [P, KC, E], FR, moe)
        lg = sb("router_logits", [P, TT, E], F32, moe)
        v8 = sb("router_top", [P, TT, 8], F32, moe)
        ix8 = sb("router_index", [P, TT, 8], U32, moe)
        ixf = sb("router_index_f", [P, TT, 8], F32, moe)
        m0 = sb("mask_first", [P, TT, E], F32, moe)
        m1 = sb("mask_second", [P, TT, E], F32, moe)
        pr = sb("gate_probs", [P, 4, TT], F32, moe)
        gate = sb("gate", [P, TT, E], F32, moe)
        pm = sb("slot_of_token", [P, TT, E], F32, moe)
        ov = sb("overflow", [P, 4, E], F32, moe)
        tmp8 = sb("routing_tmp", [P, TT, E], F32, moe)
        posj = sb("slot_by_job", [P, TT, NJ], F32, moe)
        gatej = sb("gate_by_job", [P, TT, NJ + 1], F32, moe)
        tabf = sb("job_table_f", [P, 16], F32, moe)
        tabi = sb("job_table", [P, 16], I32, moe)
        moe.close()

        bank = [ctx.enter_context(nc.psum_tensor(f"bank{i}", [P, 512], F32)) for i in range(8)]

        s_x = sem("x_loaded")
        s_cst = sem("constants_loaded")
        s_par = sem("params_loaded")
        s_wrl = sem("router_loaded")
        s_pool = [sem(f"pool_weights_loaded{i}") for i in range(2)]
        s_ld = [sem(f"chunk_loaded{i}") for i in range(2 * SLOTS)]
        s_hi = sem("chunk_hi")
        s_lo = sem("chunk_lo")
        s_use = sem("chunk_used")
        s_prt = sem("paramsT_done")
        s_pcol = sem("param_columns_ready")
        s_sq = sem("sumsq_done")
        s_ms = sem("meansq_done")
        s_rms = sem("rms_done")
        s_xs = sem("xs_done")
        s_tr = sem("transposed")
        s_thi = sem("hT_hi_done")
        s_tlo = sem("hT_lo_done")
        s_za = sem("z_evac_act")
        s_zd = sem("z_evac_dve")
        s_idx = sem("index_ready")
        s_idxT = sem("indexT_done")
        s_idxs = sem("indexT_in_sbuf")
        s_dot = sem("index_dots_done")
        s_rel = sem("relu_done")
        s_sc = sem("scores_done")
        s_qms = sem("qk_meansq")
        s_qrm = sem("qk_rms")
        s_qk = sem("qk_roped")
        s_qkT = sem("qkT_done")
        s_qks = sem("qkT_in_sbuf")
        s_lg = sem("qk_products")
        s_mx = sem("row_max_ready")
        s_ex = sem("exp_done")
        s_pt = sem("probsT_done")
        s_pta = sem("probsT_evac_act")
        s_ptd = sem("probsT_evac_dve")
        s_pv = sem("pv_done")
        s_ao = sem("attn_out_ready")
        s_aT = sem("aT_done")
        s_ahi = sem("aT_hi_done")
        s_alo = sem("aT_lo_done")
        s_df = sem("pool_diff_done")
        s_dfs = sem("pool_diff_in_sbuf")
        s_pp = sem("pool_mixed_done")
        s_phi = sem("pT_hi_done")
        s_plo = sem("pT_lo_done")
        s_sg = sem("gates_ready")
        s_m = sem("merged_ready")
        s_xd = sem("x_updated")
        s_si = sem("ffn_silu_done")
        s_hm = sem("ffn_hidden_done")
        s_ft = sem("ffn_hiddenT_done")
        s_fhi = sem("ffn_hiddenT_hi")
        s_flo = sem("ffn_hiddenT_lo")
        s_xr = sem("x_rows_hi_done")
        s_xrl = sem("x_rows_lo_done")
        s_wrh = sem("router_hi_done")
        s_rt = sem("router_done")
        s_gd = sem("gate_diff")
        s_ge = sem("gate_exp")
        s_mk = sem("expert_mask_ready")
        s_pos = sem("positions_done")
        s_tab = sem("job_table_ready")
        s_sel = sem("select_ready")
        s_g = sem("gather_done")
        s_ghi = sem("gather_hi")
        s_glo = sem("gather_lo")
        s_st = sem("selectT_done")
        s_sts = sem("selectT_in_sbuf")
        m_si = sem("moe_silu_done")
        m_hm = sem("moe_hidden_done")
        m_ft = sem("moe_hiddenT_done")
        m_fhi = sem("moe_hiddenT_hi")
        m_flo = sem("moe_hiddenT_lo")
        s_y0 = sem("moe_y_cleared")
        m_yhi = sem("moe_y_hi")
        m_ylo = sem("moe_y_lo")
        m_sc = sem("moe_scatter_done")
        m_xa = sem("moe_x_added")
        s_dve = sem("dve_step")
        s_act = sem("act_step")
        s_out = sem("out_stored")

        block = ctx.enter_context(nc.Block())

        @block.sync
        def _(sp):
            def load(c, parts, dyn=0):
                if not (isinstance(dyn, int) and c < SLOTS):
                    sp.wait_ge(s_lo, dyn * SLOTS + (c - SLOTS + 1))
                for dst, src in parts:
                    sp.dma_start(dst, src).then_inc(s_ld[c % SLOTS], 16)

            def k_halves(c, w, rows, col, width):
                t = raw[:, c % SLOTS, 0:4 * width].rearrange("p (k n) -> p k n", n=width)
                v = w[rows:rows + 512, col:col + width].rearrange("(k p) n -> p k n", p=P)
                return [(t[:, 0:2], v[:, 0:2]), (t[:, 2:4], v[:, 2:4])]

            def up_pair(c, w1, w3, half, col):
                t = raw[:, c % SLOTS, :].rearrange("p (k n) -> p k n", n=512)
                rows = slice(half * 512, half * 512 + 512)
                return [(t[:, :, 256 * j:256 * j + 256],
                         w[rows, col].rearrange("(k p) n -> p k n", p=P)) for j, w in enumerate((w1, w3))]

            def down_row(c, w2, row):
                t = raw[:, c % SLOTS, 0:HALF]
                return [(t[:, 512 * j:512 * j + 512], w2[row, 512 * j:512 * j + 512]) for j in range(2)]

            def mixer_loads(l, c):
                w = A["w_in"][l]
                for h in range(2):
                    load(c, k_halves(c, w, 512 * h, 1536, IDXW))
                    c += 1
                for col in ZCOL:
                    for h in range(2):
                        load(c, k_halves(c, w, 512 * h, col, 512))
                        c += 1
                for nh in range(2):
                    for name in ("w_attn_proj", "w_pool_proj"):
                        load(c, k_halves(c, A[name][l], 0, 512 * nh, 512))
                        c += 1
                for nh in range(2):
                    for h in range(2):
                        load(c, k_halves(c, A["w_out"][l], 512 * h, 512 * nh, 512))
                        c += 1

            sp.dma_start(X[:], A["x"][0].rearrange("(t p) d -> p t d", p=P)).then_inc(s_x, 16)
            sp.dma_start(cst[:], A["consts"]).then_inc(s_cst, 16)
            for name, r, n in (("mix_norm", 0, 16), ("ffn_norm", 16, 16), ("pool_scale", 32, 8)):
                sp.dma_start(prow[r:r + n, :], A[name].rearrange("l (k p) -> (l k) p", p=P)).then_inc(s_par, 16)
            for j, name in enumerate(("q_norm", "k_norm")):
                v = nrow[:].rearrange("o (l j d) -> o l j d", l=2, j=2)
                for l in range(2):
                    sp.dma_start(v[:, l, j], A[name][l:l + 1, :]).then_inc(s_par, 16)
            for l in range(2):
                base = l * LAYER1
                mixer_loads(l, base)
                if l == 0:
                    for b in range(NB_D):
                        for h in range(2):
                            c = DENSE0 + 2 * b + h
                            load(c, up_pair(c, A["dense_w1"][0], A["dense_w3"][0], h, slice(256 * b, 256 * b + 256)))
                    for k in range(KC_D):
                        c = DENSE0 + 2 * NB_D + k
                        load(c, down_row(c, A["dense_w2"][0], slice(P * k, P * k + P)))

            w1, w3, w2 = (A[n][0].rearrange("e k n -> (e k) n") for n in ("moe_w1", "moe_w3", "moe_w2"))

            def up_chunk(m, e, g):
                t = raw8[m % 8].rearrange("p (k n) -> p k n", n=512)
                for j, w in enumerate((w1, w3)):
                    src = w[bass.ds(e * D + (m % 2) * 512, 512), bass.ds(g * 512 + (m % 4 // 2) * 256, 256)]
                    sp.dma_start(t[:, :, 256 * j:256 * j + 256],
                                 src.rearrange("(k p) n -> p k n", p=P)).then_inc(s_ld[m % 8], 16)

            def down_chunk(m, e, g):
                for j in range(2):
                    sp.dma_start(raw8[m % 8][:, 512 * j:512 * j + 512],
                                 w2[bass.ds(e * FFE + g * 512 + (m % 4) * P, P), 512 * j:512 * j + 512]
                                 ).then_inc(s_ld[m % 8], 16)

            def group(load_chunk, i, e, first, g, more=0):
                for k in range(4):
                    sp.wait_ge(s_lo, i * JOB_CHUNKS + more + (MOE0 + first + k - 8 + 1))
                    load_chunk(first + k, e, g)

            def job_loads(i, e):
                with sp.Fori(0, 2) as it:
                    for u in range(2):
                        group(up_chunk, i, e, 8 + 4 * u, it * 2 + (2 + u), it * 8)
                group(up_chunk, i, e, 24, 6)
                group(down_chunk, i, e, 28, 0)
                with sp.Fori(0, 3) as it:
                    for u in range(2):
                        group(down_chunk, i, e, 32 + 4 * u, it * 2 + (1 + u), it * 8)

            def next_job(i, e):
                for g in range(2):
                    group(up_chunk, i, e, JOB_CHUNKS + 4 * g, g)

            for m in range(8):
                if m < 4:
                    sp.wait_ge(s_lo, MOE0 + m - SLOTS + 1)
                elif m == 4:
                    sp.wait_ge(s_xd, 3)
                elif m == 7:
                    sp.wait_ge(s_xrl, 2)
                up_chunk(m, 0, m // 4)
            with sp.Fori(0, E - 1) as i:
                job_loads(i, i)
                next_job(i, i + 1)
            sp.wait_ge(s_tab, 1)
            njobs = sp.value_load(tabi[0:1, 15:16], min_val=E, max_val=NJ - 1)
            with sp.Fori(E - 1, njobs) as i:
                e = sp.value_load(tabi[0:1, bass.ds(i, 1)], min_val=0, max_val=E - 1)
                job_loads(i, e)
                with sp.If(i < njobs - 1):
                    en = sp.value_load(tabi[0:1, bass.ds(i + 1, 1)], min_val=0, max_val=E - 1)
                    next_job(i, en)
            for k in range(SLOTS):
                sp.wait_ge(s_lo, njobs * JOB_CHUNKS + (MOE0 + k - 8 + 1))
                for j in range(2):
                    sp.dma_start(raw8[k][:, 128 * j:128 * j + 128], A["moe_w2"][0, 0, 0:P, 0:P]).then_inc(s_ld[k], 16)
            sp.wait_ge(m_xa, njobs * 4 + 4)
            sp.dma_start(out[0].rearrange("(t p) d -> p t d", p=P), X[:]).then_inc(s_out, 16)
            sp.wait_ge(s_out, 16)

        @block.gpsimd
        def _(pool):
            for l in range(2):
                if l:
                    pool.wait_ge(s_xd, 2)
                pool.dma_start(band[:], A["pool_band"]).then_inc(s_pool[0], 16)
                pool.dma_start(wpool[:], A["w_pool"][l].rearrange("g c d -> c g d")).then_inc(s_pool[1], 16)
            pool.wait_ge(s_xd, 3)
            pool.dma_start(wr[:], A["moe_router"][0].rearrange("(k p) e -> p k e", p=P)).then_inc(s_wrl, 16)

        @block.scalar
        def _(act):
            steps = [0]

            def chain(ins):
                steps[0] += 1
                ins.then_inc(s_act, 1)
                act.wait_ge(s_act, steps[0])

            def split(c, n, dyn=0):
                act.wait_ge(s_ld[c % SLOTS], dyn * 32 + 32 * (c // SLOTS + 1))
                if not (isinstance(dyn, int) and c < SLOTS):
                    act.wait_ge(s_use, dyn * SLOTS + (c - SLOTS + 1))
                act.activation(whi[:, c % SLOTS, 0:n], raw[:, c % SLOTS, 0:n], ACT.Copy).then_inc(s_hi, 1)

            def split_m(m, n, dyn):
                act.wait_ge(s_ld[m % 8], dyn * 32 + 32 * (m // 8 + 1 + (MOE0 // SLOTS if m % 8 < 4 else 0)))
                act.wait_ge(s_use, dyn * 8 + (MOE0 + m - SLOTS + 1))
                act.activation(whi[:, m % SLOTS, 0:n], raw8[m % 8][:, 0:n], ACT.Copy).then_inc(s_hi, 1)

            def ahead(c):
                split(c + LOOK, chunk_words(c + LOOK) if c + LOOK < MOE0 else FULL)

            def hT_hi(te, scale0):
                for j in range(4):
                    act.wait_ge(s_tr, 4 * te + j + 1)
                    if scale0 is None:
                        act.activation(hThi[:, 2 * j:2 * j + 2, :], bank[j][:].rearrange("p (k t) -> p k t", t=S),
                                       ACT.Copy).then_inc(s_thi, 1)
                        continue
                    for q in range(2):
                        k = 2 * j + q
                        ins = act.activation(hThi[:, k, :], bank[j][:, q * S:q * S + S], ACT.Copy,
                                             scale=pcol[:, scale0 + k:scale0 + k + 1])
                    ins.then_inc(s_thi, 1)

            def norm(k):
                if k:
                    act.wait_ge(s_xd, k)
                else:
                    act.wait_ge(s_x, 16)
                for t in range(TT):
                    act.activation(xs[:, t, :], X[:, t, :], ACT.Square, accum_out=st[:, 0, t:t + 1]).then_inc(s_sq, 1)
                act.wait_ge(s_ms, k + 1)
                act.activation(st[:, 2, :], st[:, 1, :], ACT.Sqrt).then_inc(s_rms, 1)

            def layer(l, c0):
                norm(2 * l)
                if l == 0:
                    act.wait_ge(s_pcol, 1)
                hT_hi(3 * l, 8 * l)
                c = c0
                for n in range(9):
                    ahead(c)
                    ahead(c + 1)
                    c += 2
                    act.wait_ge(s_use, c)
                    if n == 0:
                        act.activation(zi[:, 0, :], bank[4][:, 0:IDXW], ACT.Copy).then_inc(s_za, 1)
                    else:
                        act.activation(zb[:, n - 1, 0, :], bank[4 + 2 * (n % 2)][:], ACT.Copy).then_inc(s_za, 1)
                act.wait_ge(s_zd, 9 * (l + 1))
                act.wait_ge(s_za, 9 * (l + 1))
                act.activation(zb[:, ZGA:ZGA + 4].rearrange("p b t n -> p (b t n)"),
                               zb[:, ZGA:ZGA + 4].rearrange("p b t n -> p (b t n)"), ACT.Sigmoid).then_inc(s_sg, 1)
                act.wait_ge(s_idxT, l + 1)
                act.activation(qiT[:].rearrange("p c t -> p (c t)"), bank[0][:], ACT.Copy).then_inc(s_idxs, 1)
                act.activation(kiT[:], bank[1][:, 0:S], ACT.Copy).then_inc(s_idxs, 1)
                for t in range(TT):
                    nk = P * (t + 1)
                    act.wait_ge(s_dot, 2 * l + t + 1)
                    if t:
                        act.wait_ge(s_sc, 2 * l + t)
                    for j in range(4):
                        ins = act.activation(L[:, 2 * j:2 * j + 2, 0:nk],
                                             bank[4 * t + j][:].rearrange("p (c s) -> p c s", s=S)[:, :, 0:nk],
                                             ACT.Relu, scale=IDIM ** -0.5)
                    ins.then_inc(s_rel, 1)
                    if t == 0:
                        act.wait_ge(s_qms, l + 1)
                        act.activation(hs32[:, 1, :], hs32[:, 0, :], ACT.Sqrt).then_inc(s_qrm, 1)
                for j in range(4):
                    act.wait_ge(s_qkT, 4 * l + j + 1)
                    dst = (qT if j < 2 else kT)[:, 2 * (j % 2):2 * (j % 2) + 2, :]
                    act.activation(dst, bank[j][:].rearrange("p (k t) -> p k t", t=S), ACT.Copy).then_inc(s_qks, 1)
                Pr = zb[:, 0:2].rearrange("p b t (h s) -> p (b t h) s", s=S)
                for t in range(TT):
                    nk = P * (t + 1)
                    act.wait_ge(s_mx, 2 * l + t + 1)
                    if t:
                        act.wait_ge(s_pt, 6 * l + 2)
                    for h in range(HEADS):
                        ins = act.activation(Pr[:, h, 0:nk], L[:, h, 0:nk], ACT.Exp, bias=sx[:, t, 1, h:h + 1],
                                             accum_out=sx[:, t, 2, h:h + 1])
                    ins.then_inc(s_ex, 1)
                    for j in range(t + 1):
                        act.wait_ge(s_pt, 6 * l + 2 * t + 2 * j + 1)
                        act.activation(PT[:, j, 0:4, :], bank[4 * t + 2 * j][:].rearrange("p (h s) -> p h s", s=P),
                                       ACT.Copy).then_inc(s_pta, 1)
                for j in range(2):
                    act.wait_ge(s_df, 2 * l + j + 1)
                    act.activation(diffT[:, 2 * j:2 * j + 2, :], bank[4 + j][:].rearrange("p (k t) -> p k t", t=S),
                                   ACT.Copy).then_inc(s_dfs, 1)
                for j in range(2):
                    act.wait_ge(s_pp, 2 * l + j + 1)
                    for q in range(2):
                        g = 2 * j + q
                        ins = act.activation(pThi[:, g, :], bank[6 + j][:, q * S:q * S + S], ACT.Copy,
                                             scale=pcol[:, 32 + 4 * l + g:33 + 4 * l + g])
                    ins.then_inc(s_phi, 1)
                for j in range(2):
                    act.wait_ge(s_aT, 2 * l + j + 1)
                    act.activation(aThi[:, 2 * j:2 * j + 2, :], bank[j][:].rearrange("p (k t) -> p k t", t=S),
                                   ACT.Copy).then_inc(s_ahi, 1)
                for _ in range(4):
                    ahead(c)
                    c += 1
                hT_hi(3 * l + 1, None)
                for _ in range(4):
                    ahead(c)
                    c += 1
                norm(2 * l + 1)
                hT_hi(3 * l + 2, 16 + 8 * l)

            for c in range(LOOK):
                split(c, chunk_words(c))
            layer(0, 0)

            def silu_d(b, q):
                act.wait_ge(s_use, b * 2 + (DENSE0 + 2))
                for t in range(TT):
                    ins = act.activation(hsD[:, q, t, :], bank[4 + 2 * q + t][:, 0:256], ACT.Silu)
                ins.then_inc(s_si, 1)

            def hid_hi_d(b, q):
                act.wait_ge(s_ft, b + 1)
                act.activation(hidDhi[:, bass.ds(b * 2, 2), :] if not isinstance(b, int) else hidDhi[:, 2 * b:2 * b + 2, :],
                               bank[q][:].rearrange("p (k t) -> p k t", t=S), ACT.Copy).then_inc(s_fhi, 1)

            ahead(DENSE0)
            silu_d(0, 0)
            ahead(DENSE0 + 1)
            with act.Fori(0, 4) as it:
                for u in range(2):
                    c = DENSE0 + 2 + 2 * u
                    split(c + LOOK, FULL, it)
                    hid_hi_d(it * 2 + u, u)
                    silu_d(it * 2 + (1 + u), 1 - u)
                    split(c + 1 + LOOK, FULL, it)
            for b in range(9, NB_D):
                ahead(DENSE0 + 2 * b)
                hid_hi_d(b - 1, (b - 1) % 2)
                silu_d(b, b % 2)
                ahead(DENSE0 + 2 * b + 1)
            hid_hi_d(NB_D - 1, (NB_D - 1) % 2)
            c = DENSE0 + 2 * NB_D
            with act.Fori(0, 4) as it:
                for k in range(SLOTS):
                    split(c + k + LOOK, HALF, it)
            for k in range(16, KC_D):
                ahead(c + k)

            layer(1, LAYER1)

            act.wait_ge(s_xs, 2 * 4)
            for t in range(TT):
                act.activation(xrhi[:, t, :], xs[:, t, :], ACT.Copy).then_inc(s_xr, 1)
            act.activation(identR[:], ident, ACT.Copy)
            act.wait_ge(s_wrl, 16)
            act.activation(wrhi[:], wr[:], ACT.Copy).then_inc(s_wrh, 1)
            act.wait_ge(s_gd, 1)
            act.activation(pr[:, 1, :], pr[:, 0, :], ACT.Exp).then_inc(s_ge, 1)

            def gathered_hi(i):
                for j in range(2):
                    act.wait_ge(s_g, i * 2 + (j + 1))
                    for q in range(4):
                        k = 4 * j + q
                        ins = act.activation(hehi[:, k, :], bank[2 + j][:, q * P:q * P + P], ACT.Copy,
                                             scale=pcol[:, 24 + k:25 + k])
                    ins.then_inc(s_ghi, 1)

            gathered_hi(0)
            act.wait_ge(s_tab, 1)
            njobs = act.value_load(tabi[0:1, 15:16], min_val=E, max_val=NJ - 1)
            with act.Fori(0, njobs) as i:
                j8 = i * (JOB_CHUNKS // 8)

                def silu_m(b, q):
                    act.wait_ge(s_use, i * JOB_CHUNKS + b * 2 + (MOE0 + 2))
                    act.activation(hsM[:, q, :], bank[4 + q][:, 0:256], ACT.Silu).then_inc(m_si, 1)

                def hid_hi_m(b, q):
                    act.wait_ge(m_ft, i * NB_E + b + 1)
                    dst = hidMhi[:, 2 * b:2 * b + 2, :] if isinstance(b, int) else hidMhi[:, bass.ds(b * 2, 2), :]
                    act.activation(dst, bank[q][:, 0:256].rearrange("p (k t) -> p k t", t=P),
                                   ACT.Copy).then_inc(m_fhi, 1)

                def pair(p, n, more=0, dyn=0, first=False):
                    for u in range(2):
                        m = 4 * p + 2 * u + LOOK
                        b = more * 2 + (2 * p + u)
                        split_m(m, n, j8 + dyn)
                        if not (first and u == 0):
                            hid_hi_m(b - 1, 1 - u)
                        if first and u == 1:
                            act.wait_ge(s_st, i + 1)
                            act.activation(selT[:], bank[1][:, 0:S], ACT.Copy).then_inc(s_sts, 1)
                        silu_m(b, u)
                        split_m(m + 1, n, j8 + dyn)

                pair(0, FULL, first=True)
                with act.Fori(0, 2) as it:
                    pair(1, FULL, it * 2, it)
                    pair(2, FULL, it * 2, it)
                pair(5, FULL)
                pair(6, HALF)
                d0 = 2 * NB_E + LOOK
                for k in range(4):
                    split_m(d0 + k, HALF, j8)
                gathered_hi(i + 1)
                hid_hi_m(NB_E - 1, (NB_E - 1) % 2)
                with act.Fori(0, 2) as it:
                    for k in range(4, 12):
                        split_m(d0 + k, HALF, j8 + it)
                for k in range(20, 24):
                    split_m(d0 + k, HALF, j8)
                for k in range(24, 27):
                    split_m(d0 + k, FULL, j8)
                act.wait_ge(s_use, i * JOB_CHUNKS + (MOE0 + JOB_CHUNKS))
                for j in range(2):
                    act.activation(yhi[:, 4 * j:4 * j + 4, :], bank[6 + j][:].rearrange("p (k n) -> p k n", n=P),
                                   ACT.Copy).then_inc(m_yhi, 1)
                split_m(d0 + 27, FULL, j8)

        @block.tensor
        def _(pe):
            def three(dst, ahi, alo, bhi, blo, start, stop):
                pe.matmul(dst, ahi, bhi, start=start, stop=False)
                pe.matmul(dst, ahi, blo, start=False, stop=False)
                return pe.matmul(dst, alo, bhi, start=False, stop=stop)

            def weights(c, n, width):
                s = c % SLOTS
                return [t[:, s, 0:n * width].rearrange("p (k n) -> p k n", n=width) for t in (whi, wlo)]

            def chunk(c, dst, ahi, alo, k0, width, start, stop, dyn=0, tiles=TT, n=4):
                pe.wait_ge(s_lo, dyn * SLOTS + c + 1)
                bhi, blo = weights(c, n, width)
                for t in range(tiles):
                    for k in range(n):
                        a = [x[:, k0 + k, t * P:(t + 1) * P] for x in (ahi, alo)]
                        ins = three(dst[t], *a, bhi[:, k, :], blo[:, k, :], start and k == 0, stop and k == n - 1)
                ins.then_inc(s_use, 1)
                return ins

            def transposes_hT(te, src):
                for j in range(4):
                    for q in range(2):
                        for t in range(TT):
                            ins = pe.transpose(bank[j][:, q * S + t * P:q * S + t * P + P], src(2 * j + q, t), ident)
                    ins.then_inc(s_tr, 1)

            def norm_T(k, te):
                pe.wait_ge(s_xs, TT * (k + 1))
                transposes_hT(te, lambda kc, t: xs[:, t, kc * P:kc * P + P])

            def layer(l, c0):
                norm_T(2 * l, 3 * l)
                pe.wait_ge(s_tlo, 4 * (3 * l + 1))
                c = c0
                for n in range(9):
                    if n >= 2:
                        pe.wait_ge(s_za, 9 * l + n - 1)
                        pe.wait_ge(s_zd, 9 * l + n - 1)
                    w = IDXW if n == 0 else 512
                    b = [bank[4 + 2 * (n % 2) + t][:, 0:w] for t in range(TT)]
                    chunk(c, b, hThi, hTlo, 0, w, True, False)
                    chunk(c + 1, b, hThi, hTlo, 4, w, False, True)
                    c += 2
                pe.wait_ge(s_idx, l + 1)
                for hc in range(2):
                    for t in range(TT):
                        pe.transpose(bank[0][:, hc * S + t * P:hc * S + t * P + P], zi[:, t, hc * P:hc * P + P], ident)
                for t in range(TT):
                    ins = pe.transpose(bank[1][:, t * P:t * P + P], ao[:, t, 0:4 * IDIM], ident)
                ins.then_inc(s_idxT, 1)
                pe.wait_ge(s_idxs, 2 * (l + 1))
                for t in range(TT):
                    nk = P * (t + 1)
                    if t:
                        pe.wait_ge(s_za, 9 * (l + 1))
                        pe.wait_ge(s_zd, 9 * (l + 1))
                    for hc in range(2):
                        for r in range(4):
                            rows = slice(32 * r, 32 * r + 32)
                            ins = pe.matmul(bank[4 * t + r][:, hc * S:hc * S + nk], qiT[rows, hc, t * P:t * P + P],
                                            kiT[rows, 0:nk], start=True, stop=True)
                    ins.then_inc(s_dot, 1)
                pe.wait_ge(s_qk, l + 1)
                pe.wait_ge(s_rel, 2 * l + 1)
                for j in range(4):
                    z = zb[:, ZQ if j < 2 else ZK]
                    for q in range(2):
                        hp = 2 * (j % 2) + q
                        for t in range(TT):
                            ins = pe.transpose(bank[j][:, q * S + t * P:q * S + t * P + P],
                                               z[:, t, hp * P:hp * P + P], ident)
                    ins.then_inc(s_qkT, 1)
                pe.wait_ge(s_qks, 4 * (l + 1))
                for t in range(TT):
                    nk = P * (t + 1)
                    if t:
                        pe.wait_ge(s_rel, 2 * l + 2)
                    for hp in range(4):
                        for p in range(2):
                            rows = slice(64 * p, 64 * p + 64)
                            ins = pe.matmul(bank[4 * t + 2 * p + hp // 2][:, (hp % 2) * S:(hp % 2) * S + nk],
                                            qT[rows, hp, t * P:t * P + P], kT[rows, hp, 0:nk], start=True, stop=True)
                    ins.then_inc(s_lg, 1)
                Pr = zb[:, 0:2].rearrange("p b t (h s) -> p (b t h) s", s=S)
                for t in range(TT):
                    pe.wait_ge(s_ex, 2 * l + t + 1)
                    for j in range(t + 1):
                        for q in range(2):
                            for h in range(4):
                                ins = pe.transpose(bank[4 * t + 2 * j + q][:, h * P:h * P + P],
                                                   Pr[:, 4 * q + h, j * P:j * P + P], ident)
                            ins.then_inc(s_pt, 1)
                    pe.wait_ge(s_pta, 3 * l + 2 * t + 1)
                    pe.wait_ge(s_ptd, 3 * l + 2 * t + 1)
                    for h in range(HEADS):
                        i = (h % 2) * 4 + h // 2
                        for j in range(t + 1):
                            ins = pe.matmul(bank[2 + t][:, h * HD:h * HD + HD], PT[:, j, i, :],
                                            zb[:, ZV, j, h * HD:h * HD + HD], start=(j == 0), stop=(j == t))
                    ins.then_inc(s_pv, 1)
                for s in s_pool:
                    pe.wait_ge(s, 16 * (l + 1))
                for j in range(2):
                    for q in range(2):
                        g = 2 * j + q
                        for t in range(TT):
                            rhs = band[:, g, 0:S] if t == 0 else band[:, g, S:S + P]
                            ins = pe.matmul(bank[4 + j][:, q * S + t * P:q * S + S], zb[:, ZU, t, g * P:g * P + P], rhs,
                                            start=(t == 0), stop=(t == 1), skip_group_check=True)
                    ins.then_inc(s_df, 1)
                for j in range(2):
                    pe.wait_ge(s_dfs, 2 * l + j + 1)
                    for q in range(2):
                        g = 2 * j + q
                        ins = pe.matmul(bank[6 + j][:, q * S:q * S + S], wpool[:, g, :], diffT[:, g, :],
                                        start=True, stop=True)
                    ins.then_inc(s_pp, 1)
                pe.wait_ge(s_ao, 2 * (l + 1))
                for j in range(2):
                    for q in range(2):
                        for t in range(TT):
                            k = 2 * j + q
                            ins = pe.transpose(bank[j][:, q * S + t * P:q * S + t * P + P], ao[:, t, k * P:k * P + P],
                                               ident)
                    ins.then_inc(s_aT, 1)
                pe.wait_ge(s_alo, 2 * (l + 1))
                pe.wait_ge(s_plo, 2 * (l + 1))
                for nh in range(2):
                    for j, (hi, lo) in enumerate(((aThi, aTlo), (pThi, pTlo))):
                        chunk(c, [bank[4 * nh + 2 * j + t][:] for t in range(TT)], hi, lo, 0, 512, True, True)
                        c += 1
                pe.wait_ge(s_m, 2 * (l + 1))
                transposes_hT(3 * l + 1, lambda kc, t: zb[:, ZGA + kc // 4, t, (kc % 4) * P:(kc % 4) * P + P])
                pe.wait_ge(s_tlo, 4 * (3 * l + 2))
                for nh in range(2):
                    b = [bank[4 + 2 * nh + t][:] for t in range(TT)]
                    chunk(c, b, hThi, hTlo, 0, 512, True, False)
                    chunk(c + 1, b, hThi, hTlo, 4, 512, False, True)
                    c += 2
                norm_T(2 * l + 1, 3 * l + 2)
                pe.wait_ge(s_tlo, 4 * (3 * l + 3))

            pe.wait_ge(s_cst, 16)
            pe.wait_ge(s_par, 7 * 16)
            pe.transpose(bank[6][:, 0:40], prow[:], cst[0:40, C_ID:C_ID + 40])
            pe.matmul(bank[7][:, 0:4 * HD], cst[0:1, C_ONE:C_ONE + P], nrow[:], start=True, stop=True).then_inc(s_prt, 1)
            layer(0, 0)

            def hiddenT_d(b, q):
                pe.wait_ge(s_hm, b + 1)
                for f in range(2):
                    for t in range(TT):
                        ins = pe.transpose(bank[q][:, f * S + t * P:f * S + t * P + P],
                                           hsD[:, q, t, f * P:f * P + P], ident)
                ins.then_inc(s_ft, 1)

            def block_d(b, q, c, dyn, prev=True, prev2=True):
                dst = [bank[4 + 2 * q + t][:] for t in range(TT)]
                chunk(c, dst, hThi, hTlo, 0, 512, True, False, dyn)
                if prev:
                    if prev2:
                        pe.wait_ge(s_flo, b - 2 + LEAD)
                    hiddenT_d(b - 1, 1 - q)
                chunk(c + 1, dst, hThi, hTlo, 4, 512, False, True, dyn)

            block_d(0, 0, DENSE0, 0, prev=False)
            with pe.Fori(0, 5) as it:
                for u in range(2):
                    block_d(it * 2 + (1 + u), 1 - u, DENSE0 + 2 + 2 * u, it)
            hiddenT_d(NB_D - 1, (NB_D - 1) % 2)
            for k in range(KC_D):
                c = DENSE0 + 2 * NB_D + k
                pe.wait_ge(s_flo, k // 2 + 1 + LEAD)
                pe.wait_ge(s_lo, c + 1)
                if k == 0:
                    pe.wait_ge(s_hm, NB_D)
                for t in range(TT):
                    a = [x[:, k, t * P:t * P + P] for x in (hidDhi, hidDlo)]
                    for nh in range(2):
                        w = [x[:, c % SLOTS, 512 * nh:512 * nh + 512] for x in (whi, wlo)]
                        ins = three(bank[4 + 2 * t + nh][:], *a, *w, k == 0, k == KC_D - 1)
                ins.then_inc(s_use, 1)

            layer(1, LAYER1)

            pe.wait_ge(s_wrh, 2)
            for t in range(TT):
                for k in range(KC):
                    ins = three(bank[4][:, t * E:t * E + E], hThi[:, k, t * P:t * P + P], hTlo[:, k, t * P:t * P + P],
                                wrhi[:, k, :], wrlo[:, k, :], k == 0, k == KC - 1)
            ins.then_inc(s_rt, 1)
            pe.wait_ge(s_mk, 1)
            tri, ones = cst[:, C_TRI:C_TRI + P], cst[:, C_ONE:C_ONE + P]
            pe.matmul(bank[5][:, 0:E], tri, tmp8[:, 0, :], start=True, stop=True)
            pe.matmul(bank[5][:, E:2 * E], tri, tmp8[:, 1, :], start=True, stop=False)
            pe.matmul(bank[5][:, E:2 * E], ones, tmp8[:, 0, :], start=False, stop=True)
            pe.matmul(bank[5][:, 2 * E:3 * E], ones, tmp8[:, 0, :], start=True, stop=False)
            pe.matmul(bank[5][:, 2 * E:3 * E], ones, tmp8[:, 1, :], start=False, stop=True).then_inc(s_pos, 1)

            def gather(i):
                pe.wait_ge(s_sel, i + 1)
                for j in range(2):
                    for q in range(4):
                        k = 4 * j + q
                        for t in range(TT):
                            for x in (xrhi, xrlo):
                                ins = pe.matmul(bank[2 + j][:, q * P:q * P + P], x[:, t, k * P:k * P + P],
                                                selR[:, t, :], start=(t == 0 and x is xrhi),
                                                stop=(t == TT - 1 and x is xrlo))
                    ins.then_inc(s_g, 1)

            def scatter(i):
                pe.wait_ge(m_ylo, i * 2 + LEAD)
                for t in range(TT):
                    for nh in range(2):
                        for y in (yhi, ylo):
                            ins = pe.matmul(bank[4 * t + 2 + nh][:], selT[:, t * P:t * P + P],
                                            y[:, 4 * nh:4 * nh + 4, :], start=(y is yhi), stop=(y is ylo))
                        ins.then_inc(m_sc, 1)

            pe.wait_ge(s_xrl, 2)
            pe.wait_ge(s_y0, 1)
            gather(0)
            pe.wait_ge(s_tab, 1)
            njobs = pe.value_load(tabi[0:1, 15:16], min_val=E, max_val=NJ - 1)
            with pe.Fori(0, njobs) as i:
                jd = JOB_CHUNKS // SLOTS

                def hiddenT_m(b, q):
                    pe.wait_ge(m_hm, i * NB_E + b + 1)
                    for f in range(2):
                        ins = pe.transpose(bank[q][:, f * P:f * P + P], hsM[:, q, f * P:f * P + P], ident)
                    ins.then_inc(m_ft, 1)

                def pair(it, first=False):
                    for u in range(2):
                        c = MOE0 + 2 * u
                        b = it * 2 + u
                        if not first:
                            pe.wait_ge(m_hm, i * NB_E + b - 1)
                        chunk(c, [bank[4 + u][:]], hehi, helo, 0, 512, True, False, i * jd + it, tiles=1)
                        if not (first and u == 0):
                            if not first:
                                pe.wait_ge(m_flo, i * NB_E + b - 2 + LEAD)
                            hiddenT_m(b - 1, 1 - u)
                        if first and u == 1:
                            for t in range(TT):
                                ins = pe.matmul(bank[1][:, t * P:t * P + P], selR[:, t, :], identR[:],
                                                start=True, stop=True)
                            ins.then_inc(s_st, 1)
                        chunk(c + 1, [bank[4 + u][:]], hehi, helo, 4, 512, False, True, i * jd + it, tiles=1)
                        if first and u == 0:
                            scatter(i)

                pe.wait_ge(s_glo, i * 2 + 2)
                pair(0, first=True)
                with pe.Fori(1, NB_E // 2) as it:
                    pair(it)
                pe.wait_ge(m_xa, i * 4 + 4)
                gather(i + 1)
                for k in range(KC_E):
                    c = MOE0 + 2 * NB_E + k
                    if k == 4:
                        hiddenT_m(NB_E - 1, (NB_E - 1) % 2)
                    if k == 0:
                        pe.wait_ge(m_flo, i * NB_E + NB_E - 1 + LEAD)
                        pe.wait_ge(m_xa, i * 4 + 4)
                    if k == KC_E - 2:
                        pe.wait_ge(m_flo, i * NB_E + NB_E + LEAD)
                    pe.wait_ge(s_lo, i * JOB_CHUNKS + c + 1)
                    for nh in range(2):
                        w = [x[:, c % SLOTS, 512 * nh:512 * nh + 512] for x in (whi, wlo)]
                        ins = three(bank[6 + nh][:], hidMhi[:, k, :], hidMlo[:, k, :], *w, k == 0, k == KC_E - 1)
                    ins.then_inc(s_use, 1)
            scatter(njobs)

        @block.vector
        def _(dve):
            steps = [0]

            def chain(ins):
                steps[0] += 1
                ins.then_inc(s_dve, 1)
                dve.wait_ge(s_dve, steps[0])

            def split(c, n, dyn=0):
                dve.wait_ge(s_hi, dyn * SLOTS + c + 1)
                s = c % SLOTS
                dve.tensor_tensor(wlo[:, s, 0:n], raw[:, s, 0:n], whi[:, s, 0:n], ALU.subtract).then_inc(s_lo, 1)

            def split_m(m, n, dyn):
                dve.wait_ge(s_hi, dyn * 8 + (MOE0 + m + 1))
                dve.tensor_tensor(wlo[:, m % SLOTS, 0:n], raw8[m % 8][:, 0:n], whi[:, m % SLOTS, 0:n],
                                  ALU.subtract).then_inc(s_lo, 1)

            def ahead(c):
                split(c + LOOK, chunk_words(c + LOOK) if c + LOOK < MOE0 else FULL)

            def hT_lo(te, scale0):
                for j in range(4):
                    dve.wait_ge(s_thi, 4 * te + j + 1)
                    if scale0 is None:
                        dve.tensor_tensor(hTlo[:, 2 * j:2 * j + 2, :], bank[j][:].rearrange("p (k t) -> p k t", t=S),
                                          hThi[:, 2 * j:2 * j + 2, :], ALU.subtract).then_inc(s_tlo, 1)
                        continue
                    for q in range(2):
                        k = 2 * j + q
                        ins = dve.scalar_tensor_tensor(hTlo[:, k, :], bank[j][:, q * S:q * S + S],
                                                       pcol[:, scale0 + k:scale0 + k + 1], hThi[:, k, :],
                                                       ALU.mult, ALU.subtract)
                    ins.then_inc(s_tlo, 1)

            def rsqrt(r, rms, ms, t):
                chain(dve.reciprocal(r, rms))
                chain(dve.tensor_tensor(t, r, r, ALU.mult))
                chain(dve.tensor_tensor(t, t, ms, ALU.mult))
                chain(dve.tensor_scalar(t, t, -0.5, 1.5, ALU.mult, ALU.add))
                chain(dve.tensor_tensor(r, r, t, ALU.mult))

            def norm(k):
                dve.wait_ge(s_sq, TT * (k + 1))
                dve.tensor_scalar(st[:, 1, :], st[:, 0, :], 1.0 / D, EPS, ALU.mult, ALU.add).then_inc(s_ms, 1)
                dve.wait_ge(s_rms, k + 1)
                dve.wait_ge(s_ms, k + 1)
                rsqrt(st[:, 3, :], st[:, 2, :], st[:, 1, :], st[:, 0, :])
                for t in range(TT):
                    dve.tensor_scalar(xs[:, t, :], X[:, t, :], st[:, 3, t:t + 1], None, ALU.mult).then_inc(s_xs, 1)

            def rope(v, half, cos, sin, tmp):
                x1, x2 = v[:, :, :, 0:half], v[:, :, :, half:2 * half]
                dve.tensor_tensor(tmp[0], x1, cos, ALU.mult)
                dve.tensor_tensor(tmp[1], x2, sin, ALU.mult)
                dve.tensor_tensor(tmp[2], x2, cos, ALU.mult)
                chain(dve.tensor_tensor(tmp[3], x1, sin, ALU.mult))
                dve.tensor_tensor(x1, tmp[0], tmp[1], ALU.subtract)
                return dve.tensor_tensor(x2, tmp[2], tmp[3], ALU.add)

            def table(off, half, heads):
                v = cst[:, off:off + TT * half].rearrange("p (t o d) -> p t o d", t=TT, o=1)
                return v.broadcast_to([P, TT, heads, half])

            def layer(l, c0):
                norm(2 * l)
                if l == 0:
                    dve.wait_ge(s_pcol, 2)
                hT_lo(3 * l, 8 * l)
                c = c0
                for n in range(9):
                    ahead(c)
                    ahead(c + 1)
                    c += 2
                    dve.wait_ge(s_use, c)
                    if n == 0:
                        dve.tensor_copy(zi[:, 1, :], bank[5][:, 0:IDXW]).then_inc(s_zd, 1)
                    else:
                        dve.tensor_copy(zb[:, n - 1, 1, :], bank[5 + 2 * (n % 2)][:]).then_inc(s_zd, 1)
                dve.wait_ge(s_za, 9 * (l + 1))
                dve.wait_ge(s_zd, 9 * (l + 1))
                flat = PT[:].rearrange("p a h s -> p (a h s)")

                def tmps(heads, half):
                    n = TT * heads * half
                    return [flat[:, i * n:i * n + n].rearrange("p (t h d) -> p t h d", t=TT, h=heads) for i in range(4)]

                zh = zi[:, :, 0:9 * IDIM].rearrange("p t (h d) -> p t h d", d=IDIM)
                chain(rope(zh, IROT // 2, table(C_COSI, IROT // 2, 9), table(C_SINI, IROT // 2, 9), tmps(9, IROT // 2)))
                dve.tensor_copy(ki4, zh[:, :, 8:9, :].broadcast_to([P, TT, 4, IDIM]))
                dve.tensor_scalar(wis[:], zi[:, :, 9 * IDIM:IDXW], IH ** -0.5, None, ALU.mult).then_inc(s_idx, 1)
                zq = zb[:, 0:2].rearrange("p b t n -> p (b t n)")
                zqh = zb[:, 0:2].rearrange("p b t (h d) -> p (b t h) d", d=HD)
                chain(dve.tensor_tensor(flat, zq, zq, ALU.mult))
                chain(dve.tensor_reduce(hs32[:, 2, :], flat.rearrange("p (g d) -> p g d", d=HD), AX.X, ALU.add))
                chain(dve.tensor_scalar(hs32[:, 0, :], hs32[:, 2, :], 1.0 / HD, EPS, ALU.mult, ALU.add))
                dve.nop().then_inc(s_qms, 1)

                def scores(t):
                    nk = P * (t + 1)
                    w = work[:, t * P:t * P + nk]
                    dve.wait_ge(s_rel, 2 * l + t + 1)
                    for i in range(HEADS):
                        h = (i % 2) * 4 + i // 2
                        if i == 0:
                            chain(dve.tensor_scalar(w, L[:, i, 0:nk], wis[:, t, h:h + 1], None, ALU.mult))
                        else:
                            chain(dve.scalar_tensor_tensor(w, L[:, i, 0:nk], wis[:, t, h:h + 1], w, ALU.mult, ALU.add))
                    d = work[:, 2 * t * P:2 * t * P + P]
                    chain(dve.tensor_tensor(d, d, cst[:, C_NEG:C_NEG + P], ALU.add))
                    dve.nop().then_inc(s_sc, 1)

                scores(0)
                dve.wait_ge(s_qrm, l + 1)
                rsqrt(hs32[:, 2, :], hs32[:, 1, :], hs32[:, 0, :], flat[:, 0:32])
                chain(dve.tensor_tensor(zqh, zqh, hs32[:, 2, :].rearrange("p (g o) -> p g o", o=1).broadcast_to([P, 32, HD]),
                                        ALU.mult))
                for b in range(2):
                    g = gain[:, l, b:b + 1, :].broadcast_to([P, TT * HEADS, HD])
                    v = zb[:, b].rearrange("p t (h d) -> p (t h) d", d=HD)
                    chain(dve.tensor_tensor(v, v, g, ALU.mult))
                for b in range(2):
                    v = zb[:, b].rearrange("p t (h d) -> p t h d", d=HD)
                    ins = rope(v, ROT // 2, table(C_COS, ROT // 2, HEADS), table(C_SIN, ROT // 2, HEADS),
                               tmps(HEADS, ROT // 2))
                    if b == 0:
                        chain(ins)
                ins.then_inc(s_qk, 1)
                scores(1)
                w = [work[:, 0:P], work[:, P:P + S]]
                for r in range(TOPK // 8):
                    for t in range(TT):
                        chain(dve.max(m8[:, t, :], w[t]))
                    for t in range(TT):
                        chain(dve.match_replace(w[t], m8[:, t, :], w[t], MARK))
                chain(dve.tensor_scalar(madd[:], work[:], MARK, MASKED, ALU.not_equal, ALU.mult))
                for t in range(TT):
                    d = madd[:, 2 * t * P:2 * t * P + P]
                    chain(dve.tensor_tensor(d, d, cst[:, C_NEG:C_NEG + P], ALU.add))
                for t in range(TT):
                    nk = P * (t + 1)
                    dve.wait_ge(s_lg, 2 * l + t + 1)
                    if t:
                        dve.wait_ge(s_ex, 2 * l + t)
                    ma = madd[:, t * P:t * P + nk].rearrange("p (o s) -> p o s", o=1).broadcast_to([P, 2, nk])
                    for j in range(4):
                        ins = dve.scalar_tensor_tensor(L[:, 2 * j:2 * j + 2, 0:nk],
                                                       bank[4 * t + j][:].rearrange("p (c s) -> p c s", s=S)[:, :, 0:nk],
                                                       HD ** -0.5, ma, ALU.mult, ALU.add)
                    chain(ins)
                    chain(dve.tensor_reduce(sx[:, t, 0, :], L[:, :, 0:nk], AX.X, ALU.max))
                    dve.tensor_scalar(sx[:, t, 1, :], sx[:, t, 0, :], -1.0, None, ALU.mult).then_inc(s_mx, 1)
                    for j in range(t + 1):
                        dve.wait_ge(s_pt, 6 * l + 2 * t + 2 * j + 2)
                        if t and j == 0:
                            dve.wait_ge(s_pv, 2 * l + 1)
                        dve.tensor_copy(PT[:, j, 4:8, :], bank[4 * t + 2 * j + 1][:].rearrange("p (h s) -> p h s", s=P)
                                        ).then_inc(s_ptd, 1)
                    dve.wait_ge(s_ex, 2 * l + t + 1)
                    chain(dve.reciprocal(sx[:, t, 3, :], sx[:, t, 2, :]))
                    dve.wait_ge(s_pv, 2 * l + t + 1)
                    dve.tensor_tensor(ao[:, t, :].rearrange("p (a q d) -> p a q d", a=4, q=2),
                                      bank[2 + t][:].rearrange("p (a q d) -> p a q d", a=4, q=2),
                                      sx[:, t, 3, :].rearrange("p (q a o) -> p a q o", q=2, o=1).broadcast_to([P, 4, 2, HD]),
                                      ALU.mult).then_inc(s_ao, 1)
                for j in range(2):
                    dve.wait_ge(s_phi, 2 * l + j + 1)
                    for q in range(2):
                        g = 2 * j + q
                        ins = dve.scalar_tensor_tensor(pTlo[:, g, :], bank[6 + j][:, q * S:q * S + S],
                                                       pcol[:, 32 + 4 * l + g:33 + 4 * l + g], pThi[:, g, :],
                                                       ALU.mult, ALU.subtract)
                    ins.then_inc(s_plo, 1)
                for j in range(2):
                    dve.wait_ge(s_ahi, 2 * l + j + 1)
                    dve.tensor_tensor(aTlo[:, 2 * j:2 * j + 2, :], bank[j][:].rearrange("p (k t) -> p k t", t=S),
                                      aThi[:, 2 * j:2 * j + 2, :], ALU.subtract).then_inc(s_alo, 1)
                dve.wait_ge(s_sg, l + 1)
                for nh in range(2):
                    for _ in range(2):
                        ahead(c)
                        c += 1
                    dve.wait_ge(s_use, c)
                    ga, gp = zb[:, ZGA + nh], zb[:, ZGP + nh]
                    for t in range(TT):
                        dve.tensor_tensor(ga[:, t], ga[:, t], bank[4 * nh + t][:], ALU.mult)
                        ins = dve.tensor_tensor(gp[:, t], gp[:, t], bank[4 * nh + 2 + t][:], ALU.mult)
                    chain(ins)
                    dve.tensor_tensor(ga, ga, gp, ALU.add).then_inc(s_m, 1)
                hT_lo(3 * l + 1, None)
                for nh in range(2):
                    for _ in range(2):
                        ahead(c)
                        c += 1
                    dve.wait_ge(s_use, c)
                    for t in range(TT):
                        v = X[:, t, 512 * nh:512 * nh + 512]
                        ins = dve.tensor_tensor(v, v, bank[4 + 2 * nh + t][:], ALU.add)
                ins.then_inc(s_xd, 1)
                norm(2 * l + 1)
                hT_lo(3 * l + 2, 16 + 8 * l)

            for s in (s_flo, m_flo, m_ylo):
                dve.nop().then_inc(s, LEAD)
            dve.wait_ge(s_prt, 1)
            dve.tensor_copy(pcol[:], bank[6][:, 0:40]).then_inc(s_pcol, 1)
            dve.tensor_copy(gain[:].rearrange("p l j d -> p (l j d)"), bank[7][:, 0:4 * HD]).then_inc(s_pcol, 1)
            for c in range(LOOK):
                split(c, chunk_words(c))
            layer(0, 0)

            def mul_d(b, q):
                dve.wait_ge(s_si, b + 1)
                for t in range(TT):
                    ins = dve.tensor_tensor(hsD[:, q, t, :], hsD[:, q, t, :], bank[4 + 2 * q + t][:, 256:512], ALU.mult)
                ins.then_inc(s_hm, 1)

            def hid_lo_d(b, q):
                dve.wait_ge(s_fhi, b + 1)
                hi, lo = (x[:, 2 * b:2 * b + 2, :] if isinstance(b, int) else x[:, bass.ds(b * 2, 2), :]
                          for x in (hidDhi, hidDlo))
                dve.tensor_tensor(lo, bank[q][:].rearrange("p (k t) -> p k t", t=S), hi, ALU.subtract).then_inc(s_flo, 1)

            ahead(DENSE0)
            mul_d(0, 0)
            ahead(DENSE0 + 1)
            with dve.Fori(0, 4) as it:
                for u in range(2):
                    c = DENSE0 + 2 + 2 * u
                    split(c + LOOK, FULL, it)
                    hid_lo_d(it * 2 + u, u)
                    mul_d(it * 2 + (1 + u), 1 - u)
                    split(c + 1 + LOOK, FULL, it)
            for b in range(9, NB_D):
                ahead(DENSE0 + 2 * b)
                hid_lo_d(b - 1, (b - 1) % 2)
                mul_d(b, b % 2)
                ahead(DENSE0 + 2 * b + 1)
            hid_lo_d(NB_D - 1, (NB_D - 1) % 2)
            c = DENSE0 + 2 * NB_D
            with dve.Fori(0, 4) as it:
                for k in range(SLOTS):
                    split(c + k + LOOK, HALF, it)
            for k in range(16, KC_D):
                ahead(c + k)
            dve.wait_ge(s_use, LAYER1)
            for t in range(TT):
                for nh in range(2):
                    v = X[:, t, 512 * nh:512 * nh + 512]
                    ins = dve.tensor_tensor(v, v, bank[4 + 2 * t + nh][:], ALU.add)
            ins.then_inc(s_xd, 1)

            layer(1, LAYER1)

            for t in range(TT):
                dve.wait_ge(s_xr, t + 1)
                dve.tensor_tensor(xrlo[:, t, :], xs[:, t, :], xrhi[:, t, :], ALU.subtract).then_inc(s_xrl, 1)
            dve.wait_ge(s_wrh, 1)
            dve.tensor_tensor(wrlo[:], wr[:], wrhi[:], ALU.subtract).then_inc(s_wrh, 1)
            dve.wait_ge(s_rt, 1)
            for z in (yhi, ylo, selT[:]):
                ins = dve.memset(z.bitcast(F32), 0.0)
            ins.then_inc(s_y0, 1)
            chain(dve.tensor_copy(lg[:].rearrange("p t e -> p (t e)"), bank[4][:, 0:TT * E]))
            for t in range(TT):
                chain(dve.max(v8[:, t, :], lg[:, t, :]))
            for t in range(TT):
                chain(dve.max_index(ix8[:, t, :], v8[:, t, :], lg[:, t, :]))
            dve.tensor_tensor(pr[:, 0, :], v8[:, :, 1], v8[:, :, 0], ALU.subtract).then_inc(s_gd, 1)
            chain(dve.tensor_copy(ixf[:], ix8[:]))
            iota8 = cst[:, C_IOTA:C_IOTA + E]
            for t in range(TT):
                dve.tensor_scalar(m0[:, t, :], iota8, ixf[:, t, 0:1], None, ALU.is_equal)
                chain(dve.tensor_scalar(m1[:, t, :], iota8, ixf[:, t, 1:2], None, ALU.is_equal))
            chain(dve.tensor_tensor(tmp8[:], m0[:], m1[:], ALU.add))
            dve.nop().then_inc(s_mk, 1)
            dve.wait_ge(s_ge, 1)
            chain(dve.tensor_scalar(pr[:, 2, :], pr[:, 1, :], 1.0, None, ALU.add))
            chain(dve.reciprocal(pr[:, 2, :], pr[:, 2, :]))
            chain(dve.tensor_tensor(pr[:, 3, :], pr[:, 1, :], pr[:, 2, :], ALU.mult))
            for t in range(TT):
                chain(dve.tensor_scalar(gate[:, t, :], m0[:, t, :], pr[:, 2, t:t + 1], None, ALU.mult))
                chain(dve.scalar_tensor_tensor(gate[:, t, :], m1[:, t, :], pr[:, 3, t:t + 1], gate[:, t, :],
                                               ALU.mult, ALU.add))
            dve.wait_ge(s_pos, 1)
            pos = bank[5][:, 0:2 * E].rearrange("p (t e) -> p t e", t=TT)
            chain(dve.scalar_tensor_tensor(pm[:], pos, 1.0, tmp8[:], ALU.add, ALU.mult))
            chain(dve.tensor_scalar(pm[:], pm[:], -1.0, None, ALU.add))
            dve.tensor_copy(posj[:, :, 0:E], pm[:])
            dve.memset(gatej[:, :, 0:1], 0.0)
            chain(dve.tensor_copy(gatej[:, :, 1:E + 1], gate[:]))

            def select(i):
                for t in range(TT):
                    col = posj[:, t, i:i + 1] if isinstance(i, int) else posj[:, t, bass.ds(i, 1)]
                    ins = dve.tensor_scalar(selR[:, t, :], cst[:, C_IOTA:C_IOTA + P], col, None, ALU.is_equal)
                ins.then_inc(s_sel, 1)

            select(0)
            over, cum, rank, one8 = (ov[:, i, :] for i in range(4))
            dve.tensor_scalar(over, bank[5][:, 2 * E:3 * E], float(P), None, ALU.is_gt)
            chain(dve.memset(one8, 1.0))
            chain(dve.tensor_tensor_scan(cum, one8, over, 0.0, ALU.mult, ALU.add))
            chain(dve.tensor_tensor(rank, cum, over, ALU.mult))
            dve.tensor_copy(tabf[:, 0:E], iota8)
            dve.memset(tabf[:, NJ:15], 0.0)
            chain(dve.tensor_scalar(tabf[:, 15:16], cum[:, E - 1:E], float(E), None, ALU.add))
            for q in range(NJ - E):
                chain(dve.tensor_scalar(one8, rank, float(q + 1), None, ALU.is_equal))
                pick = ov[:, 3:4, :].broadcast_to([P, TT, E])
                chain(dve.tensor_tensor(tmp8[:], pm[:], pick, ALU.mult))
                chain(dve.tensor_reduce(pr[:, 0, :], tmp8[:], AX.X, ALU.add))
                dve.tensor_scalar(posj[:, :, E + q], pr[:, 0, :], -float(P), None, ALU.add)
                chain(dve.tensor_tensor(tmp8[:], gate[:], pick, ALU.mult))
                chain(dve.tensor_reduce(gatej[:, :, E + q + 1], tmp8[:], AX.X, ALU.add))
                chain(dve.tensor_tensor(tmp8[:, 0, :], iota8, one8, ALU.mult))
                chain(dve.tensor_reduce(tabf[:, E + q:E + q + 1], tmp8[:, 0, :], AX.X, ALU.add))
            dve.tensor_copy(tabi[:], tabf[:]).then_inc(s_tab, 1)

            def gathered_lo(i):
                for j in range(2):
                    dve.wait_ge(s_ghi, i * 2 + (j + 1))
                    for q in range(4):
                        k = 4 * j + q
                        ins = dve.scalar_tensor_tensor(helo[:, k, :], bank[2 + j][:, q * P:q * P + P],
                                                       pcol[:, 24 + k:25 + k], hehi[:, k, :], ALU.mult, ALU.subtract)
                    ins.then_inc(s_glo, 1)

            def add_rows(i):
                for t in range(TT):
                    for nh in range(2):
                        dve.wait_ge(m_sc, i * 4 + 2 * t + nh + 1)
                        v = X[:, t, 512 * nh:512 * nh + 512]
                        dve.scalar_tensor_tensor(v, bank[4 * t + 2 + nh][:], gatej[:, t, bass.ds(i, 1)], v,
                                                 ALU.mult, ALU.add).then_inc(m_xa, 1)

            gathered_lo(0)
            dve.wait_ge(s_tab, 1)
            njobs = dve.value_load(tabi[0:1, 15:16], min_val=E, max_val=NJ - 1)
            with dve.Fori(0, njobs) as i:
                j8 = i * (JOB_CHUNKS // 8)

                def mul_m(b, q):
                    dve.wait_ge(m_si, i * NB_E + b + 1)
                    dve.tensor_tensor(hsM[:, q, :], hsM[:, q, :], bank[4 + q][:, 256:512], ALU.mult).then_inc(m_hm, 1)

                def hid_lo_m(b, q):
                    dve.wait_ge(m_fhi, i * NB_E + b + 1)
                    hi, lo = (x[:, 2 * b:2 * b + 2, :] if isinstance(b, int) else x[:, bass.ds(b * 2, 2), :]
                              for x in (hidMhi, hidMlo))
                    dve.tensor_tensor(lo, bank[q][:, 0:256].rearrange("p (k t) -> p k t", t=P), hi,
                                      ALU.subtract).then_inc(m_flo, 1)

                def pair(p, n, more=0, dyn=0, first=False):
                    for u in range(2):
                        m = 4 * p + 2 * u + LOOK
                        b = more * 2 + (2 * p + u)
                        if first and u == 1:
                            add_rows(i)
                        split_m(m, n, j8 + dyn)
                        if not (first and u == 0):
                            hid_lo_m(b - 1, 1 - u)
                        if first and u == 1:
                            dve.wait_ge(s_st, i + 1)
                            select(i + 1)
                        mul_m(b, u)
                        split_m(m + 1, n, j8 + dyn)

                pair(0, FULL, first=True)
                with dve.Fori(0, 2) as it:
                    pair(1, FULL, it * 2, it)
                    pair(2, FULL, it * 2, it)
                pair(5, FULL)
                pair(6, HALF)
                d0 = 2 * NB_E + LOOK
                for k in range(4):
                    split_m(d0 + k, HALF, j8)
                gathered_lo(i + 1)
                hid_lo_m(NB_E - 1, (NB_E - 1) % 2)
                with dve.Fori(0, 2) as it:
                    for k in range(4, 12):
                        split_m(d0 + k, HALF, j8 + it)
                for k in range(20, 24):
                    split_m(d0 + k, HALF, j8)
                for k in range(24, 27):
                    split_m(d0 + k, FULL, j8)
                for j in range(2):
                    dve.wait_ge(m_yhi, i * 2 + j + 1)
                    dve.tensor_tensor(ylo[:, 4 * j:4 * j + 4, :], bank[6 + j][:].rearrange("p (k n) -> p k n", n=P),
                                      yhi[:, 4 * j:4 * j + 4, :], ALU.subtract).then_inc(m_ylo, 1)
                split_m(d0 + 27, FULL, j8)
            add_rows(njobs)


def shape_constants():
    c = np.zeros((P, C_END), np.float32)
    i = np.arange(P)
    c[:, C_ID:C_ID + P] = np.eye(P)
    c[:, C_TRI:C_TRI + P] = i[:, None] < i[None, :]
    c[:, C_NEG:C_NEG + P] = np.where(i[None, :] <= i[:, None], 0.0, NEG)
    c[:, C_IOTA:C_IOTA + P] = i[None, :]
    c[:, C_ONE:C_ONE + P] = 1.0
    pos = np.arange(S, dtype=np.float32)
    for rot, co, so in ((ROT, C_COS, C_SIN), (IROT, C_COSI, C_SINI)):
        inv = np.power(np.float32(THETA), -np.arange(0, rot, 2, dtype=np.float32) / np.float32(rot))
        ang = (pos[:, None] * inv[None, :]).astype(np.float32)
        for f, o in ((np.cos, co), (np.sin, so)):
            t = f(ang.astype(np.float64)).astype(np.float32).reshape(TT, P, rot // 2)
            c[:, o:o + TT * rot // 2] = t.transpose(1, 0, 2).reshape(P, -1)
    band = np.zeros((GROUPS, S, S))
    for g, w in enumerate(WINDOWS):
        for t in range(S):
            band[g, max(0, t - w + 1):t + 1, t] = 1.0 / min(t + 1, w)
            band[g, t, t] -= 1.0
    b = np.concatenate([band[:, 0:P, :], band[:, P:, P:]], axis=2).transpose(1, 0, 2)
    return c, np.ascontiguousarray(b.astype(np.float32))


_INS = ["x", "mix_norm", "w_in", "q_norm", "k_norm", "w_pool", "pool_scale", "w_attn_proj", "w_pool_proj", "w_out",
        "ffn_norm", "dense_w1", "dense_w3", "dense_w2", "moe_router", "moe_w1", "moe_w3", "moe_w2"]


def kernel(**inputs):
    import concourse.bacc as _bacc
    from concourse.bass_utils import run_bass_kernel_spmd as _run

    nc = _bacc.Bacc("TRN2", target_bir_lowering=False, num_devices=1)
    arrays = {f"in_{n}": np.ascontiguousarray(inputs[n]) for n in _INS}
    arrays["in_consts"], arrays["in_pool_band"] = shape_constants()
    A = {n[3:]: nc.dram_tensor(n, a.shape, mybir.dt.from_np(a.dtype), kind="ExternalInput").ap()
         for n, a in arrays.items()}
    o = nc.dram_tensor("out_0", (1, S, D), F32, kind="ExternalOutput").ap()
    build(nc, A, o)
    r = _run(nc, [arrays], core_ids=[0])
    return r.results[0]["out_0"]
```

```python
from contextlib import ExitStack

import numpy as np

import concourse.bass as bass
from concourse import mybir

F32 = mybir.dt.float32
FR = mybir.dt.float32r
I32 = mybir.dt.int32
U32 = mybir.dt.uint32
ALU = mybir.AluOpType
ACT = mybir.ActivationFunctionType
AX = mybir.AxisListType

P = 128
D = 1024
S = 256
TT = S // P
KC = D // P
HEADS, HD, ROT = 8, 64, 16
AW = HEADS * HD
IH, IDIM, IROT = 8, 32, 8
IDXW = IH * IDIM + IDIM + IH
TOPK = 64
GROUPS = 4
WINDOWS = (2, 4, 8, 16)
FF = 2816
E = 8
FFE = 3584
EPS = 1e-6
NEG = -1e38
MARK = -3e38
MASKED = -1e30
THETA = 500000.0

SLOTS = 4
LOOK = SLOTS
LEAD = 2
FULL = 2048
HALF = 1024
NB_D = FF // 256
NB_E = FFE // 256
KC_D = FF // P
KC_E = FFE // P
ZCOL = [0, 512, 1024, 1832, 3368, 3880, 2344, 2856]
ZQ, ZK, ZV, ZU, ZGP, ZGA = 0, 1, 2, 3, 4, 6
NZ = 1 + len(ZCOL)
MIX_CHUNKS = 2 + 2 * len(ZCOL) + 4 + 4
DENSE0 = MIX_CHUNKS
LAYER1 = DENSE0 + 2 * NB_D + KC_D
MOE0 = LAYER1 + MIX_CHUNKS
JOB_CHUNKS = 2 * NB_E + KC_E
NJ = 12

C_ID, C_TRI, C_NEG, C_IOTA, C_ONE = 0, 128, 256, 384, 512
C_COS, C_SIN, C_COSI, C_SINI = 640, 656, 672, 680
C_END = 688


def chunk_words(c):
    m = c - (LAYER1 if c >= LAYER1 else 0)
    if m < 2:
        return (KC // 2) * IDXW
    if DENSE0 + 2 * NB_D <= c < LAYER1:
        return HALF
    return FULL


def build(nc, A, out):
    with ExitStack() as ctx:
        def sb(name, shape, dt=F32, where=ctx):
            return where.enter_context(nc.sbuf_tensor(name, shape, dt))

        def sem(name):
            return ctx.enter_context(nc.semaphore(name))

        raw = sb("w_raw", [P, SLOTS, FULL])
        whi = sb("w_hi", [P, SLOTS, FULL], FR)
        wlo = sb("w_lo", [P, SLOTS, FULL], FR)
        X = sb("x_residual", [P, TT, D])
        hThi = sb("hT_hi", [P, KC, S], FR)
        hTlo = sb("hT_lo", [P, KC, S], FR)
        cst = sb("shape_constants", [P, C_END])
        pcol = sb("param_columns", [P, 40])
        gain = sb("qk_gain", [P, 2, 2, HD])
        st = sb("norm_stats", [P, 4, TT])
        ident = cst[:, C_ID:C_ID + P]
        mixer = ExitStack()
        zb = sb("z_blocks", [P, 8, TT, 512], F32, mixer)
        zi = sb("z_index", [P, TT, IDXW], F32, mixer)
        wis = sb("w_index", [P, TT, IH], F32, mixer)
        wpool = sb("w_pool", [P, GROUPS, P], F32, mixer)
        band = sb("pool_band", [P, GROUPS, 3 * P], F32, mixer)
        diffT = sb("pool_diffT", [P, GROUPS, S], F32, mixer)
        work = sb("topk_work", [P, P + S], F32, mixer)
        madd = sb("mask_add", [P, P + S], F32, mixer)
        m8 = sb("max8", [P, TT, 8], F32, mixer)
        ao = sb("attn_out", [P, TT, AW], F32, mixer)
        ki4 = ao[:, :, 0:4 * IDIM].rearrange("p t (a d) -> p t a d", d=IDIM)
        hs32 = sb("head_stats", [P, 3, 32], F32, mixer)
        sx = sb("softmax_stats", [P, TT, 4, HEADS], F32, mixer)
        PT = sb("probsT", [P, 2, HEADS, P], F32, mixer)
        L0 = PT[:, 1]
        PT0 = diffT[:].rearrange("p g (a s) -> p (g a) s", s=P)
        att = ExitStack()
        qT = sb("qT", [P, 4, S], F32, att)
        kT = sb("kT", [P, 4, S], F32, att)
        L = sb("logits", [P, HEADS, S], F32, att)
        qiT = sb("qiT", [P, 2, S], F32, att)
        kiT = sb("kiT", [P, S], F32, att)
        att.close()
        proj = ExitStack()
        pThi = sb("pT_hi", [P, 4, S], FR, proj)
        pTlo = sb("pT_lo", [P, 4, S], FR, proj)
        aThi = sb("aT_hi", [P, 4, S], FR, proj)
        aTlo = sb("aT_lo", [P, 4, S], FR, proj)
        proj.close()
        mixer.close()
        setup = ExitStack()
        xs = sb("x_normed", [P, TT, D], F32, setup)
        prow = sb("param_rows", [40, P], F32, setup)
        nrow = sb("gain_row", [1, 4 * HD], F32, setup)
        dense = ExitStack()
        hidDhi = sb("hidden_hi", [P, KC_D, S], FR, dense)
        hidDlo = sb("hidden_lo", [P, KC_D, S], FR, dense)
        hsD = sb("hidden", [P, 2, TT, 256], F32, dense)
        dense.close()
        setup.close()
        moe = ExitStack()
        raw7 = sb("w_raw_7", [P, FULL], F32, moe)
        raw456 = sb("w_raw_456", [P, 3, FULL], F32, moe)
        raw8 = [raw[:, k] for k in range(4)] + [raw456[:, k] for k in range(3)] + [raw7[:]]
        xrhi = sb("x_rows_hi", [P, TT, D], FR, moe)
        xrlo = sb("x_rows_lo", [P, TT, D], FR, moe)
        hehi, helo = hThi[:, :, 0:P], hTlo[:, :, 0:P]
        yhi, ylo = hThi[:, :, P:S], hTlo[:, :, P:S]
        hidMhi = sb("hiddenM_hi", [P, KC_E, P], FR, moe)
        hidMlo = sb("hiddenM_lo", [P, KC_E, P], FR, moe)
        hsM = sb("hiddenM", [P, 2, 256], F32, moe)
        selR = sb("select", [P, TT, P], FR, moe)
        selT = sb("selectT", [P, S], FR, moe)
        identR = sb("identity_r", [P, P], FR, moe)
        wr = sb("w_router", [P, KC, E], F32, moe)
        wrhi = sb("w_router_hi", [P, KC, E], FR, moe)
        wrlo = sb("w_router_lo", [P, KC, E], FR, moe)
        lg = sb("router_logits", [P, TT, E], F32, moe)
        v8 = sb("router_top", [P, TT, 8], F32, moe)
        ix8 = sb("router_index", [P, TT, 8], U32, moe)
        ixf = sb("router_index_f", [P, TT, 8], F32, moe)
        m0 = sb("mask_first", [P, TT, E], F32, moe)
        m1 = sb("mask_second", [P, TT, E], F32, moe)
        pr = sb("gate_probs", [P, 4, TT], F32, moe)
        gate = sb("gate", [P, TT, E], F32, moe)
        pm = sb("slot_of_token", [P, TT, E], F32, moe)
        ov = sb("overflow", [P, 4, E], F32, moe)
        tmp8 = sb("routing_tmp", [P, TT, E], F32, moe)
        posj = sb("slot_by_job", [P, TT, NJ], F32, moe)
        gatej = sb("gate_by_job", [P, TT, NJ + 1], F32, moe)
        tabf = sb("job_table_f", [P, 16], F32, moe)
        tabi = sb("job_table", [P, 16], I32, moe)
        moe.close()

        bank = [ctx.enter_context(nc.psum_tensor(f"bank{i}", [P, 512], F32)) for i in range(8)]

        s_x = sem("x_loaded")
        s_cst = sem("constants_loaded")
        s_par = sem("params_loaded")
        s_wrl = sem("router_loaded")
        s_pool = [sem(f"pool_weights_loaded{i}") for i in range(2)]
        s_ld = [sem(f"chunk_loaded{i}") for i in range(2 * SLOTS)]
        s_hi = sem("chunk_hi")
        s_lo = sem("chunk_lo")
        s_use = sem("chunk_used")
        s_prt = sem("paramsT_done")
        s_pcol = sem("param_columns_ready")
        s_sq = sem("sumsq_done")
        s_ms = sem("meansq_done")
        s_rms = sem("rms_done")
        s_rs = sem("rstd_ready")
        s_lgs = sem("logits_in_sbuf")
        s_gp = sem("pool_branch_gated")
        s_xs = sem("xs_done")
        s_tr = sem("transposed")
        s_thi = sem("hT_hi_done")
        s_tlo = sem("hT_lo_done")
        s_za = sem("z_evac_act")
        s_idx = sem("index_ready")
        s_idxT = sem("indexT_done")
        s_idxs = sem("indexT_in_sbuf")
        s_dot = sem("index_dots_done")
        s_rel = sem("relu_done")
        s_sc = sem("scores_done")
        s_qms = sem("qk_meansq")
        s_qrm = sem("qk_rms")
        s_qk = sem("qk_roped")
        s_qkT = sem("qkT_done")
        s_qks = sem("qkT_in_sbuf")
        s_lg = sem("qk_products")
        s_mx = sem("row_max_ready")
        s_ex = sem("exp_done")
        s_pt = sem("probsT_done")
        s_pta = sem("probsT_evac_act")
        s_ptd = sem("probsT_evac_dve")
        s_pv = sem("pv_done")
        s_ao = sem("attn_out_ready")
        s_aT = sem("aT_done")
        s_ahi = sem("aT_hi_done")
        s_alo = sem("aT_lo_done")
        s_df = sem("pool_diff_done")
        s_dfs = sem("pool_diff_in_sbuf")
        s_pp = sem("pool_mixed_done")
        s_phi = sem("pT_hi_done")
        s_plo = sem("pT_lo_done")
        s_m = sem("merged_ready")
        s_xd = sem("x_updated")
        s_si = sem("ffn_silu_done")
        s_hm = sem("ffn_hidden_done")
        s_ft = sem("ffn_hiddenT_done")
        s_fhi = sem("ffn_hiddenT_hi")
        s_flo = sem("ffn_hiddenT_lo")
        s_xr = sem("x_rows_hi_done")
        s_xrl = sem("x_rows_lo_done")
        s_wrh = sem("router_hi_done")
        s_rt = sem("router_done")
        s_gd = sem("gate_diff")
        s_ge = sem("gate_exp")
        s_mk = sem("expert_mask_ready")
        s_pos = sem("positions_done")
        s_tab = sem("job_table_ready")
        s_sel = sem("select_ready")
        s_g = sem("gather_done")
        s_ghi = sem("gather_hi")
        s_glo = sem("gather_lo")
        s_st = sem("selectT_done")
        s_sts = sem("selectT_in_sbuf")
        m_si = sem("moe_silu_done")
        m_hm = sem("moe_hidden_done")
        m_ft = sem("moe_hiddenT_done")
        m_fhi = sem("moe_hiddenT_hi")
        m_flo = sem("moe_hiddenT_lo")
        s_y0 = sem("moe_y_cleared")
        m_yhi = sem("moe_y_hi")
        m_ylo = sem("moe_y_lo")
        m_sc = sem("moe_scatter_done")
        m_xa = sem("moe_x_added")
        s_dve = sem("dve_step")
        s_act = sem("act_step")
        s_out = sem("out_stored")

        block = ctx.enter_context(nc.Block())

        @block.sync
        def _(sp):
            def load(c, parts, dyn=0):
                if not (isinstance(dyn, int) and c < SLOTS):
                    sp.wait_ge(s_lo, dyn * SLOTS + (c - SLOTS + 1))
                for dst, src in parts:
                    sp.dma_start(dst, src).then_inc(s_ld[c % SLOTS], 16)

            def k_halves(c, w, rows, col, width):
                t = raw[:, c % SLOTS, 0:4 * width].rearrange("p (k n) -> p k n", n=width)
                v = w[rows:rows + 512, col:col + width].rearrange("(k p) n -> p k n", p=P)
                return [(t[:, 0:2], v[:, 0:2]), (t[:, 2:4], v[:, 2:4])]

            def up_pair(c, w1, w3, half, col):
                t = raw[:, c % SLOTS, :].rearrange("p (k n) -> p k n", n=512)
                rows = slice(half * 512, half * 512 + 512)
                return [(t[:, :, 256 * j:256 * j + 256],
                         w[rows, col].rearrange("(k p) n -> p k n", p=P)) for j, w in enumerate((w1, w3))]

            def down_row(c, w2, row):
                t = raw[:, c % SLOTS, 0:HALF]
                return [(t[:, 512 * j:512 * j + 512], w2[row, 512 * j:512 * j + 512]) for j in range(2)]

            def mixer_loads(l, c):
                w = A["w_in"][l]
                for h in range(2):
                    load(c, k_halves(c, w, 512 * h, 1536, IDXW))
                    c += 1
                for col in ZCOL:
                    for h in range(2):
                        load(c, k_halves(c, w, 512 * h, col, 512))
                        c += 1
                for name in ("w_pool_proj", "w_attn_proj"):
                    for nh in range(2):
                        load(c, k_halves(c, A[name][l], 0, 512 * nh, 512))
                        c += 1
                for h in range(2):
                    for nh in range(2):
                        load(c, k_halves(c, A["w_out"][l], 512 * h, 512 * nh, 512))
                        c += 1

            sp.dma_start(X[:], A["x"][0].rearrange("(t p) d -> p t d", p=P)).then_inc(s_x, 16)
            sp.dma_start(cst[:], A["consts"]).then_inc(s_cst, 16)
            for name, r, n in (("mix_norm", 0, 16), ("ffn_norm", 16, 16), ("pool_scale", 32, 8)):
                sp.dma_start(prow[r:r + n, :], A[name].rearrange("l (k p) -> (l k) p", p=P)).then_inc(s_par, 16)
            for j, name in enumerate(("q_norm", "k_norm")):
                v = nrow[:].rearrange("o (l j d) -> o l j d", l=2, j=2)
                for l in range(2):
                    sp.dma_start(v[:, l, j], A[name][l:l + 1, :]).then_inc(s_par, 16)
            for l in range(2):
                base = l * LAYER1
                mixer_loads(l, base)
                if l == 0:
                    for b in range(NB_D):
                        for h in range(2):
                            c = DENSE0 + 2 * b + h
                            load(c, up_pair(c, A["dense_w1"][0], A["dense_w3"][0], h, slice(256 * b, 256 * b + 256)))
                    for k in range(KC_D):
                        c = DENSE0 + 2 * NB_D + k
                        load(c, down_row(c, A["dense_w2"][0], slice(P * k, P * k + P)))

            w1, w3, w2 = (A[n][0].rearrange("e k n -> (e k) n") for n in ("moe_w1", "moe_w3", "moe_w2"))

            def up_chunk(m, e, g):
                t = raw8[m % 8].rearrange("p (k n) -> p k n", n=512)
                for j, w in enumerate((w1, w3)):
                    src = w[bass.ds(e * D + (m % 2) * 512, 512), bass.ds(g * 512 + (m % 4 // 2) * 256, 256)]
                    sp.dma_start(t[:, :, 256 * j:256 * j + 256],
                                 src.rearrange("(k p) n -> p k n", p=P)).then_inc(s_ld[m % 8], 16)

            def down_chunk(m, e, g):
                for j in range(2):
                    sp.dma_start(raw8[m % 8][:, 512 * j:512 * j + 512],
                                 w2[bass.ds(e * FFE + g * 512 + (m % 4) * P, P), 512 * j:512 * j + 512]
                                 ).then_inc(s_ld[m % 8], 16)

            def group(load_chunk, i, e, first, g, more=0):
                for k in range(4):
                    sp.wait_ge(s_lo, i * JOB_CHUNKS + more + (MOE0 + first + k - 8 + 1))
                    load_chunk(first + k, e, g)

            def job_loads(i, e):
                with sp.Fori(0, 2) as it:
                    for u in range(2):
                        group(up_chunk, i, e, 8 + 4 * u, it * 2 + (2 + u), it * 8)
                group(up_chunk, i, e, 24, 6)
                group(down_chunk, i, e, 28, 0)
                with sp.Fori(0, 3) as it:
                    for u in range(2):
                        group(down_chunk, i, e, 32 + 4 * u, it * 2 + (1 + u), it * 8)

            def next_job(i, e):
                for g in range(2):
                    group(up_chunk, i, e, JOB_CHUNKS + 4 * g, g)

            for m in range(8):
                if m < 4:
                    sp.wait_ge(s_lo, MOE0 + m - SLOTS + 1)
                elif m == 4:
                    sp.wait_ge(s_xd, 6)
                elif m == 7:
                    sp.wait_ge(s_xrl, 2)
                up_chunk(m, 0, m // 4)
            with sp.Fori(0, E - 1) as i:
                job_loads(i, i)
                next_job(i, i + 1)
            sp.wait_ge(s_tab, 1)
            njobs = sp.value_load(tabi[0:1, 15:16], min_val=E, max_val=NJ - 1)
            with sp.Fori(E - 1, njobs) as i:
                e = sp.value_load(tabi[0:1, bass.ds(i, 1)], min_val=0, max_val=E - 1)
                job_loads(i, e)
                with sp.If(i < njobs - 1):
                    en = sp.value_load(tabi[0:1, bass.ds(i + 1, 1)], min_val=0, max_val=E - 1)
                    next_job(i, en)
            for k in range(SLOTS):
                sp.wait_ge(s_lo, njobs * JOB_CHUNKS + (MOE0 + k - 8 + 1))
                for j in range(2):
                    sp.dma_start(raw8[k][:, 128 * j:128 * j + 128], A["moe_w2"][0, 0, 0:P, 0:P]).then_inc(s_ld[k], 16)
            sp.wait_ge(m_xa, njobs * 4 + 4)
            sp.dma_start(out[0].rearrange("(t p) d -> p t d", p=P), X[:]).then_inc(s_out, 16)
            sp.wait_ge(s_out, 16)

        @block.gpsimd
        def _(pool):
            for l in range(2):
                if l:
                    pool.wait_ge(s_xd, 4)
                pool.dma_start(band[:], A["pool_band"]).then_inc(s_pool[0], 16)
                pool.dma_start(wpool[:], A["w_pool"][l].rearrange("g c d -> c g d")).then_inc(s_pool[1], 16)
            pool.wait_ge(s_xd, 6)
            pool.dma_start(wr[:], A["moe_router"][0].rearrange("(k p) e -> p k e", p=P)).then_inc(s_wrl, 16)

        @block.scalar
        def _(act):
            steps = [0]

            def chain(ins):
                steps[0] += 1
                ins.then_inc(s_act, 1)
                act.wait_ge(s_act, steps[0])

            def split(c, n, dyn=0):
                act.wait_ge(s_ld[c % SLOTS], dyn * 32 + 32 * (c // SLOTS + 1))
                if not (isinstance(dyn, int) and c < SLOTS):
                    act.wait_ge(s_use, dyn * SLOTS + (c - SLOTS + 1))
                act.activation(whi[:, c % SLOTS, 0:n], raw[:, c % SLOTS, 0:n], ACT.Copy).then_inc(s_hi, 1)

            def split_m(m, n, dyn):
                act.wait_ge(s_ld[m % 8], dyn * 32 + 32 * (m // 8 + 1 + (MOE0 // SLOTS if m % 8 < 4 else 0)))
                act.wait_ge(s_use, dyn * 8 + (MOE0 + m - SLOTS + 1))
                act.activation(whi[:, m % SLOTS, 0:n], raw8[m % 8][:, 0:n], ACT.Copy).then_inc(s_hi, 1)

            def ahead(c):
                split(c + LOOK, chunk_words(c + LOOK) if c + LOOK < MOE0 else FULL)

            def hT_hi(te, scale0, js=range(4)):
                for j in js:
                    act.wait_ge(s_tr, 4 * te + j + 1)
                    if scale0 is None:
                        act.activation(hThi[:, 2 * j:2 * j + 2, :], bank[j][:].rearrange("p (k t) -> p k t", t=S),
                                       ACT.Copy).then_inc(s_thi, 1)
                        continue
                    for q in range(2):
                        k = 2 * j + q
                        ins = act.activation(hThi[:, k, :], bank[j][:, q * S:q * S + S], ACT.Copy,
                                             scale=pcol[:, scale0 + k:scale0 + k + 1])
                    ins.then_inc(s_thi, 1)

            def norm(k):
                if k:
                    act.wait_ge(s_xd, 2 * k)
                for t in range(TT):
                    act.activation(xs[:, t, :], X[:, t, :], ACT.Square, accum_out=st[:, 0, t:t + 1]).then_inc(s_sq, 1)
                act.wait_ge(s_ms, k + 1)
                act.activation(st[:, 2, :], st[:, 1, :], ACT.Sqrt).then_inc(s_rms, 1)

            def layer(l, c0):
                def evac(n):
                    act.wait_ge(s_use, c0 + 2 * n + 2)
                    for t in range(TT):
                        src = bank[4 + 2 * (n % 2) + t]
                        dst, src = (zi[:, t, :], src[:, 0:IDXW]) if n == 0 else (zb[:, n - 1, t, :], src[:])
                        act.activation(dst, src, ACT.Sigmoid if n > ZGP else ACT.Copy,
                                       scale=st[:, 3, t:t + 1]).then_inc(s_za, 1)

                def relu(t):
                    nk = P * (t + 1)
                    act.wait_ge(s_dot, 2 * l + t + 1)
                    if t:
                        act.wait_ge(s_sc, 2 * l + 1)
                    for j in range(4):
                        ins = act.activation(L[:, 2 * j:2 * j + 2, 0:nk],
                                             bank[j][:].rearrange("p (c s) -> p c s", s=S)[:, :, 0:nk],
                                             ACT.Relu, scale=IDIM ** -0.5)
                    ins.then_inc(s_rel, 1)

                def exps(t):
                    nk = P * (t + 1)
                    src = L if t else L0
                    act.wait_ge(s_mx, 2 * l + t + 1)
                    if t:
                        act.wait_ge(s_pt, 6 * l + 2)
                    for h in range(HEADS):
                        ins = act.activation(Pr[:, h, 0:nk], src[:, h, 0:nk], ACT.Exp, bias=sx[:, t, 1, h:h + 1],
                                             accum_out=sx[:, t, 2, h:h + 1])
                    ins.then_inc(s_ex, 1)

                Pr = zb[:, 0:2].rearrange("p b t (h s) -> p (b t h) s", s=S)
                c = c0
                ahead(c)
                ahead(c + 1)
                act.wait_ge(s_rs, 2 * l + 1)
                evac(0)
                ahead(c + 2)
                ahead(c + 3)
                evac(1)
                act.wait_ge(s_idxT, l + 1)
                act.activation(qiT[:].rearrange("p c t -> p (c t)"), bank[0][:], ACT.Copy).then_inc(s_idxs, 1)
                act.activation(kiT[:], bank[1][:, 0:S], ACT.Copy).then_inc(s_idxs, 1)
                ahead(c + 4)
                relu(0)
                ahead(c + 5)
                evac(2)
                ahead(c + 6)
                relu(1)
                ahead(c + 7)
                evac(3)
                act.wait_ge(s_qms, l + 1)
                act.activation(hs32[:, 1, :], hs32[:, 0, :], ACT.Sqrt).then_inc(s_qrm, 1)
                ahead(c + 8)
                ahead(c + 9)
                evac(4)
                ahead(c + 10)
                for j in range(4):
                    act.wait_ge(s_qkT, 4 * l + j + 1)
                    dst = (qT if j < 2 else kT)[:, 2 * (j % 2):2 * (j % 2) + 2, :]
                    act.activation(dst, bank[j][:].rearrange("p (k t) -> p k t", t=S), ACT.Copy).then_inc(s_qks, 1)
                ahead(c + 11)
                evac(5)
                act.wait_ge(s_lg, 2 * l + 1)
                for p in range(2):
                    act.activation(L0[:, 4 * p:4 * p + 4, :], bank[p][:].rearrange("p (h s) -> p h s", s=P), ACT.Copy,
                                   scale=HD ** -0.5).then_inc(s_lgs, 1)
                ahead(c + 12)
                ahead(c + 13)
                evac(6)
                act.wait_ge(s_lg, 2 * l + 2)
                act.wait_ge(s_sc, 2 * l + 2)
                for j in range(4):
                    act.activation(L[:, 2 * j:2 * j + 2, :], bank[j][:].rearrange("p (h s) -> p h s", s=S), ACT.Copy,
                                   scale=HD ** -0.5).then_inc(s_lgs, 1)
                ahead(c + 14)
                for j in range(2):
                    act.wait_ge(s_df, 2 * l + j + 1)
                    act.activation(diffT[:, 2 * j:2 * j + 2, :], bank[j][:].rearrange("p (k t) -> p k t", t=S),
                                   ACT.Copy).then_inc(s_dfs, 1)
                ahead(c + 15)
                evac(7)
                for j in range(2):
                    act.wait_ge(s_pp, 2 * l + j + 1)
                    for q in range(2):
                        g = 2 * j + q
                        ins = act.activation(pThi[:, g, :], bank[2 + j][:, q * S:q * S + S], ACT.Copy,
                                             scale=pcol[:, 32 + 4 * l + g:33 + 4 * l + g])
                    ins.then_inc(s_phi, 1)
                ahead(c + 16)
                ahead(c + 17)
                evac(8)
                exps(0)
                ahead(c + 18)
                act.wait_ge(s_pt, 6 * l + 1)
                act.activation(PT0[:, 0:4, :], bank[0][:].rearrange("p (h s) -> p h s", s=P), ACT.Copy).then_inc(s_pta, 1)
                exps(1)
                for j in range(2):
                    act.wait_ge(s_pt, 6 * l + 2 * j + 3)
                    act.activation(PT[:, j, 0:4, :], bank[2 - 2 * j][:].rearrange("p (h s) -> p h s", s=P),
                                   ACT.Copy).then_inc(s_pta, 1)
                    if j == 0:
                        ahead(c + 19)
                for j in range(2):
                    act.wait_ge(s_aT, 2 * l + j + 1)
                    act.activation(aThi[:, 2 * j:2 * j + 2, :], bank[2 + j][:].rearrange("p (k t) -> p k t", t=S),
                                   ACT.Copy).then_inc(s_ahi, 1)
                ahead(c + 20)
                ahead(c + 21)
                hT_hi(3 * l + 1, None, (0, 1))
                ahead(c + 22)
                hT_hi(3 * l + 1, None, (2, 3))
                ahead(c + 23)
                ahead(c + 24)
                hT_hi(3 * l + 2, 16 + 8 * l)
                norm(2 * l + 1)
                ahead(c + 25)

            for c in range(LOOK):
                split(c, chunk_words(c))
            act.wait_ge(s_x, 16)
            act.wait_ge(s_pcol, 1)
            hT_hi(0, 0)
            norm(0)
            layer(0, 0)

            def silu_d(b, q):
                act.wait_ge(s_use, b * 2 + (DENSE0 + 2))
                for t in range(TT):
                    ins = act.activation(hsD[:, q, t, :], bank[4 + 2 * q + t][:, 0:256], ACT.Silu,
                                         scale=st[:, 3, t:t + 1])
                ins.then_inc(s_si, 1)

            def hid_hi_d(b, q):
                act.wait_ge(s_ft, b + 1)
                act.activation(hidDhi[:, bass.ds(b * 2, 2), :] if not isinstance(b, int) else hidDhi[:, 2 * b:2 * b + 2, :],
                               bank[q][:].rearrange("p (k t) -> p k t", t=S), ACT.Copy).then_inc(s_fhi, 1)

            ahead(DENSE0)
            act.wait_ge(s_rs, 2)
            silu_d(0, 0)
            ahead(DENSE0 + 1)
            with act.Fori(0, 4) as it:
                for u in range(2):
                    c = DENSE0 + 2 + 2 * u
                    split(c + LOOK, FULL, it)
                    hid_hi_d(it * 2 + u, u)
                    silu_d(it * 2 + (1 + u), 1 - u)
                    split(c + 1 + LOOK, FULL, it)
            for b in range(9, NB_D):
                ahead(DENSE0 + 2 * b)
                hid_hi_d(b - 1, (b - 1) % 2)
                silu_d(b, b % 2)
                ahead(DENSE0 + 2 * b + 1)
            hid_hi_d(NB_D - 1, (NB_D - 1) % 2)
            c = DENSE0 + 2 * NB_D
            with act.Fori(0, 4) as it:
                for k in range(SLOTS):
                    split(c + k + LOOK, HALF, it)
            for k in range(16, KC_D):
                ahead(c + k)
            hT_hi(3, 8)
            norm(2)
            layer(1, LAYER1)

            act.wait_ge(s_xs, TT)
            for t in range(TT):
                act.activation(xrhi[:, t, :], xs[:, t, :], ACT.Copy).then_inc(s_xr, 1)
            act.activation(identR[:], ident, ACT.Copy)
            act.wait_ge(s_wrl, 16)
            act.activation(wrhi[:], wr[:], ACT.Copy).then_inc(s_wrh, 1)
            act.wait_ge(s_gd, 1)
            act.activation(pr[:, 1, :], pr[:, 0, :], ACT.Exp).then_inc(s_ge, 1)

            def gathered_hi(i):
                for j in range(2):
                    act.wait_ge(s_g, i * 2 + (j + 1))
                    for q in range(4):
                        k = 4 * j + q
                        ins = act.activation(hehi[:, k, :], bank[2 + j][:, q * P:q * P + P], ACT.Copy,
                                             scale=pcol[:, 24 + k:25 + k])
                    ins.then_inc(s_ghi, 1)

            gathered_hi(0)
            act.wait_ge(s_tab, 1)
            njobs = act.value_load(tabi[0:1, 15:16], min_val=E, max_val=NJ - 1)
            with act.Fori(0, njobs) as i:
                j8 = i * (JOB_CHUNKS // 8)

                def silu_m(b, q):
                    act.wait_ge(s_use, i * JOB_CHUNKS + b * 2 + (MOE0 + 2))
                    act.activation(hsM[:, q, :], bank[4 + q][:, 0:256], ACT.Silu).then_inc(m_si, 1)

                def hid_hi_m(b, q):
                    act.wait_ge(m_ft, i * NB_E + b + 1)
                    dst = hidMhi[:, 2 * b:2 * b + 2, :] if isinstance(b, int) else hidMhi[:, bass.ds(b * 2, 2), :]
                    act.activation(dst, bank[q][:, 0:256].rearrange("p (k t) -> p k t", t=P),
                                   ACT.Copy).then_inc(m_fhi, 1)

                def pair(p, n, more=0, dyn=0, first=False):
                    for u in range(2):
                        m = 4 * p + 2 * u + LOOK
                        b = more * 2 + (2 * p + u)
                        split_m(m, n, j8 + dyn)
                        if not (first and u == 0):
                            hid_hi_m(b - 1, 1 - u)
                        if first and u == 1:
                            act.wait_ge(s_st, i + 1)
                            act.activation(selT[:], bank[1][:, 0:S], ACT.Copy).then_inc(s_sts, 1)
                        silu_m(b, u)
                        split_m(m + 1, n, j8 + dyn)

                pair(0, FULL, first=True)
                with act.Fori(0, 2) as it:
                    pair(1, FULL, it * 2, it)
                    pair(2, FULL, it * 2, it)
                pair(5, FULL)
                pair(6, HALF)
                d0 = 2 * NB_E + LOOK
                for k in range(4):
                    split_m(d0 + k, HALF, j8)
                gathered_hi(i + 1)
                hid_hi_m(NB_E - 1, (NB_E - 1) % 2)
                with act.Fori(0, 2) as it:
                    for k in range(4, 12):
                        split_m(d0 + k, HALF, j8 + it)
                for k in range(20, 24):
                    split_m(d0 + k, HALF, j8)
                for k in range(24, 27):
                    split_m(d0 + k, FULL, j8)
                act.wait_ge(s_use, i * JOB_CHUNKS + (MOE0 + JOB_CHUNKS))
                for j in range(2):
                    act.activation(yhi[:, 4 * j:4 * j + 4, :], bank[6 + j][:].rearrange("p (k n) -> p k n", n=P),
                                   ACT.Copy).then_inc(m_yhi, 1)
                split_m(d0 + 27, FULL, j8)

        @block.tensor
        def _(pe):
            def three(dst, ahi, alo, bhi, blo, start, stop):
                pe.matmul(dst, ahi, bhi, start=start, stop=False)
                pe.matmul(dst, ahi, blo, start=False, stop=False)
                return pe.matmul(dst, alo, bhi, start=False, stop=stop)

            def weights(c, n, width):
                s = c % SLOTS
                return [t[:, s, 0:n * width].rearrange("p (k n) -> p k n", n=width) for t in (whi, wlo)]

            def chunk(c, dst, ahi, alo, k0, width, start, stop, dyn=0, tiles=TT, n=4):
                pe.wait_ge(s_lo, dyn * SLOTS + c + 1)
                bhi, blo = weights(c, n, width)
                for t in range(tiles):
                    for k in range(n):
                        a = [x[:, k0 + k, t * P:(t + 1) * P] for x in (ahi, alo)]
                        ins = three(dst[t], *a, bhi[:, k, :], blo[:, k, :], start and k == 0, stop and k == n - 1)
                ins.then_inc(s_use, 1)
                return ins

            def transposes_hT(src, js=range(4)):
                for j in js:
                    for q in range(2):
                        for t in range(TT):
                            ins = pe.transpose(bank[j][:, q * S + t * P:q * S + t * P + P], src(2 * j + q, t), ident)
                    ins.then_inc(s_tr, 1)

            def x_T(k, n):
                if k:
                    pe.wait_ge(s_xd, 2 * k - 1 + n)
                transposes_hT(lambda kc, t: X[:, t, kc * P:kc * P + P], (2 * n, 2 * n + 1))

            def layer(l, c0):
                def z_block(n, half):
                    w = IDXW if n == 0 else 512
                    if half == 0 and n >= 2:
                        pe.wait_ge(s_za, 2 * NZ * l + 2 * (n - 1))
                    if n == 0:
                        pe.wait_ge(s_tlo, 12 * l + 2 + 2 * half)
                    chunk(c0 + 2 * n + half, [bank[4 + 2 * (n % 2) + t][:, 0:w] for t in range(TT)], hThi, hTlo,
                          4 * half, w, half == 0, half == 1)

                def dots(t):
                    nk = P * (t + 1)
                    for hc in range(2):
                        for r in range(4):
                            rows = slice(32 * r, 32 * r + 32)
                            ins = pe.matmul(bank[r][:, hc * S:hc * S + nk], qiT[rows, hc, t * P:t * P + P],
                                            kiT[rows, 0:nk], start=True, stop=True)
                    ins.then_inc(s_dot, 1)

                def qk(t):
                    nk = P * (t + 1)
                    for hp in range(4):
                        for p in range(2):
                            rows = slice(64 * p, 64 * p + 64)
                            dst = bank[2 * p + hp // 2][:, (hp % 2) * S:(hp % 2) * S + S] if t else \
                                bank[p][:, hp * P:hp * P + P]
                            ins = pe.matmul(dst, qT[rows, hp, t * P:t * P + P], kT[rows, hp, 0:nk],
                                            start=True, stop=True)
                    ins.then_inc(s_lg, 1)

                def probs_T(t, j):
                    for q in range(2):
                        for h in range(4):
                            ins = pe.transpose(bank[2 * ((t + j) % 2) + q][:, h * P:h * P + P],
                                               Pr[:, 4 * q + h, j * P:j * P + P], ident)
                        ins.then_inc(s_pt, 1)

                def pv(t):
                    for h in range(HEADS):
                        i = (h % 2) * 4 + h // 2
                        for j in range(t + 1):
                            ins = pe.matmul(bank[4 + t][:, h * HD:h * HD + HD], PT[:, j, i, :] if t else PT0[:, i, :],
                                            zb[:, ZV, j, h * HD:h * HD + HD], start=(j == 0), stop=(j == t))
                    ins.then_inc(s_pv, 1)

                Pr = zb[:, 0:2].rearrange("p b t (h s) -> p (b t h) s", s=S)
                z_block(0, 0)
                z_block(0, 1)
                z_block(1, 0)
                z_block(1, 1)
                pe.wait_ge(s_idx, l + 1)
                for hc in range(2):
                    for t in range(TT):
                        pe.transpose(bank[0][:, hc * S + t * P:hc * S + t * P + P], zi[:, t, hc * P:hc * P + P], ident)
                for t in range(TT):
                    ins = pe.transpose(bank[1][:, t * P:t * P + P], ao[:, t, 0:4 * IDIM], ident)
                ins.then_inc(s_idxT, 1)
                z_block(2, 0)
                pe.wait_ge(s_idxs, 2 * (l + 1))
                dots(0)
                z_block(2, 1)
                z_block(3, 0)
                pe.wait_ge(s_rel, 2 * l + 1)
                dots(1)
                z_block(3, 1)
                z_block(4, 0)
                z_block(4, 1)
                z_block(5, 0)
                pe.wait_ge(s_qk, l + 1)
                pe.wait_ge(s_rel, 2 * l + 2)
                for j in range(4):
                    z = zb[:, ZQ if j < 2 else ZK]
                    for q in range(2):
                        hp = 2 * (j % 2) + q
                        for t in range(TT):
                            ins = pe.transpose(bank[j][:, q * S + t * P:q * S + t * P + P],
                                               z[:, t, hp * P:hp * P + P], ident)
                    ins.then_inc(s_qkT, 1)
                z_block(5, 1)
                pe.wait_ge(s_qks, 4 * (l + 1))
                qk(0)
                z_block(6, 0)
                z_block(6, 1)
                pe.wait_ge(s_lgs, 6 * l + 2)
                qk(1)
                z_block(7, 0)
                pe.wait_ge(s_lgs, 6 * l + 6)
                for s in s_pool:
                    pe.wait_ge(s, 16 * (l + 1))
                for j in range(2):
                    for q in range(2):
                        g = 2 * j + q
                        for t in range(TT):
                            rhs = band[:, g, 0:S] if t == 0 else band[:, g, S:S + P]
                            ins = pe.matmul(bank[j][:, q * S + t * P:q * S + S], zb[:, ZU, t, g * P:g * P + P], rhs,
                                            start=(t == 0), stop=(t == 1), skip_group_check=True)
                    ins.then_inc(s_df, 1)
                z_block(7, 1)
                for j in range(2):
                    pe.wait_ge(s_dfs, 2 * l + j + 1)
                    for q in range(2):
                        g = 2 * j + q
                        ins = pe.matmul(bank[2 + j][:, q * S:q * S + S], wpool[:, g, :], diffT[:, g, :],
                                        start=True, stop=True)
                    ins.then_inc(s_pp, 1)
                z_block(8, 0)
                z_block(8, 1)
                c = c0 + 2 * NZ
                pe.wait_ge(s_plo, 2 * (l + 1))
                pe.wait_ge(s_za, 2 * NZ * (l + 1))
                chunk(c, [bank[4 + t][:] for t in range(TT)], pThi, pTlo, 0, 512, True, True)
                pe.wait_ge(s_ex, 2 * l + 1)
                probs_T(0, 0)
                chunk(c + 1, [bank[6 + t][:] for t in range(TT)], pThi, pTlo, 0, 512, True, True)
                pe.wait_ge(s_ex, 2 * l + 2)
                probs_T(1, 0)
                pe.wait_ge(s_pta, 3 * l + 1)
                pe.wait_ge(s_ptd, 3 * l + 1)
                probs_T(1, 1)
                pe.wait_ge(s_gp, 2 * l + 1)
                pv(0)
                pe.wait_ge(s_pta, 3 * l + 3)
                pe.wait_ge(s_ptd, 3 * l + 3)
                pv(1)
                pe.wait_ge(s_ao, 2 * (l + 1))
                for j in range(2):
                    for q in range(2):
                        for t in range(TT):
                            k = 2 * j + q
                            ins = pe.transpose(bank[2 + j][:, q * S + t * P:q * S + t * P + P], ao[:, t, k * P:k * P + P],
                                               ident)
                    ins.then_inc(s_aT, 1)
                pe.wait_ge(s_alo, 2 * (l + 1))
                chunk(c + 2, [bank[4 + t][:] for t in range(TT)], aThi, aTlo, 0, 512, True, True)
                pe.wait_ge(s_gp, 2 * l + 2)
                chunk(c + 3, [bank[6 + t][:] for t in range(TT)], aThi, aTlo, 0, 512, True, True)

                def m_T(n):
                    pe.wait_ge(s_m, 2 * l + n + 1)
                    transposes_hT(lambda kc, t: zb[:, ZGA + kc // 4, t, (kc % 4) * P:(kc % 4) * P + P], (2 * n, 2 * n + 1))

                m_T(0)
                pe.wait_ge(s_tlo, 12 * l + 6)
                chunk(c + 4, [bank[4 + t][:] for t in range(TT)], hThi, hTlo, 0, 512, True, False)
                m_T(1)
                chunk(c + 5, [bank[6 + t][:] for t in range(TT)], hThi, hTlo, 0, 512, True, False)
                pe.wait_ge(s_tlo, 12 * l + 8)
                chunk(c + 6, [bank[4 + t][:] for t in range(TT)], hThi, hTlo, 4, 512, False, True)
                chunk(c + 7, [bank[6 + t][:] for t in range(TT)], hThi, hTlo, 4, 512, False, True)
                x_T(2 * l + 1, 0)
                x_T(2 * l + 1, 1)
                pe.wait_ge(s_tlo, 12 * (l + 1))

            pe.wait_ge(s_cst, 16)
            pe.wait_ge(s_par, 7 * 16)
            pe.transpose(bank[6][:, 0:40], prow[:], cst[0:40, C_ID:C_ID + 40])
            pe.matmul(bank[7][:, 0:4 * HD], cst[0:1, C_ONE:C_ONE + P], nrow[:], start=True, stop=True).then_inc(s_prt, 1)
            pe.wait_ge(s_x, 16)
            x_T(0, 0)
            x_T(0, 1)
            layer(0, 0)

            def hiddenT_d(b, q):
                pe.wait_ge(s_hm, b + 1)
                for f in range(2):
                    for t in range(TT):
                        ins = pe.transpose(bank[q][:, f * S + t * P:f * S + t * P + P],
                                           hsD[:, q, t, f * P:f * P + P], ident)
                ins.then_inc(s_ft, 1)

            def block_d(b, q, c, dyn, prev=True, prev2=True):
                dst = [bank[4 + 2 * q + t][:] for t in range(TT)]
                chunk(c, dst, hThi, hTlo, 0, 512, True, False, dyn)
                if prev:
                    if prev2:
                        pe.wait_ge(s_flo, b - 2 + LEAD)
                    hiddenT_d(b - 1, 1 - q)
                chunk(c + 1, dst, hThi, hTlo, 4, 512, False, True, dyn)

            block_d(0, 0, DENSE0, 0, prev=False)
            with pe.Fori(0, 5) as it:
                for u in range(2):
                    block_d(it * 2 + (1 + u), 1 - u, DENSE0 + 2 + 2 * u, it)
            hiddenT_d(NB_D - 1, (NB_D - 1) % 2)
            for k in range(KC_D):
                c = DENSE0 + 2 * NB_D + k
                pe.wait_ge(s_flo, k // 2 + 1 + LEAD)
                pe.wait_ge(s_lo, c + 1)
                if k == 0:
                    pe.wait_ge(s_hm, NB_D)
                for t in range(TT):
                    a = [x[:, k, t * P:t * P + P] for x in (hidDhi, hidDlo)]
                    for nh in range(2):
                        w = [x[:, c % SLOTS, 512 * nh:512 * nh + 512] for x in (whi, wlo)]
                        ins = three(bank[4 + 2 * t + nh][:], *a, *w, k == 0, k == KC_D - 1)
                ins.then_inc(s_use, 1)
            x_T(2, 0)
            x_T(2, 1)
            layer(1, LAYER1)

            pe.wait_ge(s_wrh, 2)
            for t in range(TT):
                for k in range(KC):
                    ins = three(bank[4][:, t * E:t * E + E], hThi[:, k, t * P:t * P + P], hTlo[:, k, t * P:t * P + P],
                                wrhi[:, k, :], wrlo[:, k, :], k == 0, k == KC - 1)
            ins.then_inc(s_rt, 1)
            pe.wait_ge(s_mk, 1)
            tri, ones = cst[:, C_TRI:C_TRI + P], cst[:, C_ONE:C_ONE + P]
            pe.matmul(bank[5][:, 0:E], tri, tmp8[:, 0, :], start=True, stop=True)
            pe.matmul(bank[5][:, E:2 * E], tri, tmp8[:, 1, :], start=True, stop=False)
            pe.matmul(bank[5][:, E:2 * E], ones, tmp8[:, 0, :], start=False, stop=True)
            pe.matmul(bank[5][:, 2 * E:3 * E], ones, tmp8[:, 0, :], start=True, stop=False)
            pe.matmul(bank[5][:, 2 * E:3 * E], ones, tmp8[:, 1, :], start=False, stop=True).then_inc(s_pos, 1)

            def gather(i):
                pe.wait_ge(s_sel, i + 1)
                for j in range(2):
                    for q in range(4):
                        k = 4 * j + q
                        for t in range(TT):
                            for x in (xrhi, xrlo):
                                ins = pe.matmul(bank[2 + j][:, q * P:q * P + P], x[:, t, k * P:k * P + P],
                                                selR[:, t, :], start=(t == 0 and x is xrhi),
                                                stop=(t == TT - 1 and x is xrlo))
                    ins.then_inc(s_g, 1)

            def scatter(i):
                pe.wait_ge(m_ylo, i * 2 + LEAD)
                for t in range(TT):
                    for nh in range(2):
                        for y in (yhi, ylo):
                            ins = pe.matmul(bank[4 * t + 2 + nh][:], selT[:, t * P:t * P + P],
                                            y[:, 4 * nh:4 * nh + 4, :], start=(y is yhi), stop=(y is ylo))
                        ins.then_inc(m_sc, 1)

            pe.wait_ge(s_xrl, 2)
            pe.wait_ge(s_y0, 1)
            gather(0)
            pe.wait_ge(s_tab, 1)
            njobs = pe.value_load(tabi[0:1, 15:16], min_val=E, max_val=NJ - 1)
            with pe.Fori(0, njobs) as i:
                jd = JOB_CHUNKS // SLOTS

                def hiddenT_m(b, q):
                    pe.wait_ge(m_hm, i * NB_E + b + 1)
                    for f in range(2):
                        ins = pe.transpose(bank[q][:, f * P:f * P + P], hsM[:, q, f * P:f * P + P], ident)
                    ins.then_inc(m_ft, 1)

                def pair(it, first=False):
                    for u in range(2):
                        c = MOE0 + 2 * u
                        b = it * 2 + u
                        if not first:
                            pe.wait_ge(m_hm, i * NB_E + b - 1)
                        chunk(c, [bank[4 + u][:]], hehi, helo, 0, 512, True, False, i * jd + it, tiles=1)
                        if not (first and u == 0):
                            if not first:
                                pe.wait_ge(m_flo, i * NB_E + b - 2 + LEAD)
                            hiddenT_m(b - 1, 1 - u)
                        if first and u == 1:
                            for t in range(TT):
                                ins = pe.matmul(bank[1][:, t * P:t * P + P], selR[:, t, :], identR[:],
                                                start=True, stop=True)
                            ins.then_inc(s_st, 1)
                        chunk(c + 1, [bank[4 + u][:]], hehi, helo, 4, 512, False, True, i * jd + it, tiles=1)
                        if first and u == 0:
                            scatter(i)

                pe.wait_ge(s_glo, i * 2 + 2)
                pair(0, first=True)
                with pe.Fori(1, NB_E // 2) as it:
                    pair(it)
                pe.wait_ge(m_xa, i * 4 + 4)
                gather(i + 1)
                for k in range(KC_E):
                    c = MOE0 + 2 * NB_E + k
                    if k == 4:
                        hiddenT_m(NB_E - 1, (NB_E - 1) % 2)
                    if k == 0:
                        pe.wait_ge(m_flo, i * NB_E + NB_E - 1 + LEAD)
                        pe.wait_ge(m_xa, i * 4 + 4)
                    if k == KC_E - 2:
                        pe.wait_ge(m_flo, i * NB_E + NB_E + LEAD)
                    pe.wait_ge(s_lo, i * JOB_CHUNKS + c + 1)
                    for nh in range(2):
                        w = [x[:, c % SLOTS, 512 * nh:512 * nh + 512] for x in (whi, wlo)]
                        ins = three(bank[6 + nh][:], hidMhi[:, k, :], hidMlo[:, k, :], *w, k == 0, k == KC_E - 1)
                    ins.then_inc(s_use, 1)
            scatter(njobs)

        @block.vector
        def _(dve):
            steps = [0]

            def chain(ins):
                steps[0] += 1
                ins.then_inc(s_dve, 1)
                dve.wait_ge(s_dve, steps[0])

            def split(c, n, dyn=0):
                dve.wait_ge(s_hi, dyn * SLOTS + c + 1)
                s = c % SLOTS
                dve.tensor_tensor(wlo[:, s, 0:n], raw[:, s, 0:n], whi[:, s, 0:n], ALU.subtract).then_inc(s_lo, 1)

            def split_m(m, n, dyn):
                dve.wait_ge(s_hi, dyn * 8 + (MOE0 + m + 1))
                dve.tensor_tensor(wlo[:, m % SLOTS, 0:n], raw8[m % 8][:, 0:n], whi[:, m % SLOTS, 0:n],
                                  ALU.subtract).then_inc(s_lo, 1)

            def ahead(c):
                split(c + LOOK, chunk_words(c + LOOK) if c + LOOK < MOE0 else FULL)

            def hT_lo(te, scale0, js=range(4)):
                for j in js:
                    dve.wait_ge(s_thi, 4 * te + j + 1)
                    if scale0 is None:
                        dve.tensor_tensor(hTlo[:, 2 * j:2 * j + 2, :], bank[j][:].rearrange("p (k t) -> p k t", t=S),
                                          hThi[:, 2 * j:2 * j + 2, :], ALU.subtract).then_inc(s_tlo, 1)
                        continue
                    for q in range(2):
                        k = 2 * j + q
                        ins = dve.scalar_tensor_tensor(hTlo[:, k, :], bank[j][:, q * S:q * S + S],
                                                       pcol[:, scale0 + k:scale0 + k + 1], hThi[:, k, :],
                                                       ALU.mult, ALU.subtract)
                    ins.then_inc(s_tlo, 1)

            def rsqrt(r, rms, ms, t):
                chain(dve.reciprocal(r, rms))
                chain(dve.tensor_tensor(t, r, r, ALU.mult))
                chain(dve.tensor_tensor(t, t, ms, ALU.mult))
                chain(dve.tensor_scalar(t, t, -0.5, 1.5, ALU.mult, ALU.add))
                chain(dve.tensor_tensor(r, r, t, ALU.mult))

            def norm(k):
                dve.wait_ge(s_sq, TT * (k + 1))
                chain(dve.tensor_scalar(st[:, 1, :], st[:, 0, :], 1.0 / D, EPS, ALU.mult, ALU.add))
                dve.nop().then_inc(s_ms, 1)
                dve.wait_ge(s_rms, k + 1)
                rsqrt(st[:, 3, :], st[:, 2, :], st[:, 1, :], st[:, 0, :])
                dve.nop().then_inc(s_rs, 1)

            def rope(v, half, cos, sin, tmp):
                x1, x2 = v[:, :, :, 0:half], v[:, :, :, half:2 * half]
                dve.tensor_tensor(tmp[0], x1, cos, ALU.mult)
                dve.tensor_tensor(tmp[1], x2, sin, ALU.mult)
                dve.tensor_tensor(tmp[2], x2, cos, ALU.mult)
                chain(dve.tensor_tensor(tmp[3], x1, sin, ALU.mult))
                dve.tensor_tensor(x1, tmp[0], tmp[1], ALU.subtract)
                return dve.tensor_tensor(x2, tmp[2], tmp[3], ALU.add)

            def table(off, half, heads):
                v = cst[:, off:off + TT * half].rearrange("p (t o d) -> p t o d", t=TT, o=1)
                return v.broadcast_to([P, TT, heads, half])

            def layer(l, c0):
                c = c0
                flat = PT[:].rearrange("p a h s -> p (a h s)")
                work_t = [work[:, 0:P], work[:, P:P + S]]

                def tmps(heads, half):
                    n = TT * heads * half
                    return [flat[:, i * n:i * n + n].rearrange("p (t h d) -> p t h d", t=TT, h=heads) for i in range(4)]

                def scores(t):
                    nk = P * (t + 1)
                    w = work_t[t]
                    dve.wait_ge(s_rel, 2 * l + t + 1)
                    for i in range(HEADS):
                        h = (i % 2) * 4 + i // 2
                        if i == 0:
                            chain(dve.tensor_scalar(w, L[:, i, 0:nk], wis[:, t, h:h + 1], None, ALU.mult))
                        else:
                            chain(dve.scalar_tensor_tensor(w, L[:, i, 0:nk], wis[:, t, h:h + 1], w, ALU.mult, ALU.add))
                    d = work[:, 2 * t * P:2 * t * P + P]
                    chain(dve.tensor_tensor(d, d, cst[:, C_NEG:C_NEG + P], ALU.add))
                    dve.nop().then_inc(s_sc, 1)

                def top8():
                    for t in range(TT):
                        ins = dve.max(m8[:, t, :], work_t[t])
                    chain(ins)
                    for t in range(TT):
                        ins = dve.match_replace(work_t[t], m8[:, t, :], work_t[t], MARK)
                    chain(ins)

                def gain_of(b):
                    g = gain[:, l, b:b + 1, :].broadcast_to([P, TT * HEADS, HD])
                    v = zb[:, b].rearrange("p t (h d) -> p (t h) d", d=HD)
                    chain(dve.tensor_tensor(v, v, g, ALU.mult))

                def rope_of(b):
                    v = zb[:, b].rearrange("p t (h d) -> p t h d", d=HD)
                    return rope(v, ROT // 2, table(C_COS, ROT // 2, HEADS), table(C_SIN, ROT // 2, HEADS),
                                tmps(HEADS, ROT // 2))

                def mask_logits(t):
                    nk = P * (t + 1)
                    src = L[:] if t else L0
                    dve.wait_ge(s_lgs, 6 * l + 2 + 4 * t)
                    ma = madd[:, t * P:t * P + nk].rearrange("p (o s) -> p o s", o=1).broadcast_to([P, HEADS, nk])
                    chain(dve.tensor_tensor(src, src, ma, ALU.add))

                def row_max(t):
                    chain(dve.tensor_reduce(sx[:, t, 0, :], L[:] if t else L0, AX.X, ALU.max))
                    dve.tensor_scalar(sx[:, t, 1, :], sx[:, t, 0, :], -1.0, None, ALU.mult).then_inc(s_mx, 1)

                def gate_pool(nh):
                    dve.wait_ge(s_use, c0 + 2 * NZ + nh + 1)
                    for t in range(TT):
                        v = zb[:, ZGP + nh, t]
                        ins = dve.tensor_tensor(v, v, bank[4 + 2 * nh + t][:], ALU.mult)
                    ins.then_inc(s_gp, 1)

                def merge(nh):
                    dve.wait_ge(s_use, c0 + 2 * NZ + 3 + nh)
                    ga, gp = zb[:, ZGA + nh], zb[:, ZGP + nh]
                    for t in range(TT):
                        ins = dve.tensor_tensor(ga[:, t], ga[:, t], bank[4 + 2 * nh + t][:], ALU.mult)
                    chain(ins)
                    dve.tensor_tensor(ga, ga, gp, ALU.add).then_inc(s_m, 1)

                def add_out(nh):
                    dve.wait_ge(s_use, c0 + MIX_CHUNKS - 1 + nh)
                    for t in range(TT):
                        v = X[:, t, 512 * nh:512 * nh + 512]
                        ins = dve.tensor_tensor(v, v, bank[4 + 2 * nh + t][:], ALU.add)
                    ins.then_inc(s_xd, 1)

                ahead(c)
                ahead(c + 1)
                dve.wait_ge(s_za, 2 * NZ * l + 2)
                zh = zi[:, :, 0:9 * IDIM].rearrange("p t (h d) -> p t h d", d=IDIM)
                chain(rope(zh, IROT // 2, table(C_COSI, IROT // 2, 9), table(C_SINI, IROT // 2, 9), tmps(9, IROT // 2)))
                dve.tensor_copy(ki4, zh[:, :, 8:9, :].broadcast_to([P, TT, 4, IDIM]))
                dve.tensor_scalar(wis[:], zi[:, :, 9 * IDIM:IDXW], IH ** -0.5, None, ALU.mult).then_inc(s_idx, 1)
                for n in range(2, 6):
                    ahead(c + n)
                scores(0)
                dve.wait_ge(s_za, 2 * NZ * l + 6)
                zq = zb[:, 0:2].rearrange("p b t n -> p (b t n)")
                zqh = zb[:, 0:2].rearrange("p b t (h d) -> p (b t h) d", d=HD)
                chain(dve.tensor_tensor(flat, zq, zq, ALU.mult))
                ahead(c + 6)
                chain(dve.tensor_reduce(hs32[:, 2, :], flat.rearrange("p (g d) -> p g d", d=HD), AX.X, ALU.add))
                chain(dve.tensor_scalar(hs32[:, 0, :], hs32[:, 2, :], 1.0 / HD, EPS, ALU.mult, ALU.add))
                dve.nop().then_inc(s_qms, 1)
                ahead(c + 7)
                scores(1)
                dve.wait_ge(s_qrm, l + 1)
                rsqrt(hs32[:, 2, :], hs32[:, 1, :], hs32[:, 0, :], flat[:, 0:32])
                ahead(c + 8)
                chain(dve.tensor_tensor(zqh, zqh, hs32[:, 2, :].rearrange("p (g o) -> p g o", o=1).broadcast_to([P, 32, HD]),
                                        ALU.mult))
                gain_of(0)
                gain_of(1)
                ahead(c + 9)
                chain(rope_of(0))
                rope_of(1).then_inc(s_qk, 1)
                for n in range(10, 14):
                    ahead(c + n)
                    top8()
                    top8()
                chain(dve.tensor_scalar(madd[:], work[:], MARK, MASKED, ALU.not_equal, ALU.mult))
                for t in range(TT):
                    d = madd[:, 2 * t * P:2 * t * P + P]
                    ins = dve.tensor_tensor(d, d, cst[:, C_NEG:C_NEG + P], ALU.add)
                chain(ins)
                mask_logits(0)
                ahead(c + 14)
                row_max(0)
                ahead(c + 15)
                mask_logits(1)
                ahead(c + 16)
                row_max(1)
                for j in range(2):
                    dve.wait_ge(s_phi, 2 * l + j + 1)
                    for q in range(2):
                        g = 2 * j + q
                        ins = dve.scalar_tensor_tensor(pTlo[:, g, :], bank[2 + j][:, q * S:q * S + S],
                                                       pcol[:, 32 + 4 * l + g:33 + 4 * l + g], pThi[:, g, :],
                                                       ALU.mult, ALU.subtract)
                    ins.then_inc(s_plo, 1)
                ahead(c + 17)
                ahead(c + 18)
                dve.wait_ge(s_pt, 6 * l + 2)
                dve.tensor_copy(PT0[:, 4:8, :], bank[1][:].rearrange("p (h s) -> p h s", s=P)).then_inc(s_ptd, 1)
                gate_pool(0)
                for j in range(2):
                    dve.wait_ge(s_pt, 6 * l + 2 * j + 4)
                    dve.tensor_copy(PT[:, j, 4:8, :], bank[3 - 2 * j][:].rearrange("p (h s) -> p h s", s=P)
                                    ).then_inc(s_ptd, 1)
                for t in range(TT):
                    dve.wait_ge(s_ex, 2 * l + t + 1)
                    chain(dve.reciprocal(sx[:, t, 3, :], sx[:, t, 2, :]))
                    dve.wait_ge(s_pv, 2 * l + t + 1)
                    dve.tensor_tensor(ao[:, t, :].rearrange("p (a q d) -> p a q d", a=4, q=2),
                                      bank[4 + t][:].rearrange("p (a q d) -> p a q d", a=4, q=2),
                                      sx[:, t, 3, :].rearrange("p (q a o) -> p a q o", q=2, o=1).broadcast_to([P, 4, 2, HD]),
                                      ALU.mult).then_inc(s_ao, 1)
                ahead(c + 19)
                for j in range(2):
                    dve.wait_ge(s_ahi, 2 * l + j + 1)
                    dve.tensor_tensor(aTlo[:, 2 * j:2 * j + 2, :], bank[2 + j][:].rearrange("p (k t) -> p k t", t=S),
                                      aThi[:, 2 * j:2 * j + 2, :], ALU.subtract).then_inc(s_alo, 1)
                gate_pool(1)
                merge(0)
                ahead(c + 20)
                merge(1)
                ahead(c + 21)
                hT_lo(3 * l + 1, None, (0, 1))
                ahead(c + 22)
                hT_lo(3 * l + 1, None, (2, 3))
                ahead(c + 23)
                add_out(0)
                ahead(c + 24)
                add_out(1)
                hT_lo(3 * l + 2, 16 + 8 * l)
                norm(2 * l + 1)
                ahead(c + 25)

            for s in (s_flo, m_flo, m_ylo):
                dve.nop().then_inc(s, LEAD)
            dve.wait_ge(s_prt, 1)
            dve.tensor_copy(pcol[:], bank[6][:, 0:40]).then_inc(s_pcol, 1)
            dve.tensor_copy(gain[:].rearrange("p l j d -> p (l j d)"), bank[7][:, 0:4 * HD]).then_inc(s_pcol, 1)
            for c in range(LOOK):
                split(c, chunk_words(c))
            dve.wait_ge(s_pcol, 2)
            hT_lo(0, 0)
            norm(0)
            layer(0, 0)

            def mul_d(b, q):
                dve.wait_ge(s_si, b + 1)
                for t in range(TT):
                    ins = dve.scalar_tensor_tensor(hsD[:, q, t, :], bank[4 + 2 * q + t][:, 256:512],
                                                   st[:, 3, t:t + 1], hsD[:, q, t, :], ALU.mult, ALU.mult)
                ins.then_inc(s_hm, 1)

            def hid_lo_d(b, q):
                dve.wait_ge(s_fhi, b + 1)
                hi, lo = (x[:, 2 * b:2 * b + 2, :] if isinstance(b, int) else x[:, bass.ds(b * 2, 2), :]
                          for x in (hidDhi, hidDlo))
                dve.tensor_tensor(lo, bank[q][:].rearrange("p (k t) -> p k t", t=S), hi, ALU.subtract).then_inc(s_flo, 1)

            ahead(DENSE0)
            mul_d(0, 0)
            ahead(DENSE0 + 1)
            with dve.Fori(0, 4) as it:
                for u in range(2):
                    c = DENSE0 + 2 + 2 * u
                    split(c + LOOK, FULL, it)
                    hid_lo_d(it * 2 + u, u)
                    mul_d(it * 2 + (1 + u), 1 - u)
                    split(c + 1 + LOOK, FULL, it)
            for b in range(9, NB_D):
                ahead(DENSE0 + 2 * b)
                hid_lo_d(b - 1, (b - 1) % 2)
                mul_d(b, b % 2)
                ahead(DENSE0 + 2 * b + 1)
            hid_lo_d(NB_D - 1, (NB_D - 1) % 2)
            c = DENSE0 + 2 * NB_D
            with dve.Fori(0, 4) as it:
                for k in range(SLOTS):
                    split(c + k + LOOK, HALF, it)
            for k in range(16, KC_D):
                ahead(c + k)
            dve.wait_ge(s_use, LAYER1)
            for nh in range(2):
                for t in range(TT):
                    v = X[:, t, 512 * nh:512 * nh + 512]
                    ins = dve.tensor_tensor(v, v, bank[4 + 2 * t + nh][:], ALU.add)
                ins.then_inc(s_xd, 1)
            hT_lo(3, 8)
            norm(2)
            layer(1, LAYER1)

            for t in range(TT):
                dve.tensor_scalar(xs[:, t, :], X[:, t, :], st[:, 3, t:t + 1], None, ALU.mult).then_inc(s_xs, 1)
            dve.wait_ge(s_xs, TT)
            for t in range(TT):
                dve.wait_ge(s_xr, t + 1)
                dve.tensor_tensor(xrlo[:, t, :], xs[:, t, :], xrhi[:, t, :], ALU.subtract).then_inc(s_xrl, 1)
            dve.wait_ge(s_wrh, 1)
            dve.tensor_tensor(wrlo[:], wr[:], wrhi[:], ALU.subtract).then_inc(s_wrh, 1)
            dve.wait_ge(s_rt, 1)
            for z in (yhi, ylo, selT[:]):
                ins = dve.memset(z.bitcast(F32), 0.0)
            ins.then_inc(s_y0, 1)
            for t in range(TT):
                chain(dve.tensor_scalar(lg[:, t, :], bank[4][:, t * E:t * E + E], st[:, 3, t:t + 1], None, ALU.mult))
            for t in range(TT):
                chain(dve.max(v8[:, t, :], lg[:, t, :]))
            for t in range(TT):
                chain(dve.max_index(ix8[:, t, :], v8[:, t, :], lg[:, t, :]))
            dve.tensor_tensor(pr[:, 0, :], v8[:, :, 1], v8[:, :, 0], ALU.subtract).then_inc(s_gd, 1)
            chain(dve.tensor_copy(ixf[:], ix8[:]))
            iota8 = cst[:, C_IOTA:C_IOTA + E]
            for t in range(TT):
                dve.tensor_scalar(m0[:, t, :], iota8, ixf[:, t, 0:1], None, ALU.is_equal)
                chain(dve.tensor_scalar(m1[:, t, :], iota8, ixf[:, t, 1:2], None, ALU.is_equal))
            chain(dve.tensor_tensor(tmp8[:], m0[:], m1[:], ALU.add))
            dve.nop().then_inc(s_mk, 1)
            dve.wait_ge(s_ge, 1)
            chain(dve.tensor_scalar(pr[:, 2, :], pr[:, 1, :], 1.0, None, ALU.add))
            chain(dve.reciprocal(pr[:, 2, :], pr[:, 2, :]))
            chain(dve.tensor_tensor(pr[:, 3, :], pr[:, 1, :], pr[:, 2, :], ALU.mult))
            for t in range(TT):
                chain(dve.tensor_scalar(gate[:, t, :], m0[:, t, :], pr[:, 2, t:t + 1], None, ALU.mult))
                chain(dve.scalar_tensor_tensor(gate[:, t, :], m1[:, t, :], pr[:, 3, t:t + 1], gate[:, t, :],
                                               ALU.mult, ALU.add))
            dve.wait_ge(s_pos, 1)
            pos = bank[5][:, 0:2 * E].rearrange("p (t e) -> p t e", t=TT)
            chain(dve.scalar_tensor_tensor(pm[:], pos, 1.0, tmp8[:], ALU.add, ALU.mult))
            chain(dve.tensor_scalar(pm[:], pm[:], -1.0, None, ALU.add))
            dve.tensor_copy(posj[:, :, 0:E], pm[:])
            dve.memset(gatej[:, :, 0:1], 0.0)
            chain(dve.tensor_copy(gatej[:, :, 1:E + 1], gate[:]))

            def select(i):
                for t in range(TT):
                    col = posj[:, t, i:i + 1] if isinstance(i, int) else posj[:, t, bass.ds(i, 1)]
                    ins = dve.tensor_scalar(selR[:, t, :], cst[:, C_IOTA:C_IOTA + P], col, None, ALU.is_equal)
                ins.then_inc(s_sel, 1)

            select(0)
            over, cum, rank, one8 = (ov[:, i, :] for i in range(4))
            dve.tensor_scalar(over, bank[5][:, 2 * E:3 * E], float(P), None, ALU.is_gt)
            chain(dve.memset(one8, 1.0))
            chain(dve.tensor_tensor_scan(cum, one8, over, 0.0, ALU.mult, ALU.add))
            chain(dve.tensor_tensor(rank, cum, over, ALU.mult))
            dve.tensor_copy(tabf[:, 0:E], iota8)
            dve.memset(tabf[:, NJ:15], 0.0)
            chain(dve.tensor_scalar(tabf[:, 15:16], cum[:, E - 1:E], float(E), None, ALU.add))
            for q in range(NJ - E):
                chain(dve.tensor_scalar(one8, rank, float(q + 1), None, ALU.is_equal))
                pick = ov[:, 3:4, :].broadcast_to([P, TT, E])
                chain(dve.tensor_tensor(tmp8[:], pm[:], pick, ALU.mult))
                chain(dve.tensor_reduce(pr[:, 0, :], tmp8[:], AX.X, ALU.add))
                dve.tensor_scalar(posj[:, :, E + q], pr[:, 0, :], -float(P), None, ALU.add)
                chain(dve.tensor_tensor(tmp8[:], gate[:], pick, ALU.mult))
                chain(dve.tensor_reduce(gatej[:, :, E + q + 1], tmp8[:], AX.X, ALU.add))
                chain(dve.tensor_tensor(tmp8[:, 0, :], iota8, one8, ALU.mult))
                chain(dve.tensor_reduce(tabf[:, E + q:E + q + 1], tmp8[:, 0, :], AX.X, ALU.add))
            dve.tensor_copy(tabi[:], tabf[:]).then_inc(s_tab, 1)

            def gathered_lo(i):
                for j in range(2):
                    dve.wait_ge(s_ghi, i * 2 + (j + 1))
                    for q in range(4):
                        k = 4 * j + q
                        ins = dve.scalar_tensor_tensor(helo[:, k, :], bank[2 + j][:, q * P:q * P + P],
                                                       pcol[:, 24 + k:25 + k], hehi[:, k, :], ALU.mult, ALU.subtract)
                    ins.then_inc(s_glo, 1)

            def add_rows(i):
                for t in range(TT):
                    for nh in range(2):
                        dve.wait_ge(m_sc, i * 4 + 2 * t + nh + 1)
                        v = X[:, t, 512 * nh:512 * nh + 512]
                        dve.scalar_tensor_tensor(v, bank[4 * t + 2 + nh][:], gatej[:, t, bass.ds(i, 1)], v,
                                                 ALU.mult, ALU.add).then_inc(m_xa, 1)

            gathered_lo(0)
            dve.wait_ge(s_tab, 1)
            njobs = dve.value_load(tabi[0:1, 15:16], min_val=E, max_val=NJ - 1)
            with dve.Fori(0, njobs) as i:
                j8 = i * (JOB_CHUNKS // 8)

                def mul_m(b, q):
                    dve.wait_ge(m_si, i * NB_E + b + 1)
                    dve.tensor_tensor(hsM[:, q, :], hsM[:, q, :], bank[4 + q][:, 256:512], ALU.mult).then_inc(m_hm, 1)

                def hid_lo_m(b, q):
                    dve.wait_ge(m_fhi, i * NB_E + b + 1)
                    hi, lo = (x[:, 2 * b:2 * b + 2, :] if isinstance(b, int) else x[:, bass.ds(b * 2, 2), :]
                              for x in (hidMhi, hidMlo))
                    dve.tensor_tensor(lo, bank[q][:, 0:256].rearrange("p (k t) -> p k t", t=P), hi,
                                      ALU.subtract).then_inc(m_flo, 1)

                def pair(p, n, more=0, dyn=0, first=False):
                    for u in range(2):
                        m = 4 * p + 2 * u + LOOK
                        b = more * 2 + (2 * p + u)
                        if first and u == 1:
                            add_rows(i)
                        split_m(m, n, j8 + dyn)
                        if not (first and u == 0):
                            hid_lo_m(b - 1, 1 - u)
                        if first and u == 1:
                            dve.wait_ge(s_st, i + 1)
                            select(i + 1)
                        mul_m(b, u)
                        split_m(m + 1, n, j8 + dyn)

                pair(0, FULL, first=True)
                with dve.Fori(0, 2) as it:
                    pair(1, FULL, it * 2, it)
                    pair(2, FULL, it * 2, it)
                pair(5, FULL)
                pair(6, HALF)
                d0 = 2 * NB_E + LOOK
                for k in range(4):
                    split_m(d0 + k, HALF, j8)
                gathered_lo(i + 1)
                hid_lo_m(NB_E - 1, (NB_E - 1) % 2)
                with dve.Fori(0, 2) as it:
                    for k in range(4, 12):
                        split_m(d0 + k, HALF, j8 + it)
                for k in range(20, 24):
                    split_m(d0 + k, HALF, j8)
                for k in range(24, 27):
                    split_m(d0 + k, FULL, j8)
                for j in range(2):
                    dve.wait_ge(m_yhi, i * 2 + j + 1)
                    dve.tensor_tensor(ylo[:, 4 * j:4 * j + 4, :], bank[6 + j][:].rearrange("p (k n) -> p k n", n=P),
                                      yhi[:, 4 * j:4 * j + 4, :], ALU.subtract).then_inc(m_ylo, 1)
                split_m(d0 + 27, FULL, j8)
            add_rows(njobs)


def shape_constants():
    c = np.zeros((P, C_END), np.float32)
    i = np.arange(P)
    c[:, C_ID:C_ID + P] = np.eye(P)
    c[:, C_TRI:C_TRI + P] = i[:, None] < i[None, :]
    c[:, C_NEG:C_NEG + P] = np.where(i[None, :] <= i[:, None], 0.0, NEG)
    c[:, C_IOTA:C_IOTA + P] = i[None, :]
    c[:, C_ONE:C_ONE + P] = 1.0
    pos = np.arange(S, dtype=np.float32)
    for rot, co, so in ((ROT, C_COS, C_SIN), (IROT, C_COSI, C_SINI)):
        inv = np.power(np.float32(THETA), -np.arange(0, rot, 2, dtype=np.float32) / np.float32(rot))
        ang = (pos[:, None] * inv[None, :]).astype(np.float32)
        for f, o in ((np.cos, co), (np.sin, so)):
            t = f(ang.astype(np.float64)).astype(np.float32).reshape(TT, P, rot // 2)
            c[:, o:o + TT * rot // 2] = t.transpose(1, 0, 2).reshape(P, -1)
    band = np.zeros((GROUPS, S, S))
    for g, w in enumerate(WINDOWS):
        for t in range(S):
            band[g, max(0, t - w + 1):t + 1, t] = 1.0 / min(t + 1, w)
            band[g, t, t] -= 1.0
    b = np.concatenate([band[:, 0:P, :], band[:, P:, P:]], axis=2).transpose(1, 0, 2)
    return c, np.ascontiguousarray(b.astype(np.float32))


_INS = ["x", "mix_norm", "w_in", "q_norm", "k_norm", "w_pool", "pool_scale", "w_attn_proj", "w_pool_proj", "w_out",
        "ffn_norm", "dense_w1", "dense_w3", "dense_w2", "moe_router", "moe_w1", "moe_w3", "moe_w2"]


def kernel(**inputs):
    import concourse.bacc as _bacc
    from concourse.bass_utils import run_bass_kernel_spmd as _run

    nc = _bacc.Bacc("TRN2", target_bir_lowering=False, num_devices=1)
    arrays = {f"in_{n}": np.ascontiguousarray(inputs[n]) for n in _INS}
    arrays["in_consts"], arrays["in_pool_band"] = shape_constants()
    A = {n[3:]: nc.dram_tensor(n, a.shape, mybir.dt.from_np(a.dtype), kind="ExternalInput").ap()
         for n, a in arrays.items()}
    o = nc.dram_tensor("out_0", (1, S, D), F32, kind="ExternalOutput").ap()
    build(nc, A, o)
    r = _run(nc, [arrays], core_ids=[0])
    return r.results[0]["out_0"]
```
